# Optimizing a Trainium2 kernel written in Bass

```python
import jax, jax.numpy as jnp
from jax import lax
import numpy as np

D_MODEL = 1024
BATCH = 1
SEQ = 256
DEPTH = 2

CHUNK = 64
Q_BLOCK = 128
EPS = 1e-6
N_HEADS = 6
NOPE_DIM = 128
ROPE_DIM = 64
V_DIM = 128
Q_LORA = 384
KV_LORA = 256
ROPE_THETA = 10000.0
ATTN_WIDTH = N_HEADS * V_DIM
POOL_WINDOWS = (2, 4, 8, 16)
N_POOL_GROUPS = len(POOL_WINDOWS)
POOL_GROUP_DIM = 64
POOL_WIDTH = N_POOL_GROUPS * POOL_GROUP_DIM
MIX_WIDTH = ATTN_WIDTH + POOL_WIDTH
IN_COLS = Q_LORA + KV_LORA + ROPE_DIM + POOL_WIDTH
D_FF = 2816
N_EXPERTS = 8
TOP_K = 2
D_FF_EXPERT = 3584
N_DENSE = (DEPTH + 1) // 2
N_MOE = DEPTH // 2

kernel_name = "hybrid_mla_pool_moe_sandwich"

def rms_norm(x, g):
    xf = x.astype(jnp.float32)
    y = xf * lax.rsqrt(jnp.mean(xf * xf, axis=-1, keepdims=True) + EPS)
    return (y * g.astype(jnp.float32)).astype(x.dtype)

def rope_tables(seq):
    inv = 1.0 / (ROPE_THETA ** (jnp.arange(0, ROPE_DIM, 2, dtype=jnp.float32) / ROPE_DIM))
    ang = jnp.arange(seq, dtype=jnp.float32)[:, None] * inv[None, :]
    return jnp.cos(ang), jnp.sin(ang)

def apply_rope(x, cos, sin):
    x1, x2 = jnp.split(x.astype(jnp.float32), 2, axis=-1)
    return jnp.concatenate([x1 * cos - x2 * sin, x2 * cos + x1 * sin], axis=-1).astype(x.dtype)

def chunk_causal_mla(q_nope, q_rope, k_nope, k_rope, v):
    seq = q_nope.shape[1]
    scale = (NOPE_DIM + ROPE_DIM) ** -0.5
    outs = []
    for blk in range(seq // Q_BLOCK):
        q0, q1 = blk * Q_BLOCK, (blk + 1) * Q_BLOCK
        s = (jnp.einsum('bqhd,bkhd->bhqk', q_nope[:, q0:q1], k_nope[:, :q1])
             + jnp.einsum('bqhr,bkr->bhqk', q_rope[:, q0:q1], k_rope[:, :q1])).astype(jnp.float32) * scale
        q_chunk = jnp.arange(q0, q1) // CHUNK
        k_chunk = jnp.arange(q1) // CHUNK
        mask = k_chunk[None, :] <= q_chunk[:, None]
        s = jnp.where(mask[None, None], s, -jnp.inf)
        p = jax.nn.softmax(s, axis=-1).astype(v.dtype)
        outs.append(jnp.einsum('bhqk,bkhd->bqhd', p, v[:, :q1]))
    return jnp.concatenate(outs, axis=1)

def multiscale_pool(u, w, scale):
    b, seq, _ = u.shape
    ug = u.reshape(b, seq, N_POOL_GROUPS, POOL_GROUP_DIM)
    cs = jnp.cumsum(ug.astype(jnp.float32), axis=1)
    cs = jnp.pad(cs, ((0, 0), (1, 0), (0, 0), (0, 0)))
    t = jnp.arange(seq)
    pooled = []
    for g, win in enumerate(POOL_WINDOWS):
        start = jnp.maximum(t + 1 - win, 0)
        sums = cs[:, 1:, g] - jnp.take(cs[:, :, g], start, axis=1)
        cnt = (t + 1 - start).astype(jnp.float32)
        pooled.append(sums / cnt[None, :, None])
    pooled = jnp.stack(pooled, axis=2).astype(u.dtype) - ug
    y = jnp.einsum('bsgc,gcd->bsgd', pooled, w)
    return y.reshape(b, seq, POOL_WIDTH) * scale

def swiglu(h, w_gate, w_up, w_down):
    return (jax.nn.silu(h @ w_gate) * (h @ w_up)) @ w_down

def moe_swiglu(h, w_router, w_gate, w_up, w_down):
    logits = jnp.einsum('bsd,de->bse', h, w_router).astype(jnp.float32)
    top_val, top_idx = lax.top_k(logits, TOP_K)
    gates = jax.nn.softmax(top_val, axis=-1)
    combine = jnp.sum(jax.nn.one_hot(top_idx, N_EXPERTS, dtype=jnp.float32) * gates[..., None],
                      axis=-2).astype(h.dtype)
    out = jnp.zeros_like(h)
    for e in range(N_EXPERTS):
        out = out + combine[..., e:e + 1] * swiglu(h, w_gate[e], w_up[e], w_down[e])
    return out

def setup_inputs(seed: int = 0) -> dict:
    key = jax.random.key(seed)
    ks = iter(jax.random.split(key, 32))
    f32 = jnp.float32

    def w(shape, fan_in):
        return jax.random.normal(next(ks), shape, f32) * (fan_in ** -0.5)

    def gain(shape):
        return 1.0 + 0.05 * jax.random.normal(next(ks), shape, f32)

    return {
        "x": jax.random.normal(next(ks), (BATCH, SEQ, D_MODEL), f32),
        "attn_pre_g": gain((DEPTH, D_MODEL)),
        "attn_post_g": gain((DEPTH, D_MODEL)),
        "ffn_pre_g": gain((DEPTH, D_MODEL)),
        "ffn_post_g": gain((DEPTH, D_MODEL)),
        "w_in": w((DEPTH, D_MODEL, IN_COLS), D_MODEL),
        "q_norm_g": gain((DEPTH, Q_LORA)),
        "kv_norm_g": gain((DEPTH, KV_LORA)),
        "w_uq": w((DEPTH, Q_LORA, N_HEADS, NOPE_DIM + ROPE_DIM), Q_LORA),
        "w_ukv": w((DEPTH, KV_LORA, N_HEADS, NOPE_DIM + V_DIM), KV_LORA),
        "pool_w": w((DEPTH, N_POOL_GROUPS, POOL_GROUP_DIM, POOL_GROUP_DIM), POOL_GROUP_DIM),
        "pool_scale": gain((DEPTH, POOL_WIDTH)),
        "w_out": w((DEPTH, MIX_WIDTH, D_MODEL), MIX_WIDTH),
        "w_gate_d": w((N_DENSE, D_MODEL, D_FF), D_MODEL),
        "w_up_d": w((N_DENSE, D_MODEL, D_FF), D_MODEL),
        "w_down_d": w((N_DENSE, D_FF, D_MODEL), D_FF),
        "w_router": w((N_MOE, D_MODEL, N_EXPERTS), D_MODEL),
        "w_gate_e": w((N_MOE, N_EXPERTS, D_MODEL, D_FF_EXPERT), D_MODEL),
        "w_up_e": w((N_MOE, N_EXPERTS, D_MODEL, D_FF_EXPERT), D_MODEL),
        "w_down_e": w((N_MOE, N_EXPERTS, D_FF_EXPERT, D_MODEL), D_FF_EXPERT),
    }

def reference(x, attn_pre_g, attn_post_g, ffn_pre_g, ffn_post_g, w_in, q_norm_g, kv_norm_g,
              w_uq, w_ukv, pool_w, pool_scale, w_out, w_gate_d, w_up_d, w_down_d,
              w_router, w_gate_e, w_up_e, w_down_e):
    b, seq, _ = x.shape
    cos, sin = rope_tables(seq)
    splits = [Q_LORA, Q_LORA + KV_LORA, Q_LORA + KV_LORA + ROPE_DIM]
    for l in range(DEPTH):
        h = rms_norm(x, attn_pre_g[l])
        z = h @ w_in[l]
        c_q, c_kv, k_rope, u_pool = jnp.split(z, splits, axis=-1)
        q = jnp.einsum('bsc,chd->bshd', rms_norm(c_q, q_norm_g[l]), w_uq[l])
        q_nope, q_rope = q[..., :NOPE_DIM], q[..., NOPE_DIM:]
        kv = jnp.einsum('bsc,chd->bshd', rms_norm(c_kv, kv_norm_g[l]), w_ukv[l])
        k_nope, v = kv[..., :NOPE_DIM], kv[..., NOPE_DIM:]
        q_rope = apply_rope(q_rope, cos[:, None, :], sin[:, None, :])
        k_rope = apply_rope(k_rope, cos, sin)
        a = chunk_causal_mla(q_nope, q_rope, k_nope, k_rope, v).reshape(b, seq, ATTN_WIDTH)
        p = multiscale_pool(u_pool, pool_w[l], pool_scale[l])
        mix = jnp.concatenate([a, p], axis=-1) @ w_out[l]
        x = x + rms_norm(mix, attn_post_g[l])
        h = rms_norm(x, ffn_pre_g[l])
        if l % 2 == 0:
            i = l // 2
            f = swiglu(h, w_gate_d[i], w_up_d[i], w_down_d[i])
        else:
            i = l // 2
            f = moe_swiglu(h, w_router[i], w_gate_e[i], w_up_e[i], w_down_e[i])
        x = x + rms_norm(f, ffn_post_g[l])
    return x


_drawn_inputs = setup_inputs


def setup_inputs(seed=0):
    import zlib

    import numpy as np

    out = dict(_drawn_inputs(seed))
    spreads = {}
    factors = {}
    for name, (base, spread) in spreads.items():
        noise = np.random.default_rng([zlib.crc32(name.encode()), seed]).standard_normal(out[name].shape)
        drawn = base * np.exp(spread * noise) if base else spread * noise
        out[name] = __import__('jax').numpy.asarray(drawn.astype(out[name].dtype))
    for name, factor in factors.items():
        out[name] = (out[name] * factor).astype(out[name].dtype)
    return out
```

```python
import concourse.bass as bass
from concourse import mybir
import numpy as np

P = 128
D = 1024
SEQ = 256
TT = SEQ // P
KD = D // P
DEPTH = 2
CHUNK = 64
EPS = 1e-6
HEADS = 6
NOPE, ROPE, VDIM = 128, 64, 128
QL, KVL = 384, 256
KQ, KKV = QL // P, KVL // P
QK = NOPE + ROPE
KV = NOPE + VDIM
GROUPS, GDIM = 4, 64
WINDOWS = (2, 4, 8, 16)
POOLW = GROUPS * GDIM
IN_COLS = QL + KVL + ROPE + POOLW
HALF_IN = IN_COLS // 2
U0 = QL + KVL + ROPE
THETA = 10000.0
D_FF, D_FFE, EXPERTS = 2816, 3584, 8
FC = 256
KF = FC // P
DCH = D_FF // FC
ECH = D_FFE // FC
SLOTS = P
PASSES = SEQ // SLOTS
HG = 3
KPOS = 3 * P
NEG = -3.0e38
SCALE = float(QK) ** -0.5
BK = 512

SLOT = 2048
RING = 6
WOUT_ORDER = (3, 0, 1, 2)
PIECES = 12
P_IN, P_UQ, P_UKV, P_OUT = 0, (4, 6), (5, 7), 8


def attention_jobs():
    names = [f"hT{i}" for i in range(4)] + [f"z{t}{h}" for t in range(TT) for h in range(2)]
    names += ["cA", "cB", "cC", "kr", "pooled"]

    def projections(g):
        return [f"{n}{g}" for n in ("q01_", "k01_", "qk2_", "r01_", "r2_", "v0_", "v1_")]

    def heads(what, g):
        return [f"{what}{HG * g + i}" for i in range(HG)]

    names += projections(0) + heads("s", 0) + projections(1)
    names += heads("pT", 0) + heads("s", 1) + heads("a", 0) + ["poolout"] + heads("pT", 1) + heads("a", 1)
    names += [f"o{t}{h}" for t in range(TT) for h in range(2)]
    return names


def bank_plan():
    plan, full, used = {}, [0] * 8, [0] * 8

    def give(name, bank, signalled=True):
        plan[name] = (bank, full[bank], used[bank])
        full[bank] += signalled
        used[bank] += 1

    for layer in range(DEPTH):
        for i, n in enumerate(attention_jobs()):
            give((layer, n), i % 8)
        if layer == 0:
            for i in range(4):
                give((layer, f"fT{i}"), i)
            for i in range(4):
                give((layer, f"f{i // 2}{i % 2}"), 4 + i, signalled=False)
        else:
            for i in range(4):
                give((layer, f"fT{i}"), i)
            give((layer, "logits"), 4)
            give((layer, "ranks"), 5)
    return plan, used


JOBS, BANK_USES = bank_plan()

RAW = 0
HI = RAW + RING * SLOT
LO = HI + RING * SLOT
X = LO + RING * SLOT
H = X + TT * D
GPRE = H + TT * D
GPOST = GPRE + D
ET = GPOST + D
FACC = ET + 2 * KD * SEQ
Y = FACC + TT * D
SG = Y + D
ACTS = SG + FC
AT = ACTS + 2 * FC
PICK = AT + 4 * FC
PICKG = PICK + TT * SLOTS
PGT = PICKG + TT * SLOTS
IDENT = PGT + SEQ
IOTA = IDENT + P
SMALL = IOTA + P
SMALL_N = 184
WORDS = SMALL + SMALL_N
HT = HI
Z = HT + KD * SEQ
CN = Z + TT * IN_COLS
CT = CN + TT * (QL + KVL)
RW = CT + (KQ + KKV) * SEQ
ZR = RW + 2 * KQ * HG * 2 * ROPE
KRT = ZR + TT * 2 * ROPE
TA = KRT + SEQ
TB = TA + SEQ
QT = TB + SEQ
QRT = QT + HEADS * SEQ
KT = QRT + HEADS * SEQ
V = KT + HEADS * SEQ
PR = V + TT * HEADS * VDIM
PTT = PR + HEADS * KPOS
MIXT = PTT + HEADS * KPOS
PL = MIXT + KD * SEQ
PWBD = PL + 2 * SEQ
PSC = PWBD + 2 * P
assert PSC + 2 <= X
BANDS = FACC
CS = BANDS + GROUPS * KPOS
assert CS + SEQ <= Y
MASK = Y
GQ = MASK + KPOS
GKV = GQ + QL
assert GKV + KVL <= SG
TRI = Y
ONES = TRI + P
WR = ONES + P
ROUTED_HT = ET


def tables():
    f = np.float32
    ident = np.eye(P, dtype=f)
    iota = np.broadcast_to(np.arange(P, dtype=f), (P, P))
    rev = np.broadcast_to(EXPERTS - np.arange(EXPERTS, dtype=f), (P, EXPERTS))
    inv = (f(1.0) / (f(THETA) ** (np.arange(0, ROPE, 2, dtype=f) / f(ROPE)))).astype(f)
    ang = (np.arange(SEQ, dtype=f)[:, None] * inv[None, :]).astype(f)
    cos, sin = np.cos(ang).T, np.sin(ang).T
    cs = np.concatenate([cos, cos, -sin, sin], axis=0).astype(f)
    s = np.arange(SEQ)[:, None]
    t = np.arange(SEQ)[None, :]
    bands = np.zeros((P, GROUPS, KPOS), f)
    for g, w in enumerate(WINDOWS):
        b = ((s <= t) & (s > t - w)) / np.minimum(t + 1, w) - (s == t)
        bands[:, g, 0:SEQ] = b[0:P]
        bands[:, g, SEQ:KPOS] = b[P:, P:]
    mask = np.zeros((P, KPOS), f)
    mask[0:CHUNK, CHUNK:P] = NEG
    mask[0:CHUNK, KPOS - CHUNK:] = NEG
    tri = np.triu(np.ones((P, P), f), 1)
    ones = np.ones((P, P), f)
    return {
        "c_ident": ident, "c_iota": np.ascontiguousarray(np.concatenate([iota, rev], axis=1)),
        "c_bands": np.ascontiguousarray(np.concatenate([bands.reshape(P, -1), cs], axis=1)),
        "c_mask": mask, "c_rank": np.ascontiguousarray(np.concatenate([tri, ones], axis=1)),
    }


def encoder_kernel(nc, x_in, attn_pre_g, attn_post_g, ffn_pre_g, ffn_post_g, w_in, q_norm_g, kv_norm_g,
                   w_uq, w_ukv, pool_w, pool_scale, w_out, w_gate_d, w_up_d, w_down_d, w_router,
                   w_gate_e, w_up_e, w_down_e, c_ident, c_iota, c_bands, c_mask, c_rank, out):
    f32, f32r, i32 = mybir.dt.float32, mybir.dt.float32r, mybir.dt.int32
    ALU, ACT, AX = mybir.AluOpType, mybir.ActivationFunctionType, mybir.AxisListType
    ts = bass.ds

    base = (nc.sbuf_base + 63) // 64 * 64
    nc.alloc_sbuf_tensor("arena", [P, WORDS + (base - nc.sbuf_base) // 4], f32)

    def at(name, word, shape, dt=f32):
        return nc.alloc_sbuf_tensor_at(name, shape, dt, offset=base + 4 * word)

    raw = at("raw", RAW, [P, RING * SLOT])
    hi = at("hi", HI, [P, RING * SLOT], f32r)
    lo = at("lo", LO, [P, RING * SLOT], f32r)
    x = at("x", X, [P, TT, D])
    h = at("h", H, [P, TT, D])
    gpre = at("gpre", GPRE, [P, D])
    gpost = at("gpost", GPOST, [P, D])
    eT_hi = at("eT_hi", ET, [P, KD, SEQ], f32r)
    eT_lo = at("eT_lo", ET + KD * SEQ, [P, KD, SEQ], f32r)
    facc = at("facc", FACC, [P, TT, D])
    y = at("y", Y, [P, D])
    sg = at("sg", SG, [P, FC])
    acts = at("acts", ACTS, [P, 2, FC])
    aT_hi = at("aT_hi", AT, [P, 2, KF, P], f32r)
    aT_lo = at("aT_lo", AT + 2 * FC, [P, 2, KF, P], f32r)
    pick = at("pick", PICK, [P, TT, SLOTS])
    pick_gated = at("pick_gated", PICKG, [P, TT, SLOTS])
    pgT = at("pgT", PGT, [P, SEQ])
    ident = at("ident", IDENT, [P, P])
    iota = at("iota", IOTA, [P, P])
    small = at("small", SMALL, [P, SMALL_N])
    hT = at("hT", HT, [P, KD, SEQ])
    z = at("z", Z, [P, TT, IN_COLS])
    cn = at("cn", CN, [P, TT, QL + KVL])
    cT = at("cT", CT, [P, KQ + KKV, SEQ])
    rw = at("rw", RW, [P, 2, KQ, HG, 2 * ROPE])
    zr = at("zr", ZR, [P, TT, 2 * ROPE])
    krT = at("krT", KRT, [P, SEQ])
    ta = at("ta", TA, [P, SEQ])
    tb = at("tb", TB, [P, SEQ])
    qT = at("qT", QT, [P, HEADS, SEQ])
    qrT = at("qrT", QRT, [P, HEADS, SEQ])
    kT = at("kT", KT, [P, HEADS, SEQ])
    v = at("v", V, [P, TT, HEADS * VDIM])
    pr = at("pr", PR, [P, HEADS, KPOS])
    prT = at("prT", PTT, [P, HEADS, KPOS])
    mixT = at("mixT", MIXT, [P, KD, SEQ])
    pl = at("pl", PL, [P, 2, SEQ])
    pwbd = at("pwbd", PWBD, [P, 2, P])
    psc = at("psc", PSC, [P, 2])
    bands = at("bands", BANDS, [P, GROUPS, KPOS])
    cs = at("cs", CS, [P, SEQ])
    mask = at("mask", MASK, [P, KPOS])
    gq = at("gq", GQ, [P, QL])
    gkv = at("gkv", GKV, [P, KVL])
    tri = at("tri", TRI, [P, P])
    ones = at("ones", ONES, [P, P])
    wr = at("wr", WR, [P, KD, EXPERTS])
    hT_route = at("hT_route", ROUTED_HT, [P, KD, SEQ])

    cut = [0]

    def col(n):
        a = cut[0]
        cut[0] += n
        return a

    rev = small[:, col(EXPERTS):cut[0]]
    sq = [small[:, col(1):cut[0]] for _ in range(8)]
    root = [small[:, col(1):cut[0]] for _ in range(4)]
    rs = [small[:, col(1):cut[0]] for _ in range(4)]
    softmax_at = cut[0]
    neg_max = small[:, col(2 * HEADS):cut[0]]
    p_sum = small[:, col(2 * HEADS):cut[0]]
    p_inv = small[:, col(2 * HEADS):cut[0]]
    cut[0] = softmax_at

    def per_expert():
        return small[:, col(TT * EXPERTS):cut[0]].rearrange("p (t e) -> p t e", t=TT)

    lg, eq, key, oh1, oh2, lg2, gate, chosen, rank = (per_expert() for _ in range(9))
    m1, m2, kk, gap, e2, g1, g2 = (small[:, col(TT):cut[0]] for _ in range(7))
    most = small[:, col(1):cut[0]]
    assert cut[0] <= SMALL_N
    most_int = nc.alloc_sbuf_tensor("most_int", [P, 1], i32)
    eps = nc.alloc_sbuf_tensor("eps", [P, 1], f32)

    bank = [nc.alloc_psum_tensor(f"bank{i}", [P, BK], f32) for i in range(8)]

    S = nc.alloc_semaphore
    x_loaded, ident_loaded, tables_loaded = S("x_loaded"), S("ident_loaded"), S("tables_loaded")
    gpre_loaded, gpost_loaded, glow_loaded = S("gpre_loaded"), S("gpost_loaded"), S("glow_loaded")
    pool_w_loaded, rank_tables_loaded, out_stored = S("pool_w_loaded"), S("rank_tables_loaded"), S("out_stored")
    piece_loaded = [S(f"piece_loaded{i}") for i in range(RING)]
    piece_used = S("piece_used")
    raw_gu_loaded = [S(f"raw_gu_loaded{i}") for i in range(2)]
    raw_d_loaded = [S(f"raw_d_loaded{i}") for i in range(2)]
    gu_hi, gu_split = S("gu_hi"), S("gu_split")
    d_hi, d_split, d_used = S("d_hi"), S("d_split"), S("d_used")
    bank_full = [S(f"bank_full{i}") for i in range(8)]
    bank_free = [S(f"bank_free{i}") for i in range(8)]
    dve_step = S("dve_step")
    squares = S("squares")
    roots = S("roots")
    mean_ready = S("mean_ready")
    h_ready = S("h_ready")
    x_updated = S("x_updated")
    cn_ready, rope_w_ready, zr_ready, krT_ready = S("cn_ready"), S("rope_w_ready"), S("zr_ready"), S("krT_ready")
    max_ready, exp_ready, probs_ready = S("max_ready"), S("exp_ready"), S("probs_ready")
    pad_ready = S("pad_ready")
    eT_part, eT_ready = S("eT_part"), S("eT_ready")
    gap_ready, e2_ready, chosen_ready = S("gap_ready"), S("e2_ready"), S("chosen_ready")
    routed = S("routed")
    gu_full, silu_done, gated = S("gu_full"), S("silu_done"), S("gated")
    tr_full, aT_part, aT_ready = S("tr_full"), S("aT_part"), S("aT_ready")
    pick_ready, pick_gated_ready = S("pick_ready"), S("pick_gated_ready")
    gathered, pgT_full, pgT_ready = S("gathered"), S("pgT_full"), S("pgT_ready")
    y_ready = S("y_ready")
    spread, added = S("spread"), S("added")
    f_ready = S("f_ready")

    def jb(layer, name):
        return bank[JOBS[layer, name][0]]

    def wait_free(layer, name):
        b, _, n = JOBS[layer, name]
        if n:
            nc.tensor.wait_ge(bank_free[b], n)

    def fill(ins, layer, name):
        ins.then_inc(bank_full[JOBS[layer, name][0]], 1)

    def wait_full(eng, layer, name):
        b, n, _ = JOBS[layer, name]
        eng.wait_ge(bank_full[b], n + 1)

    def wait_drained(eng, layer, *names):
        for name in names:
            b, _, n = JOBS[layer, name]
            eng.wait_ge(bank_free[b], n + 1)

    def z_drained(eng, layer):
        wait_drained(eng, layer, *(f"z{t}{n}" for t in range(TT) for n in range(2)))

    def drain(ins, layer, name):
        ins.then_inc(bank_free[JOBS[layer, name][0]], 1)

    def raw_gu(s):
        return raw[:, 2 * s * SLOT:2 * (s + 1) * SLOT].rearrange("p (k w n) -> p k w n", k=KD, w=2)

    def raw_d(s):
        return raw[:, (4 + s) * SLOT:(5 + s) * SLOT]

    def part_gu(t, s, k):
        a = 2 * s * SLOT + k * 2 * FC
        return t[:, a:a + 2 * FC]

    def half_gu(t, s, i):
        a = 2 * s * SLOT + i * SLOT
        return t[:, a:a + SLOT]

    def part_d(t, s, k, n):
        a = (4 + s) * SLOT + k * D + n * BK
        return t[:, a:a + BK]

    def slot(i):
        return raw[:, i * SLOT:(i + 1) * SLOT]

    def f32v(ap):
        return ap.bitcast(f32)

    DU = DCH * TT

    block = nc.Block()
    with block:
        @block.sync
        def _(sp):
            def attention_loads(layer):
                def piece(i, src, shape):
                    s = i % RING
                    dst = slot(s)[:, 0:shape[0] * shape[1]].rearrange("p (k n) -> p k n", k=shape[0])
                    if i >= RING:
                        sp.wait_ge(piece_used, (PIECES - 1) * layer + i - RING + 1)
                    sp.dma_start(dst, src).then_inc(piece_loaded[s], 16)

                for j in range(4):
                    piece(P_IN + j, w_in[layer, 2 * j * P:2 * (j + 1) * P, :].rearrange("(k p) n -> p k n", p=P),
                          (2, IN_COLS))
                for g in range(2):
                    piece(P_UQ[g], w_uq[layer, :, HG * g:HG * (g + 1), :].rearrange("(k p) h n -> p k (h n)", p=P),
                          (KQ, HG * QK))
                    piece(P_UKV[g], w_ukv[layer, :, HG * g:HG * (g + 1), :].rearrange("(k p) h n -> p k (h n)", p=P),
                          (KKV, HG * KV))
                for i, j in enumerate(WOUT_ORDER):
                    piece(P_OUT + i, w_out[layer, 2 * j * P:2 * (j + 1) * P, :].rearrange("(k p) n -> p k n", p=P),
                          (2, D))

            def load_gu(s, gate_w, up_w):
                sp.dma_start(raw_gu(s)[:, :, 0, :], gate_w).then_inc(raw_gu_loaded[s], 16)
                sp.dma_start(raw_gu(s)[:, :, 1, :], up_w).then_inc(raw_gu_loaded[s], 16)

            def load_d(s, down_w):
                sp.dma_start(raw_d(s).rearrange("p (k n) -> p k n", k=KF), down_w).then_inc(raw_d_loaded[s], 16)

            for t in range(TT):
                sp.dma_start(x[:, t, :], x_in[0, t * P:(t + 1) * P, :]).then_inc(x_loaded, 16)
            sp.dma_start(ident[:, :], c_ident).then_inc(ident_loaded, 16)
            attention_loads(0)

            def dense_gu(c, s):
                load_gu(s, w_gate_d[0, :, ts(c * FC, FC)].rearrange("(k p) n -> p k n", p=P),
                        w_up_d[0, :, ts(c * FC, FC)].rearrange("(k p) n -> p k n", p=P))

            def dense_d(c, s):
                load_d(s, w_down_d[0, ts(c * FC, FC), :].rearrange("(k p) n -> p k n", p=P))

            for c in range(2):
                sp.wait_ge(piece_used, PIECES - RING + 2 * (c + 1))
                dense_gu(c, c)
            sp.wait_ge(piece_used, PIECES - 1)
            dense_d(0, 0)
            wait_full(sp, 0, "o11")
            dense_d(1, 1)

            def dense_chunk(c, s):
                sp.wait_ge(gu_split, (c - 1) * 2)
                dense_gu(c, s)
                sp.wait_ge(d_split, c - 1)
                dense_d(c, s)

            with sp.Fori(1, DCH // 2) as j:
                for s in range(2):
                    dense_chunk(j * 2 + s, s)
            dense_chunk(DCH - 1, 0)
            sp.wait_ge(gu_split, 2 * DCH)
            sp.wait_ge(d_split, DCH)
            attention_loads(1)

            def expert_gu(e, c, s):
                load_gu(s, w_gate_e[0, ts(e, 1), :, ts(c * FC, FC)].rearrange("a (k p) n -> p (a k) n", p=P),
                        w_up_e[0, ts(e, 1), :, ts(c * FC, FC)].rearrange("a (k p) n -> p (a k) n", p=P))

            def expert_d(e, c, s):
                load_d(s, w_down_e[0, ts(e, 1), ts(c * FC, FC), :].rearrange("a (k p) n -> p (a k) n", p=P))

            def expert_chunk(n, e, c, s):
                sp.wait_ge(gu_split, (n + (DCH - 1)) * 2)
                expert_gu(e, c, s)
                sp.wait_ge(d_split, n + (DCH - 1))
                expert_d(e, c, s)

            for c in range(2):
                sp.wait_ge(piece_used, PIECES - 1 + PIECES - RING + 2 * (c + 1))
                expert_gu(0, c, c)
            sp.wait_ge(piece_used, 2 * (PIECES - 1))
            expert_d(0, 0, 0)
            wait_full(sp, 1, "o11")
            expert_d(0, 1, 1)
            with sp.Fori(1, ECH // 2) as j:
                for s in range(2):
                    expert_chunk(j * 2 + s, 0, j * 2 + s, s)
            with sp.Fori(1, EXPERTS) as e:
                with sp.Fori(0, ECH // 2) as j:
                    for s in range(2):
                        expert_chunk(e * ECH + j * 2 + s, e, j * 2 + s, s)
            sp.wait_ge(routed, 1)
            over = sp.value_load(most_int[0:1, 0:1], min_val=0, max_val=SEQ)
            with sp.If(over > SLOTS):
                with sp.Fori(EXPERTS, 2 * EXPERTS) as e:
                    with sp.Fori(0, ECH // 2) as j:
                        for s in range(2):
                            expert_chunk(e * ECH + j * 2 + s, e - EXPERTS, j * 2 + s, s)
            with sp.Else():
                sp.nop()
            for t in range(TT):
                sp.wait_ge(x_updated, 3 * TT + t + 1)
                sp.dma_start(out[0, t * P:(t + 1) * P, :], x[:, t, :]).then_inc(out_stored, 16)
            sp.wait_ge(out_stored, 16 * TT)

        @block.gpsimd
        def _(pool):
            def gains(dst, src, sem):
                pool.dma_start(dst, src.partition_broadcast(P)).then_inc(sem, 16)

            def swapped(dst, src, last):
                half = ROPE // 2
                nc.gpsimd.tensor_copy(dst[..., 0:ROPE], src)
                nc.gpsimd.tensor_copy(dst[..., ROPE:ROPE + half], src[..., half:ROPE])
                nc.gpsimd.tensor_copy(dst[..., ROPE + half:2 * ROPE], src[..., 0:half]).then_inc(last, 1)

            nc.gpsimd.memset(eps[:, :], EPS).then_inc(pad_ready, 1)
            gains(gpre[:, :], attn_pre_g[0, :], gpre_loaded)
            gains(gq[:, :], q_norm_g[0, :], glow_loaded)
            gains(gkv[:, :], kv_norm_g[0, :], glow_loaded)
            pool.dma_start(bands[:, :, :].rearrange("p g n -> p (g n)"), c_bands[:, 0:GROUPS * KPOS]).then_inc(tables_loaded, 16)
            pool.dma_start(cs[:, :], c_bands[:, GROUPS * KPOS:]).then_inc(tables_loaded, 16)
            pool.dma_start(mask[:, :], c_mask).then_inc(tables_loaded, 16)
            pool.dma_start(iota[:, :], c_iota[:, 0:P]).then_inc(tables_loaded, 16)
            pool.dma_start(rev, c_iota[:, P:]).then_inc(tables_loaded, 16)
            gains(gpost[:, :], attn_post_g[0, :], gpost_loaded)
            for layer in range(DEPTH):
                if layer:
                    pool.wait_ge(d_used, DU)
                    gains(gq[:, :], q_norm_g[1, :], glow_loaded)
                    gains(gkv[:, :], kv_norm_g[1, :], glow_loaded)
                nc.gpsimd.memset(pwbd[:, :, :], 0.0).then_inc(pad_ready, 1)
                pool.wait_ge(pad_ready, layer + 2)
                for g in range(GROUPS):
                    a = (g % 2) * GDIM
                    pool.dma_start(pwbd[a:a + GDIM, g // 2, a:a + GDIM], pool_w[layer, g, :, :]).then_inc(pool_w_loaded, 16)
                pool.dma_start(psc[:, :], pool_scale[layer, :].rearrange("(a p) -> p a", p=P),
                               allow_slow_non_contiguous=True).then_inc(pool_w_loaded, 16)
                if layer == 0:
                    pool.wait_ge(h_ready, TT)
                gains_after = ffn_pre_g[layer, :]
                if layer:
                    pool.wait_ge(h_ready, (2 * layer + 1) * TT)
                gains(gpre[:, :], gains_after, gpre_loaded)
                z_drained(pool, layer)
                swapped(zr[:, :, :], z[:, :, QL + KVL:U0], zr_ready)
                for g in range(2):
                    i = P_UQ[g]
                    pool.wait_ge(piece_loaded[i % RING], 16 * (2 * layer + i // RING + 1))
                    w = slot(i % RING)[:, 0:KQ * HG * QK].rearrange("p (k h n) -> p k h n", k=KQ, h=HG)
                    swapped(rw[:, g, :, :, :].rearrange("p k h n -> p (k h) n"),
                            w.rearrange("p k h n -> p (k h) n")[:, :, NOPE:QK], rope_w_ready)
                pool.wait_ge(x_updated, (2 * layer + 1) * TT)
                gains(gpost[:, :], ffn_post_g[layer, :], gpost_loaded)
                if layer == 0:
                    pool.wait_ge(h_ready, 2 * TT)
                    gains(gpre[:, :], attn_pre_g[1, :], gpre_loaded)
                    pool.wait_ge(x_updated, 2 * TT)
                    gains(gpost[:, :], attn_post_g[1, :], gpost_loaded)
                else:
                    pool.dma_start(tri[:, :], c_rank[:, 0:P]).then_inc(rank_tables_loaded, 16)
                    pool.dma_start(ones[:, :], c_rank[:, P:]).then_inc(rank_tables_loaded, 16)
                    pool.dma_start(wr[:, :, :], w_router[0, :, :].rearrange("(k p) e -> p k e", p=P)).then_inc(rank_tables_loaded, 16)

        @block.scalar
        def _(act):
            copy, activation = nc.scalar.copy, nc.scalar.activation
            n_sq, n_mean = [0], [0]

            def square(src, width, dst, junk):
                n_sq[0] += 1
                activation(junk, src, ACT.Square, scale=float(width) ** -0.5, accum_out=dst).then_inc(squares, 1)

            def root_of(dst, src, folded=False):
                if folded:
                    n_mean[0] += 1
                    act.wait_ge(mean_ready, n_mean[0])
                else:
                    act.wait_ge(squares, n_sq[0])
                activation(dst, src, ACT.Sqrt, bias=eps[:, :]).then_inc(roots, 1)

            def norm_of_x(layer, which):
                for t in range(TT):
                    if layer == 0 and which == 0:
                        act.wait_ge(x_loaded, 16 * TT)
                    else:
                        act.wait_ge(x_updated, (2 * layer + which - 1) * TT + t + 1)
                    square(x[:, t, :], D, sq[t], h[:, t, :])
                for t in range(TT):
                    root_of(root[t], sq[t])

            def attention(layer):
                norm_of_x(layer, 0)
                for i in range(0, 4, 2):
                    wait_full(act, layer, f"hT{i}")
                    drain(copy(hT[:, 2 * i:2 * i + 2, :].rearrange("p k n -> p (k n)"), jb(layer, f"hT{i}")[:, :]),
                          layer, f"hT{i}")
                for t in range(TT):
                    wait_full(act, layer, f"z{t}0")
                    drain(copy(z[:, t, 0:HALF_IN], jb(layer, f"z{t}0")[:, 0:HALF_IN]), layer, f"z{t}0")
                z_drained(act, layer)
                for t in range(TT):
                    square(z[:, t, 0:QL], QL, sq[2 * t], h[:, t, 0:QL])
                    square(z[:, t, QL:QL + KVL], KVL, sq[2 * t + 1], h[:, t, QL:QL + KVL])
                for i in range(4):
                    root_of(root[i], sq[i])
                for n, a, w in (("cA", 0, 2), ("cB", 2, 2), ("cC", 4, 1)):
                    wait_full(act, layer, n)
                    ins = copy(cT[:, a:a + w, :].rearrange("p k n -> p (k n)"), jb(layer, n)[:, 0:w * SEQ])
                    drain(ins, layer, n)
                wait_full(act, layer, "pooled")
                drain(copy(pl[:, :, :].rearrange("p a n -> p (a n)"), jb(layer, "pooled")[:, :]), layer, "pooled")

                def projections(g):
                    a = HG * g
                    wait_full(act, layer, f"q01_{g}")
                    drain(copy(qT[:, a:a + 2, :].rearrange("p k n -> p (k n)"), jb(layer, f"q01_{g}")[:, :]),
                          layer, f"q01_{g}")
                    wait_full(act, layer, f"k01_{g}")
                    drain(copy(kT[:, a:a + 2, :].rearrange("p k n -> p (k n)"), jb(layer, f"k01_{g}")[:, :]),
                          layer, f"k01_{g}")
                    wait_full(act, layer, f"qk2_{g}")
                    copy(qT[:, a + 2, :], jb(layer, f"qk2_{g}")[:, 0:SEQ])
                    drain(copy(kT[:, a + 2, :], jb(layer, f"qk2_{g}")[:, SEQ:2 * SEQ]), layer, f"qk2_{g}")

                def exps(g):
                    for i in range(HG * g, HG * (g + 1)):
                        act.wait_ge(max_ready, HEADS * layer + i + 1)
                        for b, (a, w) in enumerate(((0, P), (P, SEQ))):
                            last = activation(pr[:, i, a:a + w], pr[:, i, a:a + w], ACT.Exp,
                                              bias=neg_max[:, 2 * i + b:2 * i + b + 1],
                                              accum_out=p_sum[:, 2 * i + b:2 * i + b + 1])
                        last.then_inc(exp_ready, 1)

                def transposed(g):
                    for i in range(HG * g, HG * (g + 1)):
                        wait_full(act, layer, f"pT{i}")
                        drain(copy(prT[:, i, :], jb(layer, f"pT{i}")[:, 0:KPOS]), layer, f"pT{i}")

                def attended(g):
                    for i in range(HG * g, HG * (g + 1)):
                        wait_full(act, layer, f"a{i}")
                        drain(copy(mixT[:, i, :], jb(layer, f"a{i}")[:, 0:SEQ]), layer, f"a{i}")

                projections(0)
                exps(0)
                projections(1)
                transposed(0)
                exps(1)
                attended(0)
                transposed(1)
                attended(1)
                for t in range(TT):
                    for n in range(2):
                        wait_full(act, layer, f"o{t}{n}")
                        square(jb(layer, f"o{t}{n}")[:, :], D, sq[2 * t + n], h[:, t, n * BK:(n + 1) * BK])
                for t in range(TT):
                    root_of(root[t], sq[2 * t], folded=True)

            def round_gu(s, i, loaded=None, used=None):
                if loaded is not None:
                    act.wait_ge(raw_gu_loaded[s], loaded)
                if used is not None:
                    act.wait_ge(gu_full, used)
                copy(half_gu(hi, s, i), half_gu(raw, s, i)).then_inc(gu_hi, 1)

            def round_d(s, loaded, used=None):
                act.wait_ge(raw_d_loaded[s], loaded)
                if used is not None:
                    act.wait_ge(d_used, used)
                copy(hi[:, (4 + s) * SLOT:(5 + s) * SLOT], raw_d(s)).then_inc(d_hi, 1)

            def round_aT(u, s):
                act.wait_ge(tr_full, u + 1)
                act.wait_ge(d_used, u - 1)
                copy(aT_hi[:, s, :, :].rearrange("p k n -> p (k n)"), bank[2 + s][:, 0:FC]).then_inc(aT_part, 1)

            def silu(u, s):
                act.wait_ge(gu_full, u + 1)
                act.wait_ge(gated, u)
                activation(sg[:, :], bank[s][:, 0:FC], ACT.Silu).then_inc(silu_done, 1)

            def dense():
                norm_of_x(0, 1)
                for i in range(4):
                    wait_full(act, 0, f"fT{i}")
                    copy(eT_hi[:, 2 * i:2 * i + 2, :].rearrange("p k n -> p (k n)"), jb(0, f"fT{i}")[:, :])\
                        .then_inc(eT_part, 1)

                def unit(c, t, s, first=False, more=True):
                    u = c * 2 + t
                    if t == 0:
                        round_d(s, loaded_d(c, s), None if isinstance(c, int) and c < 2 else (c - 1) * 2)
                    if not (first and t == 0):
                        if first:
                            act.wait_ge(tr_full, 1)
                            copy(aT_hi[:, 0, :, :].rearrange("p k n -> p (k n)"), bank[2][:, 0:FC]).then_inc(aT_part, 1)
                        else:
                            round_aT(u - 1, 1 - t)
                    if more:
                        if t == 0:
                            round_gu(1 - s, 0, loaded_gu(c + 1, 1 - s), None if first else c * 2)
                        else:
                            round_gu(1 - s, 1)
                    silu(u, t)

                def loaded_gu(c, s):
                    return ((c - s) // 2 + 1) * 32 if isinstance(c, int) else (c - s) * 16 + 32

                def loaded_d(c, s):
                    return ((c - s) // 2 + 1) * 16 if isinstance(c, int) else (c - s) * 8 + 16

                for i in range(2):
                    round_gu(0, i, 32 if i == 0 else None)
                for t in range(TT):
                    unit(0, t, 0, first=True)
                for t in range(TT):
                    unit(1, t, 1)
                with act.Fori(1, DCH // 2) as j:
                    for s in range(2):
                        for t in range(TT):
                            unit(j * 2 + s, t, s)
                for t in range(TT):
                    unit(DCH - 1, t, 0, more=False)
                round_aT(DU - 1, 1)
                for t in range(TT):
                    act.wait_ge(d_used, DU - 1 + t)
                    for n in range(2):
                        square(jb(0, f"f{t}{n}")[:, :], D, sq[2 * t + n], h[:, t, n * BK:(n + 1) * BK])
                for t in range(TT):
                    root_of(root[t], sq[2 * t], folded=True)

            def route():
                norm_of_x(1, 1)
                for i in range(0, 4, 2):
                    wait_full(act, 1, f"fT{i}")
                    drain(copy(hT_route[:, 2 * i:2 * i + 2, :].rearrange("p k n -> p (k n)"), jb(1, f"fT{i}")[:, :]),
                          1, f"fT{i}")
                act.wait_ge(gap_ready, 1)
                activation(e2, gap, ACT.Exp).then_inc(e2_ready, 1)

            PRE = ((DCH + 1) // 2, DCH // 2)

            def gathered_rounded(e):
                for i in range(2):
                    act.wait_ge(gathered, e * 2 + i + 1)
                    copy(eT_hi[:, 4 * i:4 * i + 4, 0:SLOTS], bank[6 + i][:, :].rearrange("p (k n) -> p k n", k=4))\
                        .then_inc(eT_part, 1)

            def sums_out(e):
                act.wait_ge(d_used, e * ECH + (ECH + DU))
                copy(y[:, 0:BK], bank[4][:, :]).then_inc(y_ready, 1)

            def expert(e, first_one, last_one):
                def one(c_pair, s, more=True):
                    start = isinstance(c_pair, int) and c_pair == 0 and s == 0
                    tail = isinstance(c_pair, int) and c_pair == ECH // 2 - 1 and s == 1
                    n = e * ECH + c_pair * 2 + s
                    k = e * (ECH // 2) + c_pair
                    u = n + DU
                    round_d(s, (k + 1 + PRE[s]) * 16, n + (DU - 1))
                    if not start:
                        round_aT(u - 1, 1 - s)
                    if more:
                        round_gu(1 - s, 0, (k + s + 1 + PRE[1 - s]) * 32, u)
                    if start and not first_one:
                        sums_out(e - 1)
                    silu(u, s)
                    if tail:
                        if not last_one:
                            act.wait_ge(gu_full, u + 1)
                            gathered_rounded(e + 1)
                        round_aT(u, s)
                        act.wait_ge(pgT_full, e + 1)
                        copy(pgT[:, :], bank[0][:, 0:SEQ]).then_inc(pgT_ready, 1)
                    if more:
                        round_gu(1 - s, 1)

                for s in range(2):
                    one(0, s)
                with act.Fori(1, ECH // 2 - 1) as j:
                    for s in range(2):
                        one(j, s)
                one(ECH // 2 - 1, 0)
                one(ECH // 2 - 1, 1, more=not last_one)

            def experts(first):
                k = first * (ECH // 2)
                gathered_rounded(first)
                for i in range(2):
                    round_gu(0, i, (k + 1 + PRE[0]) * 32 if i == 0 else None, first * ECH + DU - 1 if i == 0 else None)
                expert(first, True, False)
                with act.Fori(first + 1, first + EXPERTS - 1) as e:
                    expert(e, False, False)
                expert(first + EXPERTS - 1, False, True)
                sums_out(first + EXPERTS - 1)

            act.wait_ge(pad_ready, 1)
            attention(0)
            dense()
            attention(1)
            route()
            act.wait_ge(routed, 1)
            over = act.value_load(most_int[0:1, 0:1], min_val=0, max_val=SEQ)
            experts(0)
            with act.If(over > SLOTS):
                experts(EXPERTS)
            with act.Else():
                act.nop()
            act.wait_ge(f_ready, 1)
            for t in range(TT):
                square(facc[:, t, :], D, sq[t], h[:, t, :])
            for t in range(TT):
                root_of(root[t], sq[t])

        @block.vector
        def _(dve):
            V_ = nc.vector
            step, n_sq, n_root = [0], [0], [0]

            def link(ins):
                step[0] += 1
                ins.then_inc(dve_step, 1)
                dve.wait_ge(dve_step, step[0])

            def squares_of(parts, fold):
                n_sq[0] += parts
                if fold:
                    dve.wait_ge(squares, n_sq[0])
                    for t in range(TT):
                        V_.tensor_tensor(sq[2 * t], sq[2 * t], sq[2 * t + 1], ALU.add).then_inc(mean_ready, 1)

            def inverse_roots(n):
                for i in range(n):
                    n_root[0] += 1
                    dve.wait_ge(roots, n_root[0])
                    link(V_.reciprocal(rs[i], root[i]))

            def pre_norm(n_gain):
                squares_of(TT, False)
                inverse_roots(TT)
                dve.wait_ge(gpre_loaded, 16 * n_gain)
                for t in range(TT):
                    V_.scalar_tensor_tensor(h[:, t, :], x[:, t, :], rs[t], gpre[:, :], ALU.mult, ALU.mult)\
                        .then_inc(h_ready, 1)

            def post_norm(layer, name, n_gain):
                squares_of(2 * TT, True)
                inverse_roots(TT)
                dve.wait_ge(gpost_loaded, 16 * n_gain)
                for t in range(TT):
                    for n in range(2):
                        a = n * BK
                        ins = V_.scalar_tensor_tensor(h[:, t, a:a + BK], jb(layer, f"{name}{t}{n}")[:, :], rs[t],
                                                      gpost[:, a:a + BK], ALU.mult, ALU.mult)
                        drain(ins, layer, f"{name}{t}{n}")
                    wait_drained(dve, layer, f"{name}{t}0", f"{name}{t}1")
                    V_.tensor_tensor(x[:, t, :], x[:, t, :], h[:, t, :], ALU.add).then_inc(x_updated, 1)

            def attention(layer):
                pre_norm(2 * layer + 1)
                for i in range(1, 4, 2):
                    wait_full(dve, layer, f"hT{i}")
                    drain(V_.tensor_copy(hT[:, 2 * i:2 * i + 2, :].rearrange("p k n -> p (k n)"),
                                         jb(layer, f"hT{i}")[:, :]), layer, f"hT{i}")
                for t in range(TT):
                    wait_full(dve, layer, f"z{t}1")
                    drain(V_.tensor_copy(z[:, t, HALF_IN:IN_COLS], jb(layer, f"z{t}1")[:, 0:HALF_IN]), layer, f"z{t}1")
                z_drained(dve, layer)
                squares_of(4, False)
                inverse_roots(4)
                dve.wait_ge(glow_loaded, 32 * (layer + 1))
                for t in range(TT):
                    for i, (a, w, g) in enumerate(((0, QL, gq), (QL, KVL, gkv))):
                        V_.scalar_tensor_tensor(cn[:, t, a:a + w], z[:, t, a:a + w], rs[2 * t + i], g[:, :],
                                                ALU.mult, ALU.mult).then_inc(cn_ready, 1)
                dve.wait_ge(tables_loaded, 80)
                wait_full(dve, layer, "kr")
                kr = jb(layer, "kr")
                V_.tensor_tensor(ta[0:ROPE, :], kr[0:ROPE, 0:SEQ], cs[0:ROPE, :], ALU.mult)
                ins = V_.tensor_tensor(tb[0:ROPE, :], kr[ROPE:P, 0:SEQ], cs[ROPE:P, :], ALU.mult)
                drain(ins, layer, "kr")
                wait_drained(dve, layer, "kr")
                link(V_.tensor_tensor(krT[0:ROPE, :], ta[0:ROPE, :], tb[0:ROPE, :], ALU.add))
                V_.tensor_copy(krT[ROPE:P, :], krT[0:ROPE, :]).then_inc(krT_ready, 1)

                def projections(g):
                    a = HG * g
                    wait_full(dve, layer, f"r01_{g}")
                    csb = cs[:, :].unsqueeze(1).broadcast_to([P, 2, SEQ])
                    drain(V_.tensor_tensor(qrT[:, a:a + 2, :], jb(layer, f"r01_{g}")[:, :].rearrange("p (k n) -> p k n", k=2),
                                           csb, ALU.mult), layer, f"r01_{g}")
                    wait_full(dve, layer, f"r2_{g}")
                    drain(V_.tensor_tensor(qrT[:, a + 2, :], jb(layer, f"r2_{g}")[:, 0:SEQ], cs[:, :], ALU.mult),
                          layer, f"r2_{g}")
                    for t in range(TT):
                        wait_full(dve, layer, f"v{t}_{g}")
                        drain(V_.tensor_copy(v[:, t, a * VDIM:(a + HG) * VDIM], jb(layer, f"v{t}_{g}")[:, 0:HG * VDIM]),
                              layer, f"v{t}_{g}")

                def maxima(g):
                    for i in range(HG * g, HG * (g + 1)):
                        wait_full(dve, layer, f"s{i}")
                        ins = V_.scalar_tensor_tensor(pr[:, i, :], jb(layer, f"s{i}")[:, 0:KPOS], SCALE, mask[:, :],
                                                      ALU.mult, ALU.add)
                        drain(ins, layer, f"s{i}")
                        wait_drained(dve, layer, f"s{i}")
                        V_.tensor_reduce(neg_max[:, 2 * i:2 * i + 1], pr[:, i, 0:P], AX.X, ALU.max, negate=True)
                        V_.tensor_reduce(neg_max[:, 2 * i + 1:2 * i + 2], pr[:, i, P:KPOS], AX.X, ALU.max, negate=True)\
                            .then_inc(max_ready, 1)

                def normalized(g):
                    for i in range(HG * g, HG * (g + 1)):
                        dve.wait_ge(exp_ready, HEADS * layer + i + 1)
                        link(V_.reciprocal(p_inv[:, 2 * i:2 * i + 2], p_sum[:, 2 * i:2 * i + 2]))
                        V_.tensor_scalar(pr[:, i, 0:P], pr[:, i, 0:P], p_inv[:, 2 * i:2 * i + 1], None, ALU.mult)
                        V_.tensor_scalar(pr[:, i, P:KPOS], pr[:, i, P:KPOS], p_inv[:, 2 * i + 1:2 * i + 2], None,
                                         ALU.mult).then_inc(probs_ready, 1)

                projections(0)
                maxima(0)
                projections(1)
                normalized(0)
                maxima(1)
                normalized(1)
                dve.wait_ge(pool_w_loaded, 16 * (GROUPS + 1) * (layer + 1))
                wait_full(dve, layer, "poolout")
                po = jb(layer, "poolout")
                V_.tensor_scalar(mixT[:, HEADS, :], po[:, 0:SEQ], psc[:, 0:1], None, ALU.mult)
                drain(V_.tensor_scalar(mixT[:, HEADS + 1, :], po[:, SEQ:2 * SEQ], psc[:, 1:2], None, ALU.mult),
                      layer, "poolout")
                post_norm(layer, "o", 2 * layer + 1)

            def low_gu(s, i, n):
                dve.wait_ge(gu_hi, n)
                a = 2 * s * SLOT + i * SLOT
                V_.tensor_tensor(lo[:, a:a + SLOT], raw[:, a:a + SLOT], f32v(hi[:, a:a + SLOT]), ALU.subtract)\
                    .then_inc(gu_split, 1)

            def low_d(s, n):
                dve.wait_ge(d_hi, n)
                a = (4 + s) * SLOT
                V_.tensor_tensor(lo[:, a:a + SLOT], raw[:, a:a + SLOT], f32v(hi[:, a:a + SLOT]), ALU.subtract)\
                    .then_inc(d_split, 1)

            def low_aT(u, s):
                dve.wait_ge(aT_part, u + 1)
                V_.tensor_tensor(aT_lo[:, s, :, :].rearrange("p k n -> p (k n)"), bank[2 + s][:, 0:FC],
                                 f32v(aT_hi[:, s, :, :]).rearrange("p k n -> p (k n)"), ALU.subtract)\
                    .then_inc(aT_ready, 1)

            def gate_up(u, s):
                dve.wait_ge(silu_done, u + 1)
                V_.tensor_tensor(acts[:, s, :], sg[:, :], bank[s][:, FC:2 * FC], ALU.mult).then_inc(gated, 1)

            def dense():
                pre_norm(2)
                for i in range(4):
                    dve.wait_ge(eT_part, i + 1)
                    drain(V_.tensor_tensor(eT_lo[:, 2 * i:2 * i + 2, :].rearrange("p k n -> p (k n)"), jb(0, f"fT{i}")[:, :],
                                           f32v(eT_hi[:, 2 * i:2 * i + 2, :]).rearrange("p k n -> p (k n)"), ALU.subtract),
                          0, f"fT{i}")

                def unit(c, t, s, first=False, more=True):
                    u = c * 2 + t
                    if t == 0:
                        low_d(s, c + 1)
                    if not (first and t == 0):
                        low_aT(u - 1, 1 - t)
                    if more:
                        low_gu(1 - s, t, c * 2 + (3 + t))
                    gate_up(u, t)

                for i in range(2):
                    low_gu(0, i, i + 1)
                for t in range(TT):
                    unit(0, t, 0, first=True)
                for t in range(TT):
                    unit(1, t, 1)
                with dve.Fori(1, DCH // 2) as j:
                    for s in range(2):
                        for t in range(TT):
                            unit(j * 2 + s, t, s)
                for t in range(TT):
                    unit(DCH - 1, t, 0, more=False)
                low_aT(DU - 1, 1)
                post_norm(0, "f", 2)

            def route():
                pre_norm(4)
                for i in range(1, 4, 2):
                    wait_full(dve, 1, f"fT{i}")
                    drain(V_.tensor_copy(hT_route[:, 2 * i:2 * i + 2, :].rearrange("p k n -> p (k n)"),
                                         jb(1, f"fT{i}")[:, :]), 1, f"fT{i}")
                def over_e(a):
                    return a.unsqueeze(2).broadcast_to([P, TT, EXPERTS])

                revb = rev.unsqueeze(1).broadcast_to([P, TT, EXPERTS])
                wait_full(dve, 1, "logits")
                ins = V_.tensor_copy(lg, jb(1, "logits")[:, 0:TT * EXPERTS].rearrange("p (t e) -> p t e", t=TT))
                drain(ins, 1, "logits")
                wait_drained(dve, 1, "logits")

                def top(src, m, oh):
                    link(V_.tensor_reduce(m, src, AX.X, ALU.max))
                    link(V_.tensor_tensor(eq, src, over_e(m), ALU.is_equal))
                    link(V_.tensor_tensor(key, eq, revb, ALU.mult))
                    link(V_.tensor_reduce(kk, key, AX.X, ALU.max))
                    link(V_.tensor_tensor(oh, key, over_e(kk), ALU.is_equal))

                top(lg, m1, oh1)
                link(V_.scalar_tensor_tensor(lg2, oh1, NEG, lg, ALU.mult, ALU.add))
                top(lg2, m2, oh2)
                V_.tensor_tensor(gap, m2, m1, ALU.subtract).then_inc(gap_ready, 1)
                V_.tensor_tensor(chosen, oh1, oh2, ALU.add).then_inc(chosen_ready, 1)
                dve.wait_ge(e2_ready, 1)
                link(V_.tensor_scalar(g2, e2, 1.0, None, ALU.add))
                link(V_.reciprocal(g1, g2))
                link(V_.tensor_tensor(g2, e2, g1, ALU.mult))
                V_.tensor_tensor(gate, oh1, over_e(g1), ALU.mult)
                link(V_.tensor_tensor(eq, oh2, over_e(g2), ALU.mult))
                link(V_.tensor_tensor(gate, gate, eq, ALU.add))
                wait_full(dve, 1, "ranks")
                rk = jb(1, "ranks")
                V_.tensor_copy(rank, rk[:, 0:TT * EXPERTS].rearrange("p (t e) -> p t e", t=TT))
                ins = V_.tensor_reduce(most, rk[:, TT * EXPERTS:(TT + 1) * EXPERTS], AX.X, ALU.max)
                drain(ins, 1, "ranks")
                wait_drained(dve, 1, "ranks")
                V_.tensor_copy(most_int[:, :], most).then_inc(routed, 1)
                link(V_.memset(facc[:, :, :], 0.0))

            def picks(e, col_e):
                for t in range(TT):
                    last = V_.tensor_scalar(pick[:, t, :], iota[:, :], rank[:, t, ts(col_e, 1)], chosen[:, t, ts(col_e, 1)],
                                            ALU.is_equal, ALU.mult)
                last.then_inc(pick_ready, 1)

            def picks_gated(e, col_e):
                for t in range(TT):
                    last = V_.tensor_scalar(pick_gated[:, t, :], iota[:, :], rank[:, t, ts(col_e, 1)], gate[:, t, ts(col_e, 1)],
                                            ALU.is_equal, ALU.mult)
                last.then_inc(pick_gated_ready, 1)

            def gathered_low(e):
                for i in range(2):
                    dve.wait_ge(eT_part, e * 2 + (i + 5))
                    V_.tensor_tensor(eT_lo[:, 4 * i:4 * i + 4, 0:SLOTS], bank[6 + i][:, :].rearrange("p (k n) -> p k n", k=4),
                                     f32v(eT_hi[:, 4 * i:4 * i + 4, 0:SLOTS]), ALU.subtract).then_inc(eT_ready, 1)

            def sums_out(e):
                dve.wait_ge(d_used, e * ECH + (ECH + DU))
                V_.tensor_copy(y[:, BK:2 * BK], bank[5][:, :]).then_inc(y_ready, 1)

            def add(e, t):
                for n in range(2):
                    dve.wait_ge(spread, e * 4 + (2 * t + n + 1))
                    V_.tensor_tensor(facc[:, t, n * BK:(n + 1) * BK], facc[:, t, n * BK:(n + 1) * BK],
                                     bank[6 + n][:, :], ALU.add).then_inc(added, 1)

            def expert(e, first, first_one, last_one):
                def one(c_pair, s, more=True):
                    start = isinstance(c_pair, int) and c_pair == 0 and s == 0
                    tail = isinstance(c_pair, int) and c_pair == ECH // 2 - 1 and s == 1
                    n = e * ECH + c_pair * 2 + s
                    u = n + DU
                    low_d(s, n + (DCH + 1))
                    if not start:
                        low_aT(u - 1, 1 - s)
                    if more:
                        low_gu(1 - s, 0, (n + (DCH + 1)) * 2 + 1)
                    if start and not first_one:
                        sums_out(e - 1)
                    gate_up(u, s)
                    if tail:
                        if not last_one:
                            gathered_low(e + 1)
                        low_aT(u, s)
                    if more:
                        low_gu(1 - s, 1, (n + (DCH + 1)) * 2 + 2)

                one(0, 0)
                if not last_one:
                    picks(e + 1, e - (first - 1))
                if not (first_one and first == 0):
                    dve.wait_ge(pgT_full, e)
                picks_gated(e, e - first)
                if not first_one:
                    add(e - 1, 0)
                one(0, 1)
                if not first_one:
                    add(e - 1, 1)
                with dve.Fori(1, ECH // 2 - 1) as j:
                    for s in range(2):
                        one(j, s)
                one(ECH // 2 - 1, 0)
                one(ECH // 2 - 1, 1, more=not last_one)

            def experts(first):
                picks(first, 0)
                gathered_low(first)
                k = first * ECH + DCH
                for i in range(2):
                    low_gu(0, i, 2 * k + i + 1)
                expert(first, first, True, False)
                with dve.Fori(first + 1, first + EXPERTS - 1) as e:
                    expert(e, first, False, False)
                last = first + EXPERTS - 1
                expert(last, first, False, True)
                sums_out(last)
                dve.wait_ge(added, last * 4)
                for t in range(TT):
                    add(last, t)
                dve.wait_ge(added, last * 4 + 4)

            attention(0)
            dense()
            attention(1)
            route()
            dve.wait_ge(routed, 1)
            over = dve.value_load(most_int[0:1, 0:1], min_val=0, max_val=SEQ)
            experts(0)
            with dve.If(over > SLOTS):
                V_.tensor_scalar(rank, rank, -float(SLOTS), None, ALU.add).then_inc(routed, 1)
                dve.wait_ge(routed, 2)
                experts(EXPERTS)
            with dve.Else():
                dve.nop()
            dve.sem_inc(f_ready, 1)
            squares_of(TT, False)
            inverse_roots(TT)
            dve.wait_ge(gpost_loaded, 16 * 4)
            for t in range(TT):
                link(V_.scalar_tensor_tensor(h[:, t, :], facc[:, t, :], rs[t], gpost[:, :], ALU.mult, ALU.mult))
                V_.tensor_tensor(x[:, t, :], x[:, t, :], h[:, t, :], ALU.add).then_inc(x_updated, 1)

        @block.tensor
        def _(pe):
            mm = nc.tensor.matmul

            def transposes(layer, name, n_h):
                pe.wait_ge(ident_loaded, 16)
                pe.wait_ge(h_ready, n_h)
                for i in range(4):
                    wait_free(layer, f"{name}{i}")
                    b = jb(layer, f"{name}{i}")
                    for k in range(2):
                        for t in range(TT):
                            last = nc.tensor.transpose(b[:, k * SEQ + t * P:k * SEQ + (t + 1) * P],
                                                       h[:, t, (2 * i + k) * P:(2 * i + k + 1) * P], ident[:, :])
                    fill(last, layer, f"{name}{i}")

            def attention(layer):
                def loaded(i):
                    if layer == 0:
                        n = i // RING + 1
                    else:
                        n = 2 + i // RING + 1
                    pe.wait_ge(piece_loaded[i % RING], 16 * n)

                def drained(*names):
                    wait_drained(pe, layer, *names)

                transposes(layer, "hT", (2 * layer) * TT + TT)
                zb = [[f"z{t}{n}" for n in range(2)] for t in range(TT)]
                for t in range(TT):
                    for n in range(2):
                        wait_free(layer, zb[t][n])
                for j in range(4):
                    loaded(P_IN + j)
                    drained(f"hT{j}")
                    w = slot((P_IN + j) % RING)[:, 0:2 * IN_COLS].rearrange("p (k n) -> p k n", k=2)
                    for k in range(2):
                        for t in range(TT):
                            for n in range(2):
                                last = mm(jb(layer, zb[t][n])[:, 0:HALF_IN], hT[:, 2 * j + k, t * P:(t + 1) * P],
                                          w[:, k, n * HALF_IN:(n + 1) * HALF_IN],
                                          start=(j == 0 and k == 0), stop=(j == 3 and k == 1))
                                if j == 3 and k == 1:
                                    fill(last, layer, zb[t][n])
                    if j < 3:
                        last.then_inc(piece_used, 1)

                pe.wait_ge(cn_ready, 4 * (layer + 1))
                for n, blocks in (("cA", (0, 1)), ("cB", (2, 3)), ("cC", (4,))):
                    wait_free(layer, n)
                    for j, k in enumerate(blocks):
                        for t in range(TT):
                            last = nc.tensor.transpose(jb(layer, n)[:, j * SEQ + t * P:j * SEQ + (t + 1) * P],
                                                       cn[:, t, k * P:(k + 1) * P], ident[:, :])
                            if k == 0 and t == 0:
                                last.then_inc(piece_used, 1)
                    fill(last, layer, n)
                pe.wait_ge(zr_ready, layer + 1)
                wait_free(layer, "kr")
                for t in range(TT):
                    last = nc.tensor.transpose(jb(layer, "kr")[:, t * P:(t + 1) * P], zr[:, t, :], ident[:, :])
                fill(last, layer, "kr")

                pe.wait_ge(tables_loaded, 80)
                wait_free(layer, "pooled")
                for g in range(GROUPS):
                    a, c = (g % 2) * GDIM, (g // 2) * SEQ
                    o = jb(layer, "pooled")
                    u = [z[:, t, U0 + g * GDIM:U0 + (g + 1) * GDIM] for t in range(TT)]
                    mm(o[a:a + GDIM, c:c + P], u[0], bands[:, g, 0:P], start=True, stop=True)
                    mm(o[a:a + GDIM, c + P:c + SEQ], u[0], bands[:, g, P:SEQ], start=True, stop=False)
                    last = mm(o[a:a + GDIM, c + P:c + SEQ], u[1], bands[:, g, SEQ:KPOS], start=False, stop=True)
                fill(last, layer, "pooled")

                def over_k(dst, ks, lhs, rhs, name=None, piece_before=False):
                    for k in range(ks):
                        last = mm(dst, lhs(k), rhs(k), start=(k == 0), stop=(k == ks - 1))
                        if piece_before and k == 0:
                            last.then_inc(piece_used, 1)
                    if name:
                        fill(last, layer, name)

                def projections(g):
                    loaded(P_UQ[g])
                    wq = slot(P_UQ[g] % RING)[:, 0:KQ * HG * QK].rearrange("p (k h n) -> p k h n", k=KQ, h=HG)
                    wkv = slot(P_UKV[g] % RING)[:, 0:KKV * HG * KV].rearrange("p (k h n) -> p k h n", k=KKV, h=HG)
                    if g == 0:
                        drained("cA", "cB", "cC")

                    def q(dst, i, name=None):
                        over_k(dst, KQ, lambda k: wq[:, k, i, 0:NOPE], lambda k: cT[:, k, :], name)

                    def key(dst, i, name=None):
                        over_k(dst, KKV, lambda k: wkv[:, k, i, 0:NOPE], lambda k: cT[:, KQ + k, :], name)

                    def rope(dst, i, name=None):
                        over_k(dst, KQ, lambda k: rw[:, g, k, i, :], lambda k: cT[:, k, :], name)

                    wait_free(layer, f"q01_{g}")
                    q(jb(layer, f"q01_{g}")[:, 0:SEQ], 0)
                    q(jb(layer, f"q01_{g}")[:, SEQ:2 * SEQ], 1, f"q01_{g}")
                    loaded(P_UKV[g])
                    wait_free(layer, f"k01_{g}")
                    key(jb(layer, f"k01_{g}")[:, 0:SEQ], 0)
                    key(jb(layer, f"k01_{g}")[:, SEQ:2 * SEQ], 1, f"k01_{g}")
                    wait_free(layer, f"qk2_{g}")
                    q(jb(layer, f"qk2_{g}")[:, 0:SEQ], 2)
                    key(jb(layer, f"qk2_{g}")[:, SEQ:2 * SEQ], 2, f"qk2_{g}")
                    pe.wait_ge(rope_w_ready, 2 * layer + g + 1)
                    wait_free(layer, f"r01_{g}")
                    rope(jb(layer, f"r01_{g}")[:, 0:SEQ], 0)
                    rope(jb(layer, f"r01_{g}")[:, SEQ:2 * SEQ], 1, f"r01_{g}")
                    wait_free(layer, f"r2_{g}")
                    rope(jb(layer, f"r2_{g}")[:, 0:SEQ], 2, f"r2_{g}")
                    for t in range(TT):
                        wait_free(layer, f"v{t}_{g}")
                        over_k(jb(layer, f"v{t}_{g}")[:, 0:HG * VDIM].rearrange("p (h n) -> p h n", h=HG), KKV,
                               lambda k: cT[:, KQ + k, t * P:(t + 1) * P], lambda k: wkv[:, k, :, NOPE:KV], f"v{t}_{g}",
                               piece_before=(t == 0))

                def scores(g):
                    drained(f"q01_{g}", f"k01_{g}", f"qk2_{g}", f"r01_{g}", f"r2_{g}")
                    pe.wait_ge(krT_ready, layer + 1)
                    for i in range(HG * g, HG * (g + 1)):
                        wait_free(layer, f"s{i}")
                        o = jb(layer, f"s{i}")
                        for b, (a, w) in enumerate(((0, P), (P, SEQ))):
                            ins = mm(o[:, a:a + w], qT[:, i, b * P:(b + 1) * P], kT[:, i, 0:w], start=True, stop=False)
                            if i == 0 and b == 0:
                                ins.then_inc(piece_used, 1)
                            last = mm(o[:, a:a + w], qrT[:, i, b * P:(b + 1) * P], krT[:, 0:w], start=False, stop=True)
                        fill(last, layer, f"s{i}")

                def transposed(g):
                    for i in range(HG * g, HG * (g + 1)):
                        wait_free(layer, f"pT{i}")
                        pe.wait_ge(probs_ready, HEADS * layer + i + 1)
                        for j in range(3):
                            last = nc.tensor.transpose(jb(layer, f"pT{i}")[:, j * P:(j + 1) * P],
                                                       pr[:, i, j * P:(j + 1) * P], ident[:, :])
                            if i == 0 and j == 0:
                                last.then_inc(piece_used, 1)
                        fill(last, layer, f"pT{i}")

                def attended(g):
                    drained(f"v0_{g}", f"v1_{g}")
                    for i in range(HG * g, HG * (g + 1)):
                        drained(f"pT{i}")
                        wait_free(layer, f"a{i}")
                        o = jb(layer, f"a{i}")
                        vi = [v[:, t, i * VDIM:(i + 1) * VDIM] for t in range(TT)]
                        mm(o[:, 0:P], vi[0], prT[:, i, 0:P], start=True, stop=True)
                        mm(o[:, P:SEQ], vi[0], prT[:, i, P:2 * P], start=True, stop=False)
                        last = mm(o[:, P:SEQ], vi[1], prT[:, i, 2 * P:3 * P], start=False, stop=True)
                        fill(last, layer, f"a{i}")

                projections(0)
                scores(0)
                projections(1)
                transposed(0)
                scores(1)
                attended(0)
                drained("pooled")
                pe.wait_ge(pool_w_loaded, 16 * (GROUPS + 1) * (layer + 1))
                wait_free(layer, "poolout")
                for a in range(2):
                    last = mm(jb(layer, "poolout")[:, a * SEQ:(a + 1) * SEQ], pwbd[:, a, :], pl[:, a, :],
                              start=True, stop=True)
                fill(last, layer, "poolout")
                transposed(1)
                attended(1)
                for t in range(TT):
                    for n in range(2):
                        wait_free(layer, f"o{t}{n}")
                for i, j in enumerate(WOUT_ORDER):
                    loaded(P_OUT + i)
                    if j == 3:
                        drained("poolout")
                    else:
                        drained(f"a{2 * j}", f"a{2 * j + 1}")
                    w = slot((P_OUT + i) % RING).rearrange("p (k n) -> p k n", k=2)
                    for k in range(2):
                        for t in range(TT):
                            for n in range(2):
                                last = mm(jb(layer, f"o{t}{n}")[:, :], mixT[:, 2 * j + k, t * P:(t + 1) * P],
                                          w[:, k, n * BK:(n + 1) * BK], start=(i == 0 and k == 0), stop=(i == 3 and k == 1))
                                if i == 3 and k == 1:
                                    fill(last, layer, f"o{t}{n}")
                    if i < 3:
                        last.then_inc(piece_used, 1)

            def split_mm(dst, a_hi, a_lo, b_hi, b_lo, start, stop):
                mm(dst, a_hi, b_hi, start=start, stop=False)
                mm(dst, a_hi, b_lo, start=False, stop=False)
                return mm(dst, a_lo, b_hi, start=False, stop=stop)

            def gate_up(s, b, tok, ks):
                for k in ks:
                    last = split_mm(bank[b][:, :], eT_hi[:, k, tok], eT_lo[:, k, tok],
                                    part_gu(hi, s, k), part_gu(lo, s, k), k == 0, k == KD - 1)
                return last

            def turn(s):
                for k in range(KF):
                    last = nc.tensor.transpose(bank[2 + s][:, k * P:(k + 1) * P], acts[:, s, k * P:(k + 1) * P], ident[:, :])
                last.then_inc(tr_full, 1)

            def down(s_w, s_a, b0, start, stop):
                for n in range(2):
                    for k in range(KF):
                        last = split_mm(bank[b0 + n][:, :], aT_hi[:, s_a, k, :], aT_lo[:, s_a, k, :],
                                        part_d(hi, s_w, k, n), part_d(lo, s_w, k, n),
                                        start and k == 0, stop and k == KF - 1)
                last.then_inc(d_used, 1)

            FIRST_K, SECOND_K = range(0, KD // 2), range(KD // 2, KD)

            def dense():
                transposes(0, "fT", 2 * TT)
                wait_drained(pe, 0, *(f"fT{i}" for i in range(4)))
                for t in range(TT):
                    for n in range(2):
                        wait_free(0, f"f{t}{n}")

                def unit(c, t, s, first=False, start=False, stop=False):
                    u = c * 2 + t
                    pe.wait_ge(gu_split, c * 2 + 1)
                    if not first:
                        pe.wait_ge(gated, u - 1)
                    tok = slice(t * P, (t + 1) * P)
                    gate_up(s, t, tok, FIRST_K)
                    if not (first and t == 0):
                        pe.wait_ge(gated, u)
                        if not (isinstance(u, int) and u < 3):
                            pe.wait_ge(aT_ready, u - 2)
                        turn(1 - t)
                    pe.wait_ge(gu_split, c * 2 + 2)
                    last = gate_up(s, t, tok, SECOND_K)
                    last.then_inc(gu_full, 1)
                    if not (first and t == 0):
                        pe.wait_ge(aT_ready, u)
                        if t == 0:
                            down(1 - s, 1, 6, start, stop)
                        else:
                            pe.wait_ge(d_split, c + 1)
                            down(s, 0, 4, start, stop)

                unit(0, 0, 0, first=True)
                unit(0, 1, 0, first=True, start=True)
                unit(1, 0, 1, start=True)
                unit(1, 1, 1)
                with pe.Fori(1, DCH // 2) as j:
                    for s in range(2):
                        for t in range(TT):
                            unit(j * 2 + s, t, s)
                unit(DCH - 1, 0, 0)
                unit(DCH - 1, 1, 0, stop=True)
                pe.wait_ge(gated, DU)
                turn(1)
                pe.wait_ge(aT_ready, DU)
                down(0, 1, 6, False, True)

            def route():
                transposes(1, "fT", 4 * TT)
                wait_drained(pe, 1, *(f"fT{i}" for i in range(4)))
                pe.wait_ge(rank_tables_loaded, 48)
                wait_free(1, "logits")
                for t in range(TT):
                    for k in range(KD):
                        last = mm(jb(1, "logits")[:, t * EXPERTS:(t + 1) * EXPERTS], hT_route[:, k, t * P:(t + 1) * P],
                                  wr[:, k, :], start=(k == 0), stop=(k == KD - 1))
                fill(last, 1, "logits")
                pe.wait_ge(chosen_ready, 1)
                wait_free(1, "ranks")
                o = jb(1, "ranks")
                mm(o[:, 0:EXPERTS], tri[:, :], chosen[:, 0, :], start=True, stop=True)
                mm(o[:, EXPERTS:2 * EXPERTS], ones[:, :], chosen[:, 0, :], start=True, stop=False)
                mm(o[:, EXPERTS:2 * EXPERTS], tri[:, :], chosen[:, 1, :], start=False, stop=True)
                mm(o[:, 2 * EXPERTS:3 * EXPERTS], ones[:, :], chosen[:, 0, :], start=True, stop=False)
                last = mm(o[:, 2 * EXPERTS:3 * EXPERTS], ones[:, :], chosen[:, 1, :], start=False, stop=True)
                fill(last, 1, "ranks")
                for b in range(8):
                    pe.wait_ge(bank_free[b], BANK_USES[b])

            def gather(e):
                pe.wait_ge(pick_ready, e + 1)
                for i in range(2):
                    for k in range(4):
                        for t in range(TT):
                            last = mm(bank[6 + i][:, k * P:(k + 1) * P], h[:, t, (4 * i + k) * P:(4 * i + k + 1) * P],
                                      pick[:, t, :], start=(t == 0), stop=(t == TT - 1))
                    last.then_inc(gathered, 1)

            tok = slice(0, SLOTS)

            def scatter(e, t):
                if t == 0:
                    pe.wait_ge(y_ready, e * 2 + 2)
                else:
                    pe.wait_ge(added, e * 4 + 2)
                for n in range(2):
                    mm(bank[6 + n][:, :], pgT[:, t * P:(t + 1) * P], y[:, n * BK:(n + 1) * BK],
                       start=True, stop=True).then_inc(spread, 1)

            def expert(e, first_one, last_one):
                def one(c_pair, s):
                    start = isinstance(c_pair, int) and c_pair == 0 and s == 0
                    n = e * ECH + c_pair * 2 + s
                    u = n + DU
                    q = n + DCH
                    pe.wait_ge(gu_split, q * 2 + 1)
                    pe.wait_ge(gated, u - 1)
                    gate_up(s, s, tok, FIRST_K)
                    if not start:
                        pe.wait_ge(gated, u)
                        pe.wait_ge(aT_ready, u - 2)
                        turn(1 - s)
                    pe.wait_ge(gu_split, q * 2 + 2)
                    gate_up(s, s, tok, SECOND_K).then_inc(gu_full, 1)
                    if not start:
                        pe.wait_ge(aT_ready, u)
                        pe.wait_ge(d_split, q)
                        down(1 - s, 1 - s, 4, isinstance(c_pair, int) and c_pair == 0, False)

                pe.wait_ge(eT_ready, e * 2 + 2)
                if not first_one:
                    pe.wait_ge(pgT_ready, e)
                for s in range(2):
                    one(0, s)
                    if not first_one:
                        scatter(e - 1, s)
                with pe.Fori(1, ECH // 2 - 1) as j:
                    for s in range(2):
                        one(j, s)
                one(ECH // 2 - 1, 0)
                if not last_one:
                    if not first_one:
                        pe.wait_ge(added, e * 4)
                    gather(e + 1)
                one(ECH // 2 - 1, 1)
                u = e * ECH + (ECH - 1 + DU)
                pe.wait_ge(gated, u + 1)
                turn(1)
                pe.wait_ge(pick_gated_ready, e + 1)
                for t in range(TT):
                    last = nc.tensor.transpose(bank[0][:, t * P:(t + 1) * P], pick_gated[:, t, :], ident[:, :])
                last.then_inc(pgT_full, 1)
                pe.wait_ge(aT_ready, u + 1)
                pe.wait_ge(d_split, u + (DCH - DU + 1))
                down(1, 1, 4, False, True)

            def experts(first):
                gather(first)
                expert(first, True, False)
                with pe.Fori(first + 1, first + EXPERTS - 1) as e:
                    expert(e, False, False)
                last = first + EXPERTS - 1
                expert(last, False, True)
                pe.wait_ge(pgT_ready, last + 1)
                for t in range(TT):
                    scatter(last, t)
                pe.wait_ge(added, last * 4 + 4)

            attention(0)
            dense()
            attention(1)
            route()
            pe.wait_ge(routed, 1)
            over = pe.value_load(most_int[0:1, 0:1], min_val=0, max_val=SEQ)
            experts(0)
            with pe.If(over > SLOTS):
                experts(EXPERTS)
            with pe.Else():
                pe.nop()


_INS = ["x", "attn_pre_g", "attn_post_g", "ffn_pre_g", "ffn_post_g", "w_in", "q_norm_g", "kv_norm_g", "w_uq", "w_ukv",
        "pool_w", "pool_scale", "w_out", "w_gate_d", "w_up_d", "w_down_d", "w_router", "w_gate_e", "w_up_e", "w_down_e"]


def kernel(**inputs):
    import concourse.bacc as bacc
    from concourse.bass_utils import run_bass_kernel_spmd

    nc = bacc.Bacc("TRN2", target_bir_lowering=False, num_devices=1)
    arrays, args = {}, []
    given = {n: np.ascontiguousarray(inputs[n]) for n in _INS} | tables()
    for name, a in given.items():
        arrays[f"in_{name}"] = a
        args.append(nc.dram_tensor(f"in_{name}", a.shape, mybir.dt.from_np(a.dtype), kind="ExternalInput").ap())
    out = nc.dram_tensor("out_0", (1, SEQ, D), mybir.dt.float32, kind="ExternalOutput").ap()
    encoder_kernel(nc, *args, out)
    r = run_bass_kernel_spmd(nc, [arrays], core_ids=[0])
    return r.results[0]["out_0"]
```

```python
import concourse.bass as bass
from concourse import mybir
import numpy as np

P = 128
D = 1024
SEQ = 256
TT = SEQ // P
KD = D // P
DEPTH = 2
CHUNK = 64
EPS = 1e-6
HEADS = 6
NOPE, ROPE, VDIM = 128, 64, 128
QL, KVL = 384, 256
KQ, KKV = QL // P, KVL // P
QK = NOPE + ROPE
KV = NOPE + VDIM
GROUPS, GDIM = 4, 64
WINDOWS = (2, 4, 8, 16)
POOLW = GROUPS * GDIM
IN_COLS = QL + KVL + ROPE + POOLW
HALF_IN = IN_COLS // 2
U0 = QL + KVL + ROPE
THETA = 10000.0
D_FF, D_FFE, EXPERTS = 2816, 3584, 8
FC = 256
KF = FC // P
DCH = D_FF // FC
ECH = D_FFE // FC
SLOTS = P
PASSES = SEQ // SLOTS
HG = 3
KPOS = 3 * P
NEG = -3.0e38
SCALE = float(QK) ** -0.5
BK = 512

SLOT = 2048
RING = 6
WOUT_ORDER = (3, 0, 1, 2)
PIECES = 12
P_IN, P_UQ, P_UKV, P_OUT = 0, (4, 6), (5, 7), 8


def attention_jobs():
    names = ["hT00", "hT01", "z00", "z01", "hT10", "hT11", "z10", "z11", "cA0", "cB0", "cA1", "pooled"]

    def projections(g, between=()):
        return [f"q01_{g}", f"r01_{g}", f"qr2_{g}", *between, f"k01_{g}", f"k2_{g}", f"v0_{g}", f"v1_{g}"]

    def heads(what, g):
        return [f"{what}{HG * g + i}" for i in range(HG)]

    names += projections(0, ("cB1",)) + heads("s", 0) + projections(1)
    names += heads("pT", 0) + heads("s", 1) + heads("a", 0) + ["poolout"] + heads("pT", 1) + heads("a", 1)
    return names


def bank_plan():
    plan, full, used, after_attention = {}, [0] * 8, [0] * 8, []

    def give(name, bank, signalled=True):
        plan[name] = (bank, full[bank], used[bank])
        full[bank] += signalled
        used[bank] += 1

    for layer in range(DEPTH):
        for i, n in enumerate(attention_jobs()):
            give((layer, n), i % 8)
        for t, first in enumerate((6, 4)):
            for n in range(2):
                give((layer, f"o{t}{n}"), first + n)
        for t in range(TT):
            for i in range(2):
                give((layer, f"fT{t}{i}"), 2 + i)
        if layer:
            give((layer, "logits"), 0)
            give((layer, "ranks"), 1)
        after_attention.append(list(used))
        if layer == 0:
            for i in range(4):
                give((layer, f"f{i // 2}{i % 2}"), 4 + i, signalled=False)
    return plan, after_attention


JOBS, USES_BEFORE_UNITS = bank_plan()

RAW = 0
HI = RAW + RING * SLOT
LO = HI + RING * SLOT
X = LO + RING * SLOT
H = X + TT * D
GPRE = H + TT * D
GPOST = GPRE + D
ET = GPOST + D
FACC = ET + 2 * KD * SEQ
Y = FACC + TT * D
SG = Y + D
ACTS = SG + FC
AT = ACTS + 2 * FC
PICK = AT + 4 * FC
PICKG = PICK + TT * SLOTS
PGT = PICKG + TT * SLOTS
IDENT = PGT + SEQ
IOTA = IDENT + P
SMALL = IOTA + P
SMALL_N = 196
WORDS = SMALL + SMALL_N
HT = HI
Z = HT + KD * SEQ
CN = Z + TT * IN_COLS
CT = CN + TT * (QL + KVL)
RW = CT + (KQ + KKV) * SEQ
ZR = RW + 2 * KQ * HG * 2 * ROPE
KRT = ZR + TT * 2 * ROPE
TA = KRT + SEQ
TB = TA + SEQ
QT = TB + SEQ
QRT = QT + HEADS * SEQ
KT = QRT + HEADS * SEQ
V = KT + HEADS * SEQ
PR = V + TT * HEADS * VDIM
PTT = PR + HEADS * KPOS
MIXT = PTT + HEADS * KPOS
PL = MIXT + KD * SEQ
PWBD = PL + 2 * SEQ
PSC = PWBD + 2 * P
assert PSC + 2 <= X
BANDS = FACC
CS = BANDS + GROUPS * KPOS
assert CS + SEQ <= Y
MASK = Y
GQ = MASK + KPOS
GKV = GQ + QL
assert GKV + KVL <= SG
TRI = Y
ONES = TRI + P
WR = ONES + P
ROUTED_HT = ET


def tables():
    f = np.float32
    ident = np.eye(P, dtype=f)
    iota = np.broadcast_to(np.arange(P, dtype=f), (P, P))
    rev = np.broadcast_to(EXPERTS - np.arange(EXPERTS, dtype=f), (P, EXPERTS))
    inv = (f(1.0) / (f(THETA) ** (np.arange(0, ROPE, 2, dtype=f) / f(ROPE)))).astype(f)
    ang = (np.arange(SEQ, dtype=f)[:, None] * inv[None, :]).astype(f)
    cos, sin = np.cos(ang).T, np.sin(ang).T
    cs = np.concatenate([cos, cos, -sin, sin], axis=0).astype(f)
    s = np.arange(SEQ)[:, None]
    t = np.arange(SEQ)[None, :]
    bands = np.zeros((P, GROUPS, KPOS), f)
    for g, w in enumerate(WINDOWS):
        b = ((s <= t) & (s > t - w)) / np.minimum(t + 1, w) - (s == t)
        bands[:, g, 0:SEQ] = b[0:P]
        bands[:, g, SEQ:KPOS] = b[P:, P:]
    mask = np.zeros((P, KPOS), f)
    mask[0:CHUNK, CHUNK:P] = NEG
    mask[0:CHUNK, KPOS - CHUNK:] = NEG
    tri = np.triu(np.ones((P, P), f), 1)
    ones = np.ones((P, P), f)
    return {
        "c_ident": ident, "c_iota": np.ascontiguousarray(np.concatenate([iota, rev], axis=1)),
        "c_bands": np.ascontiguousarray(np.concatenate([bands.reshape(P, -1), cs], axis=1)),
        "c_mask": mask, "c_rank": np.ascontiguousarray(np.concatenate([tri, ones], axis=1)),
    }


def encoder_kernel(nc, x_in, attn_pre_g, attn_post_g, ffn_pre_g, ffn_post_g, w_in, q_norm_g, kv_norm_g,
                   w_uq, w_ukv, pool_w, pool_scale, w_out, w_gate_d, w_up_d, w_down_d, w_router,
                   w_gate_e, w_up_e, w_down_e, c_ident, c_iota, c_bands, c_mask, c_rank, out):
    f32, f32r, i32 = mybir.dt.float32, mybir.dt.float32r, mybir.dt.int32
    ALU, ACT, AX = mybir.AluOpType, mybir.ActivationFunctionType, mybir.AxisListType
    ts = bass.ds

    base = (nc.sbuf_base + 63) // 64 * 64
    nc.alloc_sbuf_tensor("arena", [P, WORDS + (base - nc.sbuf_base) // 4], f32)

    def at(name, word, shape, dt=f32):
        return nc.alloc_sbuf_tensor_at(name, shape, dt, offset=base + 4 * word)

    raw = at("raw", RAW, [P, RING * SLOT])
    hi = at("hi", HI, [P, RING * SLOT], f32r)
    lo = at("lo", LO, [P, RING * SLOT], f32r)
    x = at("x", X, [P, TT, D])
    h = at("h", H, [P, TT, D])
    gpre = at("gpre", GPRE, [P, D])
    gpost = at("gpost", GPOST, [P, D])
    eT_hi = at("eT_hi", ET, [P, KD, SEQ], f32r)
    eT_lo = at("eT_lo", ET + KD * SEQ, [P, KD, SEQ], f32r)
    facc = at("facc", FACC, [P, TT, D])
    y = at("y", Y, [P, D])
    sg = at("sg", SG, [P, FC])
    acts = at("acts", ACTS, [P, 2, FC])
    aT_hi = at("aT_hi", AT, [P, 2, KF, P], f32r)
    aT_lo = at("aT_lo", AT + 2 * FC, [P, 2, KF, P], f32r)
    pick = at("pick", PICK, [P, TT, SLOTS])
    pick_gated = at("pick_gated", PICKG, [P, TT, SLOTS])
    pgT = at("pgT", PGT, [P, SEQ])
    ident = at("ident", IDENT, [P, P])
    iota = at("iota", IOTA, [P, P])
    small = at("small", SMALL, [P, SMALL_N])
    hT = at("hT", HT, [P, KD, SEQ])
    z = at("z", Z, [P, TT, IN_COLS])
    cn = at("cn", CN, [P, TT, QL + KVL])
    cT = at("cT", CT, [P, KQ + KKV, SEQ])
    rw = at("rw", RW, [P, 2, KQ, HG, 2 * ROPE])
    zr = at("zr", ZR, [P, TT, 2 * ROPE])
    krT = at("krT", KRT, [P, SEQ])
    ta = at("ta", TA, [P, SEQ])
    tb = at("tb", TB, [P, SEQ])
    qT = at("qT", QT, [P, HEADS, SEQ])
    qrT = at("qrT", QRT, [P, HEADS, SEQ])
    kT = at("kT", KT, [P, HEADS, SEQ])
    v = at("v", V, [P, TT, HEADS * VDIM])
    pr = at("pr", PR, [P, HEADS, KPOS])
    prT = at("prT", PTT, [P, HEADS, KPOS])
    mixT = at("mixT", MIXT, [P, KD, SEQ])
    pl = at("pl", PL, [P, 2, SEQ])
    pwbd = at("pwbd", PWBD, [P, 2, P])
    psc = at("psc", PSC, [P, 2])
    bands = at("bands", BANDS, [P, GROUPS, KPOS])
    cs = at("cs", CS, [P, SEQ])
    mask = at("mask", MASK, [P, KPOS])
    gq = at("gq", GQ, [P, QL])
    gkv = at("gkv", GKV, [P, KVL])
    tri = at("tri", TRI, [P, P])
    ones = at("ones", ONES, [P, P])
    wr = at("wr", WR, [P, KD, EXPERTS])
    hT_route = at("hT_route", ROUTED_HT, [P, KD, SEQ])
    junk = at("junk", PICK, [P, D], mybir.dt.bfloat16)

    cut = [0]

    def col(n):
        a = cut[0]
        cut[0] += n
        return a

    rev = small[:, col(EXPERTS):cut[0]]
    NORMS = [(n, t) for n in ("x", "kv", "q", "f") for t in range(TT)]
    sq, root, rs = ({n: small[:, col(1):cut[0]] for n in NORMS} for _ in range(3))
    sq_half = [small[:, col(1):cut[0]] for _ in range(TT)]
    softmax_at = cut[0]
    neg_max = small[:, col(2 * HEADS):cut[0]]
    p_sum = small[:, col(2 * HEADS):cut[0]]
    p_inv = small[:, col(2 * HEADS):cut[0]]
    cut[0] = softmax_at

    def per_expert():
        return small[:, col(TT * EXPERTS):cut[0]].rearrange("p (t e) -> p t e", t=TT)

    lg, eq, key, oh1, oh2, lg2, gate, chosen, rank = (per_expert() for _ in range(9))
    m1, m2, kk, gap, e2, g1, g2 = (small[:, col(TT):cut[0]] for _ in range(7))
    most = small[:, col(1):cut[0]]
    eps = small[:, col(1):cut[0]]
    most_int = small[:, col(1):cut[0]].bitcast(i32)
    assert cut[0] <= SMALL_N

    bank = [nc.alloc_psum_tensor(f"bank{i}", [P, BK], f32) for i in range(8)]

    S = nc.alloc_semaphore
    x_loaded = [S(f"x_loaded{t}") for t in range(TT)]
    ident_loaded, tables_loaded = S("ident_loaded"), S("tables_loaded")
    gpre_loaded, gpost_loaded, glow_loaded = S("gpre_loaded"), S("gpost_loaded"), S("glow_loaded")
    pool_w_loaded, rank_tables_loaded, out_stored = S("pool_w_loaded"), S("rank_tables_loaded"), S("out_stored")
    piece_loaded = [S(f"piece_loaded{i}") for i in range(RING)]
    piece_used = S("piece_used")
    raw_gu_loaded = [S(f"raw_gu_loaded{i}") for i in range(2)]
    raw_d_loaded = [S(f"raw_d_loaded{i}") for i in range(2)]
    gu_hi, gu_split = S("gu_hi"), S("gu_split")
    d_hi, d_split, d_used = S("d_hi"), S("d_split"), S("d_used")
    bank_full = [S(f"bank_full{i}") for i in range(8)]
    bank_free = [S(f"bank_free{i}") for i in range(8)]
    dve_step = S("dve_step")
    squares = S("squares")
    roots = S("roots")
    mean_ready = S("mean_ready")
    rs_ready = S("rs_ready")
    h_ready = S("h_ready")
    x_updated = S("x_updated")
    cn_ready, rope_w_ready, zr_ready, krT_ready = S("cn_ready"), S("rope_w_ready"), S("zr_ready"), S("krT_ready")
    max_ready, exp_ready, probs_ready = S("max_ready"), S("exp_ready"), S("probs_ready")
    pad_ready = S("pad_ready")
    eT_part, eT_ready = S("eT_part"), S("eT_ready")
    gap_ready, e2_ready, chosen_ready = S("gap_ready"), S("e2_ready"), S("chosen_ready")
    routed = S("routed")
    gu_full, silu_done, gated = S("gu_full"), S("silu_done"), S("gated")
    tr_full, aT_part, aT_ready = S("tr_full"), S("aT_part"), S("aT_ready")
    pick_ready, pick_gated_ready = S("pick_ready"), S("pick_gated_ready")
    gathered, pgT_full, pgT_ready = S("gathered"), S("pgT_full"), S("pgT_ready")
    y_ready = S("y_ready")
    spread, added = S("spread"), S("added")
    f_ready = S("f_ready")

    def jb(layer, name):
        return bank[JOBS[layer, name][0]]

    def wait_free(layer, name):
        b, _, n = JOBS[layer, name]
        if n:
            nc.tensor.wait_ge(bank_free[b], n)

    def fill(ins, layer, name):
        ins.then_inc(bank_full[JOBS[layer, name][0]], 1)

    def wait_full(eng, layer, name):
        b, n, _ = JOBS[layer, name]
        eng.wait_ge(bank_full[b], n + 1)

    def wait_drained(eng, layer, *names):
        for name in names:
            b, _, n = JOBS[layer, name]
            eng.wait_ge(bank_free[b], n + 1)

    def z_drained(eng, layer, t):
        wait_drained(eng, layer, f"z{t}0", f"z{t}1")

    root_no, square_no = {}, {}

    def drain(ins, layer, name):
        ins.then_inc(bank_free[JOBS[layer, name][0]], 1)

    def bank_k(layer, name, k=4):
        return jb(layer, name)[:, 0:k * P].rearrange("p (k n) -> p k n", k=k)

    def raw_gu(s):
        return raw[:, 2 * s * SLOT:2 * (s + 1) * SLOT].rearrange("p (k w n) -> p k w n", k=KD, w=2)

    def raw_d(s):
        return raw[:, (4 + s) * SLOT:(5 + s) * SLOT]

    def part_gu(t, s, k):
        a = 2 * s * SLOT + k * 2 * FC
        return t[:, a:a + 2 * FC]

    def half_gu(t, s, i):
        a = 2 * s * SLOT + i * SLOT
        return t[:, a:a + SLOT]

    def part_d(t, s, k, n):
        a = (4 + s) * SLOT + k * D + n * BK
        return t[:, a:a + BK]

    def slot(i):
        return raw[:, i * SLOT:(i + 1) * SLOT]

    def f32v(ap):
        return ap.bitcast(f32)

    DU = DCH * TT

    block = nc.Block()
    with block:
        @block.sync
        def _(sp):
            def attention_loads(layer):
                def piece(i, src, shape):
                    s = i % RING
                    dst = slot(s)[:, 0:shape[0] * shape[1]].rearrange("p (k n) -> p k n", k=shape[0])
                    if i >= RING:
                        sp.wait_ge(piece_used, (PIECES - 1) * layer + i - RING + 1)
                    sp.dma_start(dst, src).then_inc(piece_loaded[s], 16)

                for j in range(4):
                    piece(P_IN + j, w_in[layer, 2 * j * P:2 * (j + 1) * P, :].rearrange("(k p) n -> p k n", p=P),
                          (2, IN_COLS))
                for g in range(2):
                    piece(P_UQ[g], w_uq[layer, :, HG * g:HG * (g + 1), :].rearrange("(k p) h n -> p k (h n)", p=P),
                          (KQ, HG * QK))
                    piece(P_UKV[g], w_ukv[layer, :, HG * g:HG * (g + 1), :].rearrange("(k p) h n -> p k (h n)", p=P),
                          (KKV, HG * KV))
                for i, j in enumerate(WOUT_ORDER):
                    piece(P_OUT + i, w_out[layer, 2 * j * P:2 * (j + 1) * P, :].rearrange("(k p) n -> p k n", p=P),
                          (2, D))

            def load_gu(s, gate_w, up_w):
                sp.dma_start(raw_gu(s)[:, :, 0, :], gate_w).then_inc(raw_gu_loaded[s], 16)
                sp.dma_start(raw_gu(s)[:, :, 1, :], up_w).then_inc(raw_gu_loaded[s], 16)

            def load_d(s, down_w):
                sp.dma_start(raw_d(s).rearrange("p (k n) -> p k n", k=KF), down_w).then_inc(raw_d_loaded[s], 16)

            for t in range(TT):
                sp.dma_start(x[:, t, :], x_in[0, t * P:(t + 1) * P, :]).then_inc(x_loaded[t], 16)
            sp.dma_start(ident[:, :], c_ident).then_inc(ident_loaded, 16)
            attention_loads(0)

            def dense_gu(c, s):
                load_gu(s, w_gate_d[0, :, ts(c * FC, FC)].rearrange("(k p) n -> p k n", p=P),
                        w_up_d[0, :, ts(c * FC, FC)].rearrange("(k p) n -> p k n", p=P))

            def dense_d(c, s):
                load_d(s, w_down_d[0, ts(c * FC, FC), :].rearrange("(k p) n -> p k n", p=P))

            for c in range(2):
                sp.wait_ge(piece_used, PIECES - RING + 2 * (c + 1))
                dense_gu(c, c)
            sp.wait_ge(piece_used, PIECES - 1)
            dense_d(0, 0)
            wait_full(sp, 0, "o11")
            dense_d(1, 1)

            def dense_chunk(c, s):
                sp.wait_ge(gu_split, (c - 1) * 2)
                dense_gu(c, s)
                sp.wait_ge(d_split, c - 1)
                dense_d(c, s)

            with sp.Fori(1, DCH // 2) as j:
                for s in range(2):
                    dense_chunk(j * 2 + s, s)
            dense_chunk(DCH - 1, 0)
            sp.wait_ge(gu_split, 2 * DCH)
            sp.wait_ge(d_split, DCH)
            attention_loads(1)

            def expert_gu(e, c, s):
                load_gu(s, w_gate_e[0, ts(e, 1), :, ts(c * FC, FC)].rearrange("a (k p) n -> p (a k) n", p=P),
                        w_up_e[0, ts(e, 1), :, ts(c * FC, FC)].rearrange("a (k p) n -> p (a k) n", p=P))

            def expert_d(e, c, s):
                load_d(s, w_down_e[0, ts(e, 1), ts(c * FC, FC), :].rearrange("a (k p) n -> p (a k) n", p=P))

            def expert_chunk(n, e, c, s):
                sp.wait_ge(gu_split, (n + (DCH - 1)) * 2)
                expert_gu(e, c, s)
                sp.wait_ge(d_split, n + (DCH - 1))
                expert_d(e, c, s)

            for c in range(2):
                sp.wait_ge(piece_used, PIECES - 1 + PIECES - RING + 2 * (c + 1))
                expert_gu(0, c, c)
            sp.wait_ge(piece_used, 2 * (PIECES - 1))
            expert_d(0, 0, 0)
            wait_full(sp, 1, "o11")
            expert_d(0, 1, 1)
            with sp.Fori(1, ECH // 2) as j:
                for s in range(2):
                    expert_chunk(j * 2 + s, 0, j * 2 + s, s)
            with sp.Fori(1, EXPERTS) as e:
                with sp.Fori(0, ECH // 2) as j:
                    for s in range(2):
                        expert_chunk(e * ECH + j * 2 + s, e, j * 2 + s, s)
            sp.wait_ge(routed, 1)
            over = sp.value_load(most_int[0:1, 0:1], min_val=0, max_val=SEQ)
            with sp.If(over > SLOTS):
                with sp.Fori(EXPERTS, 2 * EXPERTS) as e:
                    with sp.Fori(0, ECH // 2) as j:
                        for s in range(2):
                            expert_chunk(e * ECH + j * 2 + s, e - EXPERTS, j * 2 + s, s)
            with sp.Else():
                sp.nop()
            for t in range(TT):
                sp.wait_ge(x_updated, 3 * TT + t + 1)
                sp.dma_start(out[0, t * P:(t + 1) * P, :], x[:, t, :]).then_inc(out_stored, 16)
            sp.wait_ge(out_stored, 16 * TT)

        @block.gpsimd
        def _(pool):
            def gains(dst, src, sem):
                pool.dma_start(dst, src.partition_broadcast(P)).then_inc(sem, 16)

            def swapped(dst, src, last):
                half = ROPE // 2
                nc.gpsimd.tensor_copy(dst[..., 0:ROPE], src)
                nc.gpsimd.tensor_copy(dst[..., ROPE:ROPE + half], src[..., half:ROPE])
                nc.gpsimd.tensor_copy(dst[..., ROPE + half:2 * ROPE], src[..., 0:half]).then_inc(last, 1)

            nc.gpsimd.memset(eps[:, :], EPS).then_inc(pad_ready, 1)
            gains(gpre[:, :], attn_pre_g[0, :], gpre_loaded)
            gains(gq[:, :], q_norm_g[0, :], glow_loaded)
            gains(gkv[:, :], kv_norm_g[0, :], glow_loaded)
            pool.dma_start(bands[:, :, :].rearrange("p g n -> p (g n)"), c_bands[:, 0:GROUPS * KPOS]).then_inc(tables_loaded, 16)
            pool.dma_start(cs[:, :], c_bands[:, GROUPS * KPOS:]).then_inc(tables_loaded, 16)
            pool.dma_start(mask[:, :], c_mask).then_inc(tables_loaded, 16)
            pool.dma_start(iota[:, :], c_iota[:, 0:P]).then_inc(tables_loaded, 16)
            pool.dma_start(rev, c_iota[:, P:]).then_inc(tables_loaded, 16)
            gains(gpost[:, :], attn_post_g[0, :], gpost_loaded)
            for layer in range(DEPTH):
                if layer:
                    pool.wait_ge(d_used, DU)
                    gains(gq[:, :], q_norm_g[1, :], glow_loaded)
                    gains(gkv[:, :], kv_norm_g[1, :], glow_loaded)
                nc.gpsimd.memset(pwbd[:, :, :], 0.0).then_inc(pad_ready, 1)
                pool.wait_ge(pad_ready, layer + 2)
                for g in range(GROUPS):
                    a = (g % 2) * GDIM
                    pool.dma_start(pwbd[a:a + GDIM, g // 2, a:a + GDIM], pool_w[layer, g, :, :]).then_inc(pool_w_loaded, 16)
                pool.dma_start(psc[:, :], pool_scale[layer, :].rearrange("(a p) -> p a", p=P),
                               allow_slow_non_contiguous=True).then_inc(pool_w_loaded, 16)
                if layer == 0:
                    pool.wait_ge(h_ready, TT)
                gains_after = ffn_pre_g[layer, :]
                if layer:
                    pool.wait_ge(h_ready, (2 * layer + 1) * TT)
                gains(gpre[:, :], gains_after, gpre_loaded)
                for t in range(TT):
                    z_drained(pool, layer, t)
                    swapped(zr[:, t, :], z[:, t, QL + KVL:U0], zr_ready)
                    i = P_UQ[t]
                    pool.wait_ge(piece_loaded[i % RING], 16 * (2 * layer + i // RING + 1))
                    w = slot(i % RING)[:, 0:KQ * HG * QK].rearrange("p (kh n) -> p kh n", n=QK)
                    swapped(rw[:, t, :, :, :].rearrange("p k h n -> p (k h) n"), w[:, :, NOPE:QK], rope_w_ready)
                pool.wait_ge(x_updated, (2 * layer + 1) * TT)
                gains(gpost[:, :], ffn_post_g[layer, :], gpost_loaded)
                if layer == 0:
                    pool.wait_ge(h_ready, 2 * TT)
                    gains(gpre[:, :], attn_pre_g[1, :], gpre_loaded)
                    pool.wait_ge(x_updated, 2 * TT)
                    gains(gpost[:, :], attn_post_g[1, :], gpost_loaded)
                else:
                    pool.dma_start(tri[:, :], c_rank[:, 0:P]).then_inc(rank_tables_loaded, 16)
                    pool.dma_start(ones[:, :], c_rank[:, P:]).then_inc(rank_tables_loaded, 16)
                    pool.dma_start(wr[:, :, :], w_router[0, :, :].rearrange("(k p) e -> p k e", p=P)).then_inc(rank_tables_loaded, 16)

        @block.scalar
        def _(act):
            copy, activation = nc.scalar.copy, nc.scalar.activation
            def square(src, width, dst, name, at=0):
                square_no[name] = len(square_no) + 1
                activation(junk[:, at:at + src.free_size()], src, ACT.Square, scale=float(width) ** -0.5,
                           accum_out=dst).then_inc(squares, 1)

            def root_of(layer, n, t):
                root_no[layer, n, t] = len(root_no) + 1
                activation(root[n, t], sq[n, t], ACT.Sqrt, bias=eps[:, :]).then_inc(roots, 1)

            def norm(layer, n, t, src, width):
                square(src, width, sq[n, t], (layer, n, t))
                act.wait_ge(squares, square_no[layer, n, t])
                root_of(layer, n, t)

            def norm_of_banks(layer, name, t, folded):
                for n, dst in enumerate((sq["f", t], sq_half[t])):
                    if name == "o":
                        wait_full(act, layer, f"o{t}{n}")
                    square(jb(layer, f"{name}{t}{n}")[:, :], D, dst, (layer, name, t, n), n * BK)
                act.wait_ge(mean_ready, folded)
                root_no[layer, name, t] = len(root_no) + 1
                activation(root["f", t], sq["f", t], ACT.Sqrt, bias=eps[:, :]).then_inc(roots, 1)

            def attention(layer, loaded):
                for t in range(TT):
                    if layer == 0:
                        act.wait_ge(x_loaded[t], 16)
                        norm(layer, "x", t, x[:, t, :], D)
                    wait_full(act, layer, f"hT{t}0")
                    drain(copy(hT[:, 0:4, t * P:(t + 1) * P], bank_k(layer, f"hT{t}0")), layer, f"hT{t}0")
                for t in range(TT):
                    wait_full(act, layer, f"z{t}0")
                    act.wait_ge(rs_ready, 2 * layer + t + 1)
                    drain(activation(z[:, t, 0:HALF_IN], jb(layer, f"z{t}0")[:, 0:HALF_IN], ACT.Copy, scale=rs["x", t]),
                          layer, f"z{t}0")
                    z_drained(act, layer, t)
                    norm(layer, "kv", t, z[:, t, QL:QL + KVL], KVL)
                    norm(layer, "q", t, z[:, t, 0:QL], QL)
                for t in range(TT):
                    wait_full(act, layer, f"cA{t}")
                    drain(copy(cT[:, 0:KQ, t * P:(t + 1) * P], bank_k(layer, f"cA{t}", KQ)), layer, f"cA{t}")
                wait_full(act, layer, "pooled")
                drain(copy(pl[:, :, :].rearrange("p a n -> p (a n)"), jb(layer, "pooled")[:, :]), layer, "pooled")

                def projections(g):
                    a = HG * g
                    wait_full(act, layer, f"q01_{g}")
                    drain(copy(qT[:, a:a + 2, :].rearrange("p k n -> p (k n)"), jb(layer, f"q01_{g}")[:, :]),
                          layer, f"q01_{g}")
                    wait_full(act, layer, f"k01_{g}")
                    drain(copy(kT[:, a:a + 2, :].rearrange("p k n -> p (k n)"), jb(layer, f"k01_{g}")[:, :]),
                          layer, f"k01_{g}")
                    wait_full(act, layer, f"k2_{g}")
                    drain(copy(kT[:, a + 2, :], jb(layer, f"k2_{g}")[:, 0:SEQ]), layer, f"k2_{g}")

                def exps(g):
                    for i in range(HG * g, HG * (g + 1)):
                        act.wait_ge(max_ready, HEADS * layer + i + 1)
                        for b, (a, w) in enumerate(((0, P), (P, SEQ))):
                            last = activation(pr[:, i, a:a + w], pr[:, i, a:a + w], ACT.Exp,
                                              bias=neg_max[:, 2 * i + b:2 * i + b + 1],
                                              accum_out=p_sum[:, 2 * i + b:2 * i + b + 1])
                        last.then_inc(exp_ready, 1)

                def transposed(g):
                    for i in range(HG * g, HG * (g + 1)):
                        wait_full(act, layer, f"pT{i}")
                        drain(copy(prT[:, i, :], jb(layer, f"pT{i}")[:, 0:KPOS]), layer, f"pT{i}")

                def attended(g):
                    for i in range(HG * g, HG * (g + 1)):
                        wait_full(act, layer, f"a{i}")
                        drain(copy(mixT[:, i, :], jb(layer, f"a{i}")[:, 0:SEQ]), layer, f"a{i}")

                projections(0)
                exps(0)
                projections(1)
                transposed(0)
                exps(1)
                attended(0)
                transposed(1)
                attended(1)
                round_gu(0, 0, loaded)
                round_gu(0, 1)

            def junction(layer, name, t):
                number = 2 * layer + (name == "f")
                norm_of_banks(layer, name, t, number * TT + t + 1)
                act.wait_ge(x_updated, number * TT + t + 1)
                norm((layer, name), "x", t, x[:, t, :], D)

            def round_gu(s, i, loaded=None, used=None):
                if loaded is not None:
                    act.wait_ge(raw_gu_loaded[s], loaded)
                if used is not None:
                    act.wait_ge(gu_full, used)
                copy(half_gu(hi, s, i), half_gu(raw, s, i)).then_inc(gu_hi, 1)

            def round_d(s, loaded, used=None):
                act.wait_ge(raw_d_loaded[s], loaded)
                if used is not None:
                    act.wait_ge(d_used, used)
                copy(hi[:, (4 + s) * SLOT:(5 + s) * SLOT], raw_d(s)).then_inc(d_hi, 1)

            def round_aT(u, s):
                act.wait_ge(tr_full, u + 1)
                act.wait_ge(d_used, u - 1)
                copy(aT_hi[:, s, :, :].rearrange("p k n -> p (k n)"), bank[2 + s][:, 0:FC]).then_inc(aT_part, 1)

            def silu(u, s, scale=1.0):
                act.wait_ge(gu_full, u + 1)
                if not (isinstance(u, int) and u == 0):
                    act.wait_ge(gated, u)
                activation(sg[:, :], bank[s][:, 0:FC], ACT.Silu, scale=scale).then_inc(silu_done, 1)

            def dense():
                for t in range(TT):
                    junction(0, "o", t)
                    if t:
                        silu(0, 0, rs["x", 0])
                    for i in range(2):
                        wait_full(act, 0, f"fT{t}{i}")
                        copy(eT_hi[:, 4 * i:4 * i + 4, t * P:(t + 1) * P], bank_k(0, f"fT{t}{i}")).then_inc(eT_part, 1)

                def unit(c, t, s, first=False, more=True):
                    u = c * 2 + t
                    if t == 0:
                        round_d(s, loaded_d(c, s), None if isinstance(c, int) and c < 2 else (c - 1) * 2)
                    if not (first and t == 0):
                        if first:
                            act.wait_ge(tr_full, 1)
                            copy(aT_hi[:, 0, :, :].rearrange("p k n -> p (k n)"), bank[2][:, 0:FC]).then_inc(aT_part, 1)
                        else:
                            round_aT(u - 1, 1 - t)
                    if more:
                        if t == 0:
                            round_gu(1 - s, 0, loaded_gu(c + 1, 1 - s), None if first else c * 2)
                        else:
                            round_gu(1 - s, 1)
                    if not (first and t == 0):
                        silu(u, t, rs["x", t])

                def loaded_gu(c, s):
                    return ((c - s) // 2 + 1) * 32 if isinstance(c, int) else (c - s) * 16 + 32

                def loaded_d(c, s):
                    return ((c - s) // 2 + 1) * 16 if isinstance(c, int) else (c - s) * 8 + 16

                for t in range(TT):
                    unit(0, t, 0, first=True)
                for t in range(TT):
                    unit(1, t, 1)
                with act.Fori(1, DCH // 2) as j:
                    for s in range(2):
                        for t in range(TT):
                            unit(j * 2 + s, t, s)
                for t in range(TT):
                    unit(DCH - 1, t, 0, more=False)
                round_aT(DU - 1, 1)
                for t in range(TT):
                    act.wait_ge(d_used, DU - 1 + t)
                    junction(0, "f", t)

            def route():
                for t in range(TT):
                    junction(1, "o", t)
                    wait_full(act, 1, f"fT{t}0")
                    drain(copy(hT_route[:, 0:4, t * P:(t + 1) * P], bank_k(1, f"fT{t}0")), 1, f"fT{t}0")
                act.wait_ge(gap_ready, 1)
                activation(e2, gap, ACT.Exp).then_inc(e2_ready, 1)

            PRE = ((DCH + 1) // 2, DCH // 2)

            def gathered_rounded(e):
                for i in range(2):
                    act.wait_ge(gathered, e * 2 + i + 1)
                    copy(eT_hi[:, 4 * i:4 * i + 4, 0:SLOTS], bank[6 + i][:, :].rearrange("p (k n) -> p k n", k=4))\
                        .then_inc(eT_part, 1)

            def sums_out(e):
                act.wait_ge(d_used, e * ECH + (ECH + DU))
                copy(y[:, 0:BK], bank[4][:, :]).then_inc(y_ready, 1)

            def expert(e, first_one, last_one):
                def one(c_pair, s, more=True):
                    start = isinstance(c_pair, int) and c_pair == 0 and s == 0
                    tail = isinstance(c_pair, int) and c_pair == ECH // 2 - 1 and s == 1
                    n = e * ECH + c_pair * 2 + s
                    k = e * (ECH // 2) + c_pair
                    u = n + DU
                    round_d(s, (k + 1 + PRE[s]) * 16, n + (DU - 1))
                    if not start:
                        round_aT(u - 1, 1 - s)
                    if more:
                        round_gu(1 - s, 0, (k + s + 1 + PRE[1 - s]) * 32, u)
                    if start and not first_one:
                        sums_out(e - 1)
                    silu(u, s)
                    if tail:
                        if not last_one:
                            act.wait_ge(gu_full, u + 1)
                            gathered_rounded(e + 1)
                        round_aT(u, s)
                        act.wait_ge(pgT_full, e + 1)
                        copy(pgT[:, :], bank[0][:, 0:SEQ]).then_inc(pgT_ready, 1)
                    if more:
                        round_gu(1 - s, 1)

                for s in range(2):
                    one(0, s)
                with act.Fori(1, ECH // 2 - 1) as j:
                    for s in range(2):
                        one(j, s)
                one(ECH // 2 - 1, 0)
                one(ECH // 2 - 1, 1, more=not last_one)

            def experts(first):
                k = first * (ECH // 2)
                if first:
                    for i in range(2):
                        round_gu(0, i, (k + 1 + PRE[0]) * 32 if i == 0 else None, first * ECH + DU - 1 if i == 0 else None)
                gathered_rounded(first)
                expert(first, True, False)
                with act.Fori(first + 1, first + EXPERTS - 1) as e:
                    expert(e, False, False)
                expert(first + EXPERTS - 1, False, True)
                sums_out(first + EXPERTS - 1)

            act.wait_ge(pad_ready, 1)
            attention(0, 32)
            dense()
            attention(1, (PRE[0] + 1) * 32)
            route()
            experts(0)
            act.wait_ge(routed, 1)
            over = act.value_load(most_int[0:1, 0:1], min_val=0, max_val=SEQ)
            with act.If(over > SLOTS):
                experts(EXPERTS)
            with act.Else():
                act.nop()
            act.wait_ge(f_ready, 1)
            for t in range(TT):
                norm(DEPTH, "f", t, facc[:, t, :], D)

        @block.vector
        def _(dve):
            V_ = nc.vector
            step = [0]

            def link(ins):
                step[0] += 1
                ins.then_inc(dve_step, 1)
                dve.wait_ge(dve_step, step[0])

            def inverse(layer, n, t, name=None):
                dve.wait_ge(roots, root_no[layer, name or n, t])
                return V_.reciprocal(rs[n, t], root[n, t])

            def weigh(t, n):
                dve.wait_ge(gpre_loaded, 16 * n)
                V_.tensor_tensor(h[:, t, :], x[:, t, :], gpre[:, :], ALU.mult).then_inc(h_ready, 1)

            def junction(layer, name, t):
                number = 2 * layer + (name == "f")
                dve.wait_ge(gpost_loaded, 16 * (number + 1))
                for n in range(2):
                    a = n * BK
                    dve.wait_ge(squares, square_no[layer, name, t, n])
                    drain(V_.tensor_tensor(h[:, t, a:a + BK], jb(layer, f"{name}{t}{n}")[:, :], gpost[:, a:a + BK],
                                           ALU.mult), layer, f"{name}{t}{n}")
                V_.tensor_tensor(sq["f", t], sq["f", t], sq_half[t], ALU.add).then_inc(mean_ready, 1)
                link(inverse(layer, "f", t, name))
                wait_drained(dve, layer, f"{name}{t}0", f"{name}{t}1")
                V_.scalar_tensor_tensor(x[:, t, :], h[:, t, :], rs["f", t], x[:, t, :], ALU.mult, ALU.add)\
                    .then_inc(x_updated, 1)
                dve.wait_ge(x_updated, number * TT + t + 1)
                weigh(t, number + 2)

            def attention(layer):
                before = (0, "f") if layer else 0
                for t in range(TT):
                    if layer == 0:
                        dve.wait_ge(x_loaded[t], 16)
                        weigh(t, 1)
                    wait_full(dve, layer, f"hT{t}1")
                    drain(V_.tensor_copy(hT[:, 4:8, t * P:(t + 1) * P], bank_k(layer, f"hT{t}1")), layer, f"hT{t}1")
                    inverse(before, "x", t).then_inc(rs_ready, 1)
                dve.wait_ge(glow_loaded, 32 * (layer + 1))
                for t in range(TT):
                    wait_full(dve, layer, f"z{t}1")
                    dve.wait_ge(rs_ready, 2 * layer + t + 1)
                    drain(V_.tensor_scalar(z[:, t, HALF_IN:IN_COLS], jb(layer, f"z{t}1")[:, 0:HALF_IN], rs["x", t], None,
                                           ALU.mult), layer, f"z{t}1")
                    z_drained(dve, layer, t)
                    V_.tensor_tensor(cn[:, t, 0:QL], z[:, t, 0:QL], gq[:, :], ALU.mult).then_inc(cn_ready, 1)
                    link(inverse(layer, "kv", t))
                    V_.scalar_tensor_tensor(cn[:, t, QL:QL + KVL], z[:, t, QL:QL + KVL], rs["kv", t], gkv[:, :],
                                            ALU.mult, ALU.mult).then_inc(cn_ready, 1)
                    link(inverse(layer, "q", t))
                    link(V_.tensor_scalar(rs["q", t], rs["q", t], SCALE, None, ALU.mult))
                dve.wait_ge(tables_loaded, 80)

                def keys(t):
                    tok = slice(t * P, (t + 1) * P)
                    wait_full(dve, layer, f"cB{t}")
                    b = jb(layer, f"cB{t}")
                    V_.tensor_copy(cT[:, KQ:KQ + KKV, tok], bank_k(layer, f"cB{t}", KKV))
                    V_.tensor_tensor(ta[0:ROPE, tok], b[0:ROPE, KVL:KVL + P], cs[0:ROPE, tok], ALU.mult)
                    drain(V_.tensor_tensor(tb[0:ROPE, tok], b[ROPE:P, KVL:KVL + P], cs[ROPE:P, tok], ALU.mult),
                          layer, f"cB{t}")
                    wait_drained(dve, layer, f"cB{t}")
                    link(V_.tensor_tensor(krT[0:ROPE, tok], ta[0:ROPE, tok], tb[0:ROPE, tok], ALU.add))
                    V_.tensor_copy(krT[ROPE:P, tok], krT[0:ROPE, tok]).then_inc(krT_ready, 1)

                def projections(g):
                    a = HG * g
                    wait_full(dve, layer, f"r01_{g}")
                    csb = cs[:, :].unsqueeze(1).broadcast_to([P, 2, SEQ])
                    drain(V_.tensor_tensor(qrT[:, a:a + 2, :], jb(layer, f"r01_{g}")[:, :].rearrange("p (k n) -> p k n", k=2),
                                           csb, ALU.mult), layer, f"r01_{g}")
                    wait_full(dve, layer, f"qr2_{g}")
                    V_.tensor_copy(qT[:, a + 2, :], jb(layer, f"qr2_{g}")[:, 0:SEQ])
                    drain(V_.tensor_tensor(qrT[:, a + 2, :], jb(layer, f"qr2_{g}")[:, SEQ:2 * SEQ], cs[:, :], ALU.mult),
                          layer, f"qr2_{g}")
                    if g == 0:
                        keys(1)
                    for t in range(TT):
                        wait_full(dve, layer, f"v{t}_{g}")
                        drain(V_.tensor_copy(v[:, t, a * VDIM:(a + HG) * VDIM], jb(layer, f"v{t}_{g}")[:, 0:HG * VDIM]),
                              layer, f"v{t}_{g}")

                def maxima(g):
                    for i in range(HG * g, HG * (g + 1)):
                        wait_full(dve, layer, f"s{i}")
                        for b, (a, w) in enumerate(((0, P), (P, SEQ))):
                            ins = V_.scalar_tensor_tensor(pr[:, i, a:a + w], jb(layer, f"s{i}")[:, a:a + w], rs["q", b],
                                                          mask[:, a:a + w], ALU.mult, ALU.add)
                        drain(ins, layer, f"s{i}")
                        wait_drained(dve, layer, f"s{i}")
                        V_.tensor_reduce(neg_max[:, 2 * i:2 * i + 1], pr[:, i, 0:P], AX.X, ALU.max, negate=True)
                        V_.tensor_reduce(neg_max[:, 2 * i + 1:2 * i + 2], pr[:, i, P:KPOS], AX.X, ALU.max, negate=True)\
                            .then_inc(max_ready, 1)

                def normalized(g):
                    for i in range(HG * g, HG * (g + 1)):
                        dve.wait_ge(exp_ready, HEADS * layer + i + 1)
                        link(V_.reciprocal(p_inv[:, 2 * i:2 * i + 2], p_sum[:, 2 * i:2 * i + 2]))
                        V_.tensor_scalar(pr[:, i, 0:P], pr[:, i, 0:P], p_inv[:, 2 * i:2 * i + 1], None, ALU.mult)
                        V_.tensor_scalar(pr[:, i, P:KPOS], pr[:, i, P:KPOS], p_inv[:, 2 * i + 1:2 * i + 2], None,
                                         ALU.mult).then_inc(probs_ready, 1)

                keys(0)
                projections(0)
                maxima(0)
                projections(1)
                normalized(0)
                maxima(1)
                normalized(1)
                dve.wait_ge(pool_w_loaded, 16 * (GROUPS + 1) * (layer + 1))
                wait_full(dve, layer, "poolout")
                po = jb(layer, "poolout")
                V_.tensor_scalar(mixT[:, HEADS, :], po[:, 0:SEQ], psc[:, 0:1], None, ALU.mult)
                drain(V_.tensor_scalar(mixT[:, HEADS + 1, :], po[:, SEQ:2 * SEQ], psc[:, 1:2], None, ALU.mult),
                      layer, "poolout")
                for i in range(2):
                    low_gu(0, i, layer * 2 * DCH + i + 1)

            def low_gu(s, i, n):
                dve.wait_ge(gu_hi, n)
                a = 2 * s * SLOT + i * SLOT
                V_.tensor_tensor(lo[:, a:a + SLOT], raw[:, a:a + SLOT], f32v(hi[:, a:a + SLOT]), ALU.subtract)\
                    .then_inc(gu_split, 1)

            def low_d(s, n):
                dve.wait_ge(d_hi, n)
                a = (4 + s) * SLOT
                V_.tensor_tensor(lo[:, a:a + SLOT], raw[:, a:a + SLOT], f32v(hi[:, a:a + SLOT]), ALU.subtract)\
                    .then_inc(d_split, 1)

            def low_aT(u, s):
                dve.wait_ge(aT_part, u + 1)
                V_.tensor_tensor(aT_lo[:, s, :, :].rearrange("p k n -> p (k n)"), bank[2 + s][:, 0:FC],
                                 f32v(aT_hi[:, s, :, :]).rearrange("p k n -> p (k n)"), ALU.subtract)\
                    .then_inc(aT_ready, 1)

            def gate_up(u, s, scale=None):
                dve.wait_ge(silu_done, u + 1)
                if scale is None:
                    V_.tensor_tensor(acts[:, s, :], sg[:, :], bank[s][:, FC:2 * FC], ALU.mult).then_inc(gated, 1)
                else:
                    V_.scalar_tensor_tensor(acts[:, s, :], bank[s][:, FC:2 * FC], scale, sg[:, :], ALU.mult, ALU.mult)\
                        .then_inc(gated, 1)

            def dense():
                for t in range(TT):
                    junction(0, "o", t)
                    link(inverse((0, "o"), "x", t))
                    if t:
                        gate_up(0, 0, rs["x", 0])
                    for i in range(2):
                        dve.wait_ge(eT_part, 2 * t + i + 1)
                        drain(V_.tensor_tensor(eT_lo[:, 4 * i:4 * i + 4, t * P:(t + 1) * P], bank_k(0, f"fT{t}{i}"),
                                               f32v(eT_hi[:, 4 * i:4 * i + 4, t * P:(t + 1) * P]), ALU.subtract),
                              0, f"fT{t}{i}")

                def unit(c, t, s, first=False, more=True):
                    u = c * 2 + t
                    if t == 0:
                        low_d(s, c + 1)
                    if not (first and t == 0):
                        low_aT(u - 1, 1 - t)
                    if more:
                        low_gu(1 - s, t, c * 2 + (3 + t))
                    if not (first and t == 0):
                        gate_up(u, t, rs["x", t])

                for t in range(TT):
                    unit(0, t, 0, first=True)
                for t in range(TT):
                    unit(1, t, 1)
                with dve.Fori(1, DCH // 2) as j:
                    for s in range(2):
                        for t in range(TT):
                            unit(j * 2 + s, t, s)
                for t in range(TT):
                    unit(DCH - 1, t, 0, more=False)
                low_aT(DU - 1, 1)
                for t in range(TT):
                    dve.wait_ge(d_used, DU - 1 + t)
                    junction(0, "f", t)

            def over_e(a):
                return a.unsqueeze(2).broadcast_to([P, TT, EXPERTS])

            def route():
                for t in range(TT):
                    junction(1, "o", t)
                    wait_full(dve, 1, f"fT{t}1")
                    drain(V_.tensor_copy(hT_route[:, 4:8, t * P:(t + 1) * P], bank_k(1, f"fT{t}1")), 1, f"fT{t}1")
                    link(inverse((1, "o"), "x", t))
                    V_.tensor_scalar(h[:, t, :], h[:, t, :], rs["x", t], None, ALU.mult)

                revb = rev.unsqueeze(1).broadcast_to([P, TT, EXPERTS])
                wait_full(dve, 1, "logits")
                for t in range(TT):
                    ins = V_.tensor_scalar(lg[:, t, :], jb(1, "logits")[:, t * EXPERTS:(t + 1) * EXPERTS], rs["x", t], None,
                                           ALU.mult)
                drain(ins, 1, "logits")
                wait_drained(dve, 1, "logits")

                def top(src, m, oh):
                    link(V_.tensor_reduce(m, src, AX.X, ALU.max))
                    link(V_.tensor_tensor(eq, src, over_e(m), ALU.is_equal))
                    link(V_.tensor_tensor(key, eq, revb, ALU.mult))
                    link(V_.tensor_reduce(kk, key, AX.X, ALU.max))
                    link(V_.tensor_tensor(oh, key, over_e(kk), ALU.is_equal))

                top(lg, m1, oh1)
                link(V_.scalar_tensor_tensor(lg2, oh1, NEG, lg, ALU.mult, ALU.add))
                top(lg2, m2, oh2)
                V_.tensor_tensor(chosen, oh1, oh2, ALU.add).then_inc(chosen_ready, 1)
                V_.tensor_tensor(gap, m2, m1, ALU.subtract).then_inc(gap_ready, 1)
                wait_full(dve, 1, "ranks")
                rk = jb(1, "ranks")
                V_.tensor_copy(rank, rk[:, 0:TT * EXPERTS].rearrange("p (t e) -> p t e", t=TT))
                ins = V_.tensor_reduce(most, rk[:, TT * EXPERTS:(TT + 1) * EXPERTS], AX.X, ALU.max)
                drain(ins, 1, "ranks")
                wait_drained(dve, 1, "ranks")

            def gates():
                dve.wait_ge(e2_ready, 1)
                link(V_.tensor_scalar(g2, e2, 1.0, None, ALU.add))
                link(V_.reciprocal(g1, g2))
                link(V_.tensor_tensor(g2, e2, g1, ALU.mult))
                V_.tensor_tensor(gate, oh1, over_e(g1), ALU.mult)
                link(V_.tensor_tensor(eq, oh2, over_e(g2), ALU.mult))
                link(V_.tensor_tensor(gate, gate, eq, ALU.add))
                V_.tensor_copy(most_int[:, :], most).then_inc(routed, 1)

            def picks(e, col_e):
                for t in range(TT):
                    last = V_.tensor_scalar(pick[:, t, :], iota[:, :], rank[:, t, ts(col_e, 1)], chosen[:, t, ts(col_e, 1)],
                                            ALU.is_equal, ALU.mult)
                last.then_inc(pick_ready, 1)

            def picks_gated(e, col_e):
                for t in range(TT):
                    last = V_.tensor_scalar(pick_gated[:, t, :], iota[:, :], rank[:, t, ts(col_e, 1)], gate[:, t, ts(col_e, 1)],
                                            ALU.is_equal, ALU.mult)
                last.then_inc(pick_gated_ready, 1)

            def gathered_low(e):
                for i in range(2):
                    dve.wait_ge(eT_part, e * 2 + (i + 5))
                    V_.tensor_tensor(eT_lo[:, 4 * i:4 * i + 4, 0:SLOTS], bank[6 + i][:, :].rearrange("p (k n) -> p k n", k=4),
                                     f32v(eT_hi[:, 4 * i:4 * i + 4, 0:SLOTS]), ALU.subtract).then_inc(eT_ready, 1)

            def sums_out(e):
                dve.wait_ge(d_used, e * ECH + (ECH + DU))
                V_.tensor_copy(y[:, BK:2 * BK], bank[5][:, :]).then_inc(y_ready, 1)

            def add(e, t):
                for n in range(2):
                    dve.wait_ge(spread, e * 4 + (2 * t + n + 1))
                    V_.tensor_tensor(facc[:, t, n * BK:(n + 1) * BK], facc[:, t, n * BK:(n + 1) * BK],
                                     bank[6 + n][:, :], ALU.add).then_inc(added, 1)

            def expert(e, first, first_one, last_one):
                def one(c_pair, s, more=True):
                    start = isinstance(c_pair, int) and c_pair == 0 and s == 0
                    tail = isinstance(c_pair, int) and c_pair == ECH // 2 - 1 and s == 1
                    n = e * ECH + c_pair * 2 + s
                    u = n + DU
                    low_d(s, n + (DCH + 1))
                    if not start:
                        low_aT(u - 1, 1 - s)
                    if more:
                        low_gu(1 - s, 0, (n + (DCH + 1)) * 2 + 1)
                    if start and not first_one:
                        sums_out(e - 1)
                    gate_up(u, s)
                    if tail:
                        if not last_one:
                            gathered_low(e + 1)
                        low_aT(u, s)
                    if more:
                        low_gu(1 - s, 1, (n + (DCH + 1)) * 2 + 2)

                one(0, 0)
                if not last_one:
                    picks(e + 1, e - (first - 1))
                if not (first_one and first == 0):
                    dve.wait_ge(pgT_full, e)
                picks_gated(e, e - first)
                if not first_one:
                    add(e - 1, 0)
                one(0, 1)
                if not first_one:
                    add(e - 1, 1)
                with dve.Fori(1, ECH // 2 - 1) as j:
                    for s in range(2):
                        one(j, s)
                one(ECH // 2 - 1, 0)
                one(ECH // 2 - 1, 1, more=not last_one)

            def experts(first):
                picks(first, 0)
                if first == 0:
                    gates()
                else:
                    for i in range(2):
                        low_gu(0, i, 2 * (first * ECH + DCH) + i + 1)
                gathered_low(first)
                if first == 0:
                    link(V_.memset(facc[:, :, :], 0.0))
                expert(first, first, True, False)
                with dve.Fori(first + 1, first + EXPERTS - 1) as e:
                    expert(e, first, False, False)
                last = first + EXPERTS - 1
                expert(last, first, False, True)
                sums_out(last)
                dve.wait_ge(added, last * 4)
                for t in range(TT):
                    add(last, t)
                dve.wait_ge(added, last * 4 + 4)

            attention(0)
            dense()
            attention(1)
            route()
            experts(0)
            dve.wait_ge(routed, 1)
            over = dve.value_load(most_int[0:1, 0:1], min_val=0, max_val=SEQ)
            with dve.If(over > SLOTS):
                V_.tensor_scalar(rank, rank, -float(SLOTS), None, ALU.add).then_inc(routed, 1)
                dve.wait_ge(routed, 2)
                experts(EXPERTS)
            with dve.Else():
                dve.nop()
            dve.sem_inc(f_ready, 1)
            dve.wait_ge(gpost_loaded, 16 * 4)
            for t in range(TT):
                link(V_.tensor_tensor(h[:, t, :], facc[:, t, :], gpost[:, :], ALU.mult))
            for t in range(TT):
                link(inverse(DEPTH, "f", t))
                V_.scalar_tensor_tensor(x[:, t, :], h[:, t, :], rs["f", t], x[:, t, :], ALU.mult, ALU.add)\
                    .then_inc(x_updated, 1)

        @block.tensor
        def _(pe):
            mm = nc.tensor.matmul

            def transposes(layer, name, t, n_h):
                pe.wait_ge(ident_loaded, 16)
                pe.wait_ge(h_ready, n_h + t + 1)
                for i in range(2):
                    wait_free(layer, f"{name}{t}{i}")
                    for k in range(4):
                        last = nc.tensor.transpose(jb(layer, f"{name}{t}{i}")[:, k * P:(k + 1) * P],
                                                   h[:, t, (4 * i + k) * P:(4 * i + k + 1) * P], ident[:, :])
                    fill(last, layer, f"{name}{t}{i}")

            def attention(layer):
                def loaded(i):
                    pe.wait_ge(piece_loaded[i % RING], 16 * (2 * layer + i // RING + 1))

                def drained(*names):
                    wait_drained(pe, layer, *names)

                def latents(t, part):
                    pe.wait_ge(cn_ready, 4 * layer + 2 * t + (1 if part == "A" else 2))
                    name = f"c{part}{t}"
                    wait_free(layer, name)
                    blocks = [cn[:, t, k * P:(k + 1) * P] for k in (range(KQ) if part == "A" else range(KQ, KQ + KKV))]
                    if part == "B":
                        pe.wait_ge(zr_ready, TT * layer + t + 1)
                        blocks.append(zr[:, t, :])
                    for j, b in enumerate(blocks):
                        last = nc.tensor.transpose(jb(layer, name)[:, j * P:(j + 1) * P], b, ident[:, :])
                        if part == "A" and t == 1 and j == 0:
                            last.then_inc(piece_used, 1)
                    fill(last, layer, name)

                transposes(layer, "hT", 0, 2 * layer * TT)
                for t in range(TT):
                    zb = [f"z{t}{n}" for n in range(2)]
                    for n in range(2):
                        wait_free(layer, zb[n])
                    for j in range(4):
                        if j == 2:
                            if t == 0:
                                transposes(layer, "hT", 1, 2 * layer * TT)
                            else:
                                latents(0, "A")
                        if j == 3 and t == 1:
                            latents(0, "B")
                        loaded(P_IN + j)
                        drained(f"hT{t}{j // 2}")
                        w = slot((P_IN + j) % RING)[:, 0:2 * IN_COLS].rearrange("p (k n) -> p k n", k=2)
                        for k in range(2):
                            for n in range(2):
                                last = mm(jb(layer, zb[n])[:, 0:HALF_IN], hT[:, 2 * j + k, t * P:(t + 1) * P],
                                          w[:, k, n * HALF_IN:(n + 1) * HALF_IN],
                                          start=(j == 0 and k == 0), stop=(j == 3 and k == 1))
                                if j == 3 and k == 1:
                                    fill(last, layer, zb[n])
                        if j < 3 and t == 1:
                            last.then_inc(piece_used, 1)
                latents(1, "A")

                pe.wait_ge(tables_loaded, 80)
                drained("z01", "z11")
                wait_free(layer, "pooled")
                for g in range(GROUPS):
                    a, c = (g % 2) * GDIM, (g // 2) * SEQ
                    o = jb(layer, "pooled")
                    u = [z[:, t, U0 + g * GDIM:U0 + (g + 1) * GDIM] for t in range(TT)]
                    mm(o[a:a + GDIM, c:c + P], u[0], bands[:, g, 0:P], start=True, stop=True)
                    mm(o[a:a + GDIM, c + P:c + SEQ], u[0], bands[:, g, P:SEQ], start=True, stop=False)
                    last = mm(o[a:a + GDIM, c + P:c + SEQ], u[1], bands[:, g, SEQ:KPOS], start=False, stop=True)
                fill(last, layer, "pooled")

                def over_k(dst, ks, lhs, rhs, name=None, piece_before=False):
                    for k in range(ks):
                        last = mm(dst, lhs(k), rhs(k), start=(k == 0), stop=(k == ks - 1))
                        if piece_before and k == 0:
                            last.then_inc(piece_used, 1)
                    if name:
                        fill(last, layer, name)

                def projections(g):
                    loaded(P_UQ[g])
                    wq = slot(P_UQ[g] % RING)[:, 0:KQ * HG * QK].rearrange("p (k h n) -> p k h n", k=KQ, h=HG)
                    wkv = slot(P_UKV[g] % RING)[:, 0:KKV * HG * KV].rearrange("p (k h n) -> p k h n", k=KKV, h=HG)
                    if g == 0:
                        drained("cA0", "cA1")

                    def q(dst, i, name=None):
                        over_k(dst, KQ, lambda k: wq[:, k, i, 0:NOPE], lambda k: cT[:, k, :], name)

                    def key(dst, i, name=None, piece_before=False):
                        over_k(dst, KKV, lambda k: wkv[:, k, i, 0:NOPE], lambda k: cT[:, KQ + k, :], name, piece_before)

                    def rope(dst, i, name=None):
                        over_k(dst, KQ, lambda k: rw[:, g, k, i, :], lambda k: cT[:, k, :], name)

                    wait_free(layer, f"q01_{g}")
                    q(jb(layer, f"q01_{g}")[:, 0:SEQ], 0)
                    q(jb(layer, f"q01_{g}")[:, SEQ:2 * SEQ], 1, f"q01_{g}")
                    pe.wait_ge(rope_w_ready, 2 * layer + g + 1)
                    wait_free(layer, f"r01_{g}")
                    rope(jb(layer, f"r01_{g}")[:, 0:SEQ], 0)
                    rope(jb(layer, f"r01_{g}")[:, SEQ:2 * SEQ], 1, f"r01_{g}")
                    wait_free(layer, f"qr2_{g}")
                    q(jb(layer, f"qr2_{g}")[:, 0:SEQ], 2)
                    rope(jb(layer, f"qr2_{g}")[:, SEQ:2 * SEQ], 2, f"qr2_{g}")
                    loaded(P_UKV[g])
                    if g == 0:
                        latents(1, "B")
                        drained("cB0", "cB1")
                    wait_free(layer, f"k01_{g}")
                    key(jb(layer, f"k01_{g}")[:, 0:SEQ], 0, piece_before=True)
                    key(jb(layer, f"k01_{g}")[:, SEQ:2 * SEQ], 1, f"k01_{g}")
                    wait_free(layer, f"k2_{g}")
                    key(jb(layer, f"k2_{g}")[:, 0:SEQ], 2, f"k2_{g}")
                    for t in range(TT):
                        wait_free(layer, f"v{t}_{g}")
                        over_k(jb(layer, f"v{t}_{g}")[:, 0:HG * VDIM].rearrange("p (h n) -> p h n", h=HG), KKV,
                               lambda k: cT[:, KQ + k, t * P:(t + 1) * P], lambda k: wkv[:, k, :, NOPE:KV], f"v{t}_{g}")

                def scores(g):
                    drained(f"q01_{g}", f"k01_{g}", f"k2_{g}", f"r01_{g}", f"qr2_{g}")
                    pe.wait_ge(krT_ready, TT * (layer + 1))
                    for i in range(HG * g, HG * (g + 1)):
                        wait_free(layer, f"s{i}")
                        o = jb(layer, f"s{i}")
                        for b, (a, w) in enumerate(((0, P), (P, SEQ))):
                            ins = mm(o[:, a:a + w], qT[:, i, b * P:(b + 1) * P], kT[:, i, 0:w], start=True, stop=False)
                            if i == 0 and b == 0:
                                ins.then_inc(piece_used, 1)
                            last = mm(o[:, a:a + w], qrT[:, i, b * P:(b + 1) * P], krT[:, 0:w], start=False, stop=True)
                        fill(last, layer, f"s{i}")

                def transposed(g):
                    for i in range(HG * g, HG * (g + 1)):
                        wait_free(layer, f"pT{i}")
                        pe.wait_ge(probs_ready, HEADS * layer + i + 1)
                        for j in range(3):
                            last = nc.tensor.transpose(jb(layer, f"pT{i}")[:, j * P:(j + 1) * P],
                                                       pr[:, i, j * P:(j + 1) * P], ident[:, :])
                            if i == 0 and j == 0:
                                last.then_inc(piece_used, 1)
                        fill(last, layer, f"pT{i}")

                def attended(g):
                    drained(f"v0_{g}", f"v1_{g}")
                    for i in range(HG * g, HG * (g + 1)):
                        drained(f"pT{i}")
                        wait_free(layer, f"a{i}")
                        o = jb(layer, f"a{i}")
                        vi = [v[:, t, i * VDIM:(i + 1) * VDIM] for t in range(TT)]
                        mm(o[:, 0:P], vi[0], prT[:, i, 0:P], start=True, stop=True)
                        mm(o[:, P:SEQ], vi[0], prT[:, i, P:2 * P], start=True, stop=False)
                        last = mm(o[:, P:SEQ], vi[1], prT[:, i, 2 * P:3 * P], start=False, stop=True)
                        fill(last, layer, f"a{i}")

                projections(0)
                scores(0)
                projections(1)
                transposed(0)
                scores(1)
                attended(0)
                drained("pooled")
                pe.wait_ge(pool_w_loaded, 16 * (GROUPS + 1) * (layer + 1))
                wait_free(layer, "poolout")
                for a in range(2):
                    last = mm(jb(layer, "poolout")[:, a * SEQ:(a + 1) * SEQ], pwbd[:, a, :], pl[:, a, :],
                              start=True, stop=True)
                fill(last, layer, "poolout")
                transposed(1)
                attended(1)
                for t in range(TT):
                    for n in range(2):
                        wait_free(layer, f"o{t}{n}")
                    for i, j in enumerate(WOUT_ORDER):
                        if t == 0:
                            loaded(P_OUT + i)
                            if j == 3:
                                drained("poolout")
                            else:
                                drained(f"a{2 * j}", f"a{2 * j + 1}")
                        elif i == 3:
                            transposes(layer, "fT", 0, (2 * layer + 1) * TT)
                        w = slot((P_OUT + i) % RING).rearrange("p (k n) -> p k n", k=2)
                        for k in range(2):
                            for n in range(2):
                                last = mm(jb(layer, f"o{t}{n}")[:, :], mixT[:, 2 * j + k, t * P:(t + 1) * P],
                                          w[:, k, n * BK:(n + 1) * BK], start=(i == 0 and k == 0), stop=(i == 3 and k == 1))
                                if i == 3 and k == 1:
                                    fill(last, layer, f"o{t}{n}")
                        if t == 1 and i < 3:
                            last.then_inc(piece_used, 1)

            def split_mm(dst, a_hi, a_lo, b_hi, b_lo, start, stop):
                mm(dst, a_hi, b_hi, start=start, stop=False)
                mm(dst, a_hi, b_lo, start=False, stop=False)
                return mm(dst, a_lo, b_hi, start=False, stop=stop)

            def gate_up(s, b, tok, ks):
                for k in ks:
                    last = split_mm(bank[b][:, :], eT_hi[:, k, tok], eT_lo[:, k, tok],
                                    part_gu(hi, s, k), part_gu(lo, s, k), k == 0, k == KD - 1)
                return last

            def turn(s):
                for k in range(KF):
                    last = nc.tensor.transpose(bank[2 + s][:, k * P:(k + 1) * P], acts[:, s, k * P:(k + 1) * P], ident[:, :])
                last.then_inc(tr_full, 1)

            def down(s_w, s_a, b0, start, stop):
                for n in range(2):
                    for k in range(KF):
                        last = split_mm(bank[b0 + n][:, :], aT_hi[:, s_a, k, :], aT_lo[:, s_a, k, :],
                                        part_d(hi, s_w, k, n), part_d(lo, s_w, k, n),
                                        start and k == 0, stop and k == KF - 1)
                last.then_inc(d_used, 1)

            FIRST_K, SECOND_K = range(0, KD // 2), range(KD // 2, KD)

            def dense():
                for b in range(4):
                    pe.wait_ge(bank_free[b], USES_BEFORE_UNITS[0][b] - (b in (2, 3)))

                def unit(c, t, s, first=False, start=False, stop=False):
                    u = c * 2 + t
                    pe.wait_ge(gu_split, c * 2 + 1)
                    if not first:
                        pe.wait_ge(gated, u - 1)
                    tok = slice(t * P, (t + 1) * P)
                    gate_up(s, t, tok, FIRST_K)
                    if not (first and t == 0):
                        pe.wait_ge(gated, u)
                        if not (isinstance(u, int) and u < 3):
                            pe.wait_ge(aT_ready, u - 2)
                        turn(1 - t)
                    pe.wait_ge(gu_split, c * 2 + 2)
                    last = gate_up(s, t, tok, SECOND_K)
                    last.then_inc(gu_full, 1)
                    if not (first and t == 0):
                        pe.wait_ge(aT_ready, u)
                        if t == 0:
                            down(1 - s, 1, 6, start, stop)
                        else:
                            pe.wait_ge(d_split, c + 1)
                            down(s, 0, 4, start, stop)

                unit(0, 0, 0, first=True)
                transposes(0, "fT", 1, TT)
                wait_drained(pe, 0, "fT10", "fT11")
                for t in range(TT):
                    for n in range(2):
                        wait_free(0, f"f{t}{n}")
                unit(0, 1, 0, first=True, start=True)
                unit(1, 0, 1, start=True)
                unit(1, 1, 1)
                with pe.Fori(1, DCH // 2) as j:
                    for s in range(2):
                        for t in range(TT):
                            unit(j * 2 + s, t, s)
                unit(DCH - 1, 0, 0)
                unit(DCH - 1, 1, 0, stop=True)
                pe.wait_ge(gated, DU)
                turn(1)
                pe.wait_ge(aT_ready, DU)
                down(0, 1, 6, False, True)

            def route():
                transposes(1, "fT", 1, 3 * TT)
                wait_drained(pe, 1, *(f"fT{t}{i}" for t in range(TT) for i in range(2)))
                pe.wait_ge(rank_tables_loaded, 48)
                wait_free(1, "logits")
                for t in range(TT):
                    for k in range(KD):
                        last = mm(jb(1, "logits")[:, t * EXPERTS:(t + 1) * EXPERTS], hT_route[:, k, t * P:(t + 1) * P],
                                  wr[:, k, :], start=(k == 0), stop=(k == KD - 1))
                fill(last, 1, "logits")
                pe.wait_ge(chosen_ready, 1)
                wait_free(1, "ranks")
                o = jb(1, "ranks")
                mm(o[:, 0:EXPERTS], tri[:, :], chosen[:, 0, :], start=True, stop=True)
                mm(o[:, EXPERTS:2 * EXPERTS], ones[:, :], chosen[:, 0, :], start=True, stop=False)
                mm(o[:, EXPERTS:2 * EXPERTS], tri[:, :], chosen[:, 1, :], start=False, stop=True)
                mm(o[:, 2 * EXPERTS:3 * EXPERTS], ones[:, :], chosen[:, 0, :], start=True, stop=False)
                last = mm(o[:, 2 * EXPERTS:3 * EXPERTS], ones[:, :], chosen[:, 1, :], start=False, stop=True)
                fill(last, 1, "ranks")
                for b in range(8):
                    pe.wait_ge(bank_free[b], USES_BEFORE_UNITS[1][b])

            def gather(e, halves=range(2)):
                pe.wait_ge(pick_ready, e + 1)
                for i in halves:
                    for k in range(4):
                        for t in range(TT):
                            last = mm(bank[6 + i][:, k * P:(k + 1) * P], h[:, t, (4 * i + k) * P:(4 * i + k + 1) * P],
                                      pick[:, t, :], start=(t == 0), stop=(t == TT - 1))
                    last.then_inc(gathered, 1)

            tok = slice(0, SLOTS)

            def scatter(e, t):
                if t == 0:
                    pe.wait_ge(y_ready, e * 2 + 2)
                else:
                    pe.wait_ge(added, e * 4 + 2)
                for n in range(2):
                    mm(bank[6 + n][:, :], pgT[:, t * P:(t + 1) * P], y[:, n * BK:(n + 1) * BK],
                       start=True, stop=True).then_inc(spread, 1)

            def expert(e, first_one, last_one):
                def one(c_pair, s):
                    start = isinstance(c_pair, int) and c_pair == 0 and s == 0
                    n = e * ECH + c_pair * 2 + s
                    u = n + DU
                    q = n + DCH
                    pe.wait_ge(gu_split, q * 2 + 1)
                    pe.wait_ge(gated, u - 1)
                    gate_up(s, s, tok, FIRST_K)
                    if not start:
                        pe.wait_ge(gated, u)
                        pe.wait_ge(aT_ready, u - 2)
                        turn(1 - s)
                    pe.wait_ge(gu_split, q * 2 + 2)
                    gate_up(s, s, tok, SECOND_K).then_inc(gu_full, 1)
                    if not start:
                        pe.wait_ge(aT_ready, u)
                        pe.wait_ge(d_split, q)
                        down(1 - s, 1 - s, 4, isinstance(c_pair, int) and c_pair == 0, False)

                pe.wait_ge(eT_ready, e * 2 + 2)
                if not first_one:
                    pe.wait_ge(pgT_ready, e)
                for s in range(2):
                    one(0, s)
                    if not first_one:
                        scatter(e - 1, s)
                cuts = (1, 3, 5, ECH // 2 - 1)
                for i in range(3):
                    if i and not last_one:
                        if i == 1 and not first_one:
                            pe.wait_ge(added, e * 4)
                        gather(e + 1, (i - 1,))
                    with pe.Fori(cuts[i], cuts[i + 1]) as j:
                        for s in range(2):
                            one(j, s)
                for s in range(2):
                    one(ECH // 2 - 1, s)
                u = e * ECH + (ECH - 1 + DU)
                pe.wait_ge(gated, u + 1)
                turn(1)
                pe.wait_ge(pick_gated_ready, e + 1)
                for t in range(TT):
                    last = nc.tensor.transpose(bank[0][:, t * P:(t + 1) * P], pick_gated[:, t, :], ident[:, :])
                last.then_inc(pgT_full, 1)
                pe.wait_ge(aT_ready, u + 1)
                pe.wait_ge(d_split, u + (DCH - DU + 1))
                down(1, 1, 4, False, True)

            def experts(first):
                gather(first)
                expert(first, True, False)
                with pe.Fori(first + 1, first + EXPERTS - 1) as e:
                    expert(e, False, False)
                last = first + EXPERTS - 1
                expert(last, False, True)
                pe.wait_ge(pgT_ready, last + 1)
                for t in range(TT):
                    scatter(last, t)
                pe.wait_ge(added, last * 4 + 4)

            attention(0)
            dense()
            attention(1)
            route()
            experts(0)
            pe.wait_ge(routed, 1)
            over = pe.value_load(most_int[0:1, 0:1], min_val=0, max_val=SEQ)
            with pe.If(over > SLOTS):
                experts(EXPERTS)
            with pe.Else():
                pe.nop()


_INS = ["x", "attn_pre_g", "attn_post_g", "ffn_pre_g", "ffn_post_g", "w_in", "q_norm_g", "kv_norm_g", "w_uq", "w_ukv",
        "pool_w", "pool_scale", "w_out", "w_gate_d", "w_up_d", "w_down_d", "w_router", "w_gate_e", "w_up_e", "w_down_e"]


def kernel(**inputs):
    import concourse.bacc as bacc
    from concourse.bass_utils import run_bass_kernel_spmd

    nc = bacc.Bacc("TRN2", target_bir_lowering=False, num_devices=1)
    arrays, args = {}, []
    given = {n: np.ascontiguousarray(inputs[n]) for n in _INS} | tables()
    for name, a in given.items():
        arrays[f"in_{name}"] = a
        args.append(nc.dram_tensor(f"in_{name}", a.shape, mybir.dt.from_np(a.dtype), kind="ExternalInput").ap())
    out = nc.dram_tensor("out_0", (1, SEQ, D), mybir.dt.float32, kind="ExternalOutput").ap()
    encoder_kernel(nc, *args, out)
    r = run_bass_kernel_spmd(nc, [arrays], core_ids=[0])
    return r.results[0]["out_0"]
```

```python
import concourse.bass as bass
from concourse import mybir
import numpy as np

P = 128
D = 1024
SEQ = 256
TT = SEQ // P
KD = D // P
DEPTH = 2
CHUNK = 64
EPS = 1e-6
HEADS = 6
NOPE, ROPE, VDIM = 128, 64, 128
QL, KVL = 384, 256
KQ, KKV = QL // P, KVL // P
QK = NOPE + ROPE
KV = NOPE + VDIM
GROUPS, GDIM = 4, 64
WINDOWS = (2, 4, 8, 16)
POOLW = GROUPS * GDIM
IN_COLS = QL + KVL + ROPE + POOLW
HALF_IN = IN_COLS // 2
U0 = QL + KVL + ROPE
THETA = 10000.0
D_FF, D_FFE, EXPERTS = 2816, 3584, 8
FC = 256
KF = FC // P
DCH = D_FF // FC
ECH = D_FFE // FC
SLOTS = P
HG = 3
KPOS = 3 * P
NEG = -3.0e38
SCALE = float(QK) ** -0.5
BK = 512
ASKED = (1, 3, 4, ECH // 2 - 1)
HELD = (1, 4, 5, ECH // 2 - 1)

SLOT = 2048
RING = 6
WOUT_ORDER = (3, 0, 1, 2)
PIECES = 12
P_IN, P_UQ, P_UKV, P_OUT = 0, (4, 6), (5, 7), 8
PIECE_WORDS = (2 * IN_COLS,) * 4 + (KQ * HG * QK, KKV * HG * KV) * 2 + (2 * D,) * 4


def attention_jobs():
    names = ["hT00", "hT01", "z00", "z01", "hT10", "hT11", "z10", "z11", "cA0", "cB0", "cA1", "pooled"]

    def projections(g, between=()):
        rope, rest = [f"r01_{g}", f"qr2_{g}"], [f"k01_{g}", f"k2_{g}", f"v0_{g}", f"v1_{g}"]
        return [f"q01_{g}", *between, *(rest + rope if g else rope + rest)]

    def heads(what, g):
        return [f"{what}{HG * g + i}" for i in range(HG)]

    names += projections(0, ("cB1",)) + heads("s", 0) + projections(1)
    names += heads("pT", 0) + heads("s", 1) + heads("a", 0) + ["poolout"] + heads("pT", 1) + heads("a", 1)
    return names


def bank_plan():
    plan, full, used, after_attention = {}, [0] * 8, [0] * 8, []

    def give(name, bank, signalled=True):
        plan[name] = (bank, full[bank], used[bank])
        full[bank] += signalled
        used[bank] += 1

    for layer in range(DEPTH):
        for i, n in enumerate(attention_jobs()):
            give((layer, n), i % 8)
        for t, first in enumerate((6, 4)):
            for n in range(2):
                give((layer, f"o{t}{n}"), first + n)
        for t in range(TT):
            for i in range(2):
                give((layer, f"fT{t}{i}"), 2 + i)
        if layer:
            give((layer, "logits"), 0)
            give((layer, "ranks"), 1)
        after_attention.append(list(used))
        if layer == 0:
            for i in range(4):
                give((layer, f"f{i // 2}{i % 2}"), 4 + i, signalled=False)
    return plan, after_attention


JOBS, USES_BEFORE_UNITS = bank_plan()

RAW = 0
HI = RAW + RING * SLOT
LO = HI + RING * SLOT
X = LO + RING * SLOT
H = X + TT * D
GPRE = H + TT * D
GPOST = GPRE + D
ET = GPOST + D
FACC = ET + 2 * KD * SEQ
Y = FACC + TT * D
SG = Y + D
ACTS = SG + FC
AT = ACTS + 2 * FC
PICK = AT + 4 * FC
PICKG = PICK + TT * SLOTS
PGT = PICKG + TT * SLOTS
IDENT = PGT + SEQ
IOTA = IDENT + P
SMALL = IOTA + P
SMALL_N = 196
WORDS = SMALL + SMALL_N
QT = HI
QRT = QT + HEADS * SEQ
PWBD = QRT + HEADS * SEQ
ZR = PWBD + 2 * P
KRT = ZR + TT * 2 * ROPE
assert KRT + SEQ <= HI + 2 * SLOT
CT_HI = HI + 2 * SLOT
CT_LO = CT_HI + (KQ + KKV) * SEQ
RW_HI = CT_LO + (KQ + KKV) * SEQ
RW_LO = RW_HI + KQ * HG * 2 * ROPE
CN = RW_LO + KQ * HG * 2 * ROPE
assert CN + TT * (QL + KVL) <= HI + 5 * SLOT
KT = LO
PR = KT + HEADS * SEQ
assert PR + HEADS * KPOS <= LO + 2 * SLOT
Z = LO + 2 * SLOT
assert Z + TT * IN_COLS <= LO + 3 * SLOT
V = LO + 3 * SLOT
PTT = V + TT * HEADS * VDIM
assert PTT + HEADS * KPOS <= LO + 5 * SLOT
TURNED_HI, TURNED_LO = HI + 5 * SLOT, LO + 5 * SLOT
PIECE_HI = (ET, ET + SLOT, LO, LO + SLOT, ET, ET + SLOT, ET, ET + SLOT,
            LO + 2 * SLOT, HI + 2 * SLOT, HI + 3 * SLOT, HI + 4 * SLOT)
PL = ACTS
TA = AT
TB = TA + SEQ
BANDS = FACC
CS = BANDS + GROUPS * KPOS
PSC = CS + SEQ
assert PSC + 2 <= Y
MASK = Y
GQ = MASK + KPOS
GKV = GQ + QL
assert GKV + KVL <= SG
TRI = PGT
ONES = TRI + P
WR = SG
ROUTED_HT = ET


def tables():
    f = np.float32
    ident = np.eye(P, dtype=f)
    iota = np.broadcast_to(np.arange(P, dtype=f), (P, P))
    rev = np.broadcast_to(EXPERTS - np.arange(EXPERTS, dtype=f), (P, EXPERTS))
    inv = (f(1.0) / (f(THETA) ** (np.arange(0, ROPE, 2, dtype=f) / f(ROPE)))).astype(f)
    ang = (np.arange(SEQ, dtype=f)[:, None] * inv[None, :]).astype(f)
    cos, sin = np.cos(ang).T, np.sin(ang).T
    cs = np.concatenate([cos, cos, -sin, sin], axis=0).astype(f)
    s = np.arange(SEQ)[:, None]
    t = np.arange(SEQ)[None, :]
    bands = np.zeros((P, GROUPS, KPOS), f)
    for g, w in enumerate(WINDOWS):
        b = ((s <= t) & (s > t - w)) / np.minimum(t + 1, w) - (s == t)
        bands[:, g, 0:SEQ] = b[0:P]
        bands[:, g, SEQ:KPOS] = b[P:, P:]
    mask = np.zeros((P, KPOS), f)
    mask[0:CHUNK, CHUNK:P] = NEG
    mask[0:CHUNK, KPOS - CHUNK:] = NEG
    tri = np.triu(np.ones((P, P), f), 1)
    ones = np.ones((P, P), f)
    return {
        "c_ident": ident, "c_iota": np.ascontiguousarray(np.concatenate([iota, rev], axis=1)),
        "c_bands": np.ascontiguousarray(np.concatenate([bands.reshape(P, -1), cs], axis=1)),
        "c_mask": mask, "c_rank": np.ascontiguousarray(np.concatenate([tri, ones], axis=1)),
    }


def encoder_kernel(nc, x_in, attn_pre_g, attn_post_g, ffn_pre_g, ffn_post_g, w_in, q_norm_g, kv_norm_g,
                   w_uq, w_ukv, pool_w, pool_scale, w_out, w_gate_d, w_up_d, w_down_d, w_router,
                   w_gate_e, w_up_e, w_down_e, c_ident, c_iota, c_bands, c_mask, c_rank, out):
    f32, f32r, i32 = mybir.dt.float32, mybir.dt.float32r, mybir.dt.int32
    ALU, ACT, AX = mybir.AluOpType, mybir.ActivationFunctionType, mybir.AxisListType
    ts = bass.ds

    base = (nc.sbuf_base + 63) // 64 * 64
    nc.alloc_sbuf_tensor("arena", [P, WORDS + (base - nc.sbuf_base) // 4], f32)

    def at(name, word, shape, dt=f32):
        return nc.alloc_sbuf_tensor_at(name, shape, dt, offset=base + 4 * word)

    raw = at("raw", RAW, [P, RING * SLOT])
    hi = at("hi", HI, [P, RING * SLOT], f32r)
    lo = at("lo", LO, [P, RING * SLOT], f32r)
    x = at("x", X, [P, TT, D])
    h = at("h", H, [P, TT, D])
    gpre = at("gpre", GPRE, [P, D])
    gpost = at("gpost", GPOST, [P, D])
    eT_hi = at("eT_hi", ET, [P, KD, SEQ], f32r)
    eT_lo = at("eT_lo", ET + KD * SEQ, [P, KD, SEQ], f32r)
    xT_hi = [at(f"xT_hi{b}", ET + 2 * b * KD * SLOTS, [P, KD, SLOTS], f32r) for b in range(2)]
    xT_lo = [at(f"xT_lo{b}", ET + (2 * b + 1) * KD * SLOTS, [P, KD, SLOTS], f32r) for b in range(2)]
    facc = at("facc", FACC, [P, TT, D])
    y = at("y", Y, [P, D])
    sg = at("sg", SG, [P, FC])
    acts = at("acts", ACTS, [P, 2, FC])
    aT_hi = at("aT_hi", AT, [P, 2, KF, P], f32r)
    aT_lo = at("aT_lo", AT + 2 * FC, [P, 2, KF, P], f32r)
    pick = at("pick", PICK, [P, TT, SLOTS])
    pick_gated = at("pick_gated", PICKG, [P, TT, SLOTS])
    pgT = at("pgT", PGT, [P, SEQ])
    ident = at("ident", IDENT, [P, P])
    iota = at("iota", IOTA, [P, P])
    small = at("small", SMALL, [P, SMALL_N])
    hT_hi = at("hT_hi", TURNED_HI, [P, KD, SEQ], f32r)
    hT_lo = at("hT_lo", TURNED_LO, [P, KD, SEQ], f32r)
    z = at("z", Z, [P, TT, IN_COLS])
    cn = at("cn", CN, [P, TT, QL + KVL])
    cT_hi = at("cT_hi", CT_HI, [P, KQ + KKV, SEQ], f32r)
    cT_lo = at("cT_lo", CT_LO, [P, KQ + KKV, SEQ], f32r)
    rw_hi = at("rw_hi", RW_HI, [P, KQ, HG, 2 * ROPE], f32r)
    rw_lo = at("rw_lo", RW_LO, [P, KQ, HG, 2 * ROPE], f32r)
    zr = at("zr", ZR, [P, TT, 2 * ROPE])
    krT = at("krT", KRT, [P, SEQ])
    ta = at("ta", TA, [P, SEQ])
    tb = at("tb", TB, [P, SEQ])
    qT = at("qT", QT, [P, HEADS, SEQ])
    qrT = at("qrT", QRT, [P, HEADS, SEQ])
    kT = at("kT", KT, [P, HEADS, SEQ])
    v = at("v", V, [P, TT, HEADS * VDIM])
    pr = at("pr", PR, [P, HEADS, KPOS])
    prT = at("prT", PTT, [P, HEADS, KPOS])
    mixT_hi = at("mixT_hi", TURNED_HI, [P, KD, SEQ], f32r)
    mixT_lo = at("mixT_lo", TURNED_LO, [P, KD, SEQ], f32r)
    piece_hi = [at(f"piece_hi{i}", w, [P, SLOT], f32r) for i, w in enumerate(PIECE_HI)]
    piece_lo = [at(f"piece_lo{i}", RAW + (i % RING) * SLOT, [P, SLOT], f32r) for i in range(PIECES)]
    pl = at("pl", PL, [P, 2, SEQ])
    pwbd = at("pwbd", PWBD, [P, 2, P])
    psc = at("psc", PSC, [P, 2])
    bands = at("bands", BANDS, [P, GROUPS, KPOS])
    cs = at("cs", CS, [P, SEQ])
    mask = at("mask", MASK, [P, KPOS])
    gq = at("gq", GQ, [P, QL])
    gkv = at("gkv", GKV, [P, KVL])
    tri = at("tri", TRI, [P, P])
    ones = at("ones", ONES, [P, P])
    wr = at("wr", WR, [P, KD, EXPERTS])
    hT_route = at("hT_route", ROUTED_HT, [P, KD, SEQ])
    junk = at("junk", PICK, [P, D], mybir.dt.bfloat16)

    cut = [0]

    def col(n):
        a = cut[0]
        cut[0] += n
        return a

    rev = small[:, col(EXPERTS):cut[0]]
    NORMS = [(n, t) for n in ("x", "kv", "q", "f") for t in range(TT)]
    sq, root, rs = ({n: small[:, col(1):cut[0]] for n in NORMS} for _ in range(3))
    sq_half = [small[:, col(1):cut[0]] for _ in range(TT)]
    softmax_at = cut[0]
    neg_max = small[:, col(2 * HEADS):cut[0]]
    p_sum = small[:, col(2 * HEADS):cut[0]]
    p_inv = small[:, col(2 * HEADS):cut[0]]
    cut[0] = softmax_at

    def per_expert():
        return small[:, col(TT * EXPERTS):cut[0]].rearrange("p (t e) -> p t e", t=TT)

    lg, eq, key, oh1, oh2, lg2, gate, chosen, rank = (per_expert() for _ in range(9))
    m1, m2, kk, gap, e2, g1, g2 = (small[:, col(TT):cut[0]] for _ in range(7))
    most = small[:, col(1):cut[0]]
    eps = small[:, col(1):cut[0]]
    ahead = small[:, col(1):cut[0]]
    most_int = small[:, col(1):cut[0]].bitcast(i32)
    assert cut[0] <= SMALL_N

    bank = [nc.alloc_psum_tensor(f"bank{i}", [P, BK], f32) for i in range(8)]

    S = nc.alloc_semaphore
    x_loaded = [S(f"x_loaded{t}") for t in range(TT)]
    ident_loaded, tables_loaded = S("ident_loaded"), S("tables_loaded")
    gpre_loaded, gpost_loaded, glow_loaded = S("gpre_loaded"), S("gpost_loaded"), S("glow_loaded")
    pool_w_loaded, rank_tables_loaded, out_stored = S("pool_w_loaded"), S("rank_tables_loaded"), S("out_stored")
    facc_zeroed = S("facc_zeroed")
    piece_loaded = [S(f"piece_loaded{i}") for i in range(RING)]
    piece_rounded, piece_split = S("piece_rounded"), S("piece_split")
    hT_rounded, cT_rounded, mixT_rounded = S("hT_rounded"), S("cT_rounded"), S("mixT_rounded")
    piece_used = S("piece_used")
    raw_gu_loaded = [S(f"raw_gu_loaded{i}") for i in range(2)]
    raw_d_loaded = [S(f"raw_d_loaded{i}") for i in range(2)]
    gu_hi, gu_split = S("gu_hi"), S("gu_split")
    d_hi, d_split, d_used = S("d_hi"), S("d_split"), S("d_used")
    bank_full = [S(f"bank_full{i}") for i in range(8)]
    bank_free = [S(f"bank_free{i}") for i in range(8)]
    dve_step = S("dve_step")
    squares = S("squares")
    roots = S("roots")
    mean_ready = S("mean_ready")
    rs_ready = S("rs_ready")
    h_ready = S("h_ready")
    x_updated = S("x_updated")
    cn_ready, rope_w_ready, zr_ready, krT_ready = S("cn_ready"), S("rope_w_ready"), S("zr_ready"), S("krT_ready")
    max_ready, exp_ready, probs_ready = S("max_ready"), S("exp_ready"), S("probs_ready")
    pad_ready = S("pad_ready")
    eT_part, eT_ready = S("eT_part"), S("eT_ready")
    gap_ready, e2_ready, chosen_ready = S("gap_ready"), S("e2_ready"), S("chosen_ready")
    routed = S("routed")
    gu_full, silu_done, gated = S("gu_full"), S("silu_done"), S("gated")
    tr_full, aT_part, aT_ready = S("tr_full"), S("aT_part"), S("aT_ready")
    pick_ready, pick_gated_ready = S("pick_ready"), S("pick_gated_ready")
    gathered, pgT_full, pgT_ready = S("gathered"), S("pgT_full"), S("pgT_ready")
    y_ready = S("y_ready")
    spread, added = S("spread"), S("added")
    f_ready = S("f_ready")

    def jb(layer, name):
        return bank[JOBS[layer, name][0]]

    def wait_free(layer, name):
        b, _, n = JOBS[layer, name]
        if n:
            nc.tensor.wait_ge(bank_free[b], n)

    def fill(ins, layer, name):
        ins.then_inc(bank_full[JOBS[layer, name][0]], 1)

    def wait_full(eng, layer, name):
        b, n, _ = JOBS[layer, name]
        eng.wait_ge(bank_full[b], n + 1)

    def wait_drained(eng, layer, *names):
        for name in names:
            b, _, n = JOBS[layer, name]
            eng.wait_ge(bank_free[b], n + 1)

    def z_drained(eng, layer, t):
        wait_drained(eng, layer, f"z{t}0", f"z{t}1")

    root_no, square_no = {}, {}

    def drain(ins, layer, name):
        ins.then_inc(bank_free[JOBS[layer, name][0]], 1)

    def bank_k(layer, name, k=4):
        return jb(layer, name)[:, 0:k * P].rearrange("p (k n) -> p k n", k=k)

    def raw_gu(s):
        return raw[:, 2 * s * SLOT:2 * (s + 1) * SLOT].rearrange("p (k w n) -> p k w n", k=KD, w=2)

    def raw_d(s):
        return raw[:, (4 + s) * SLOT:(5 + s) * SLOT]

    def part_gu(t, s, k):
        a = 2 * s * SLOT + k * 2 * FC
        return t[:, a:a + 2 * FC]

    def half_gu(t, s, i):
        a = 2 * s * SLOT + i * SLOT
        return t[:, a:a + SLOT]

    def part_d(t, s, k, n):
        a = (4 + s) * SLOT + k * D + n * BK
        return t[:, a:a + BK]

    def slot(i):
        return raw[:, i * SLOT:(i + 1) * SLOT]

    def f32v(ap):
        return ap.bitcast(f32)

    DU = DCH * TT

    block = nc.Block()
    with block:
        @block.sync
        def _(sp):
            def load_x(t):
                sp.dma_start(x[:, t, :], x_in[0, t * P:(t + 1) * P, :]).then_inc(x_loaded[t], 16)

            def attention_loads(layer):
                def piece(i, src, shape):
                    s = i % RING
                    dst = slot(s)[:, 0:shape[0] * shape[1]].rearrange("p (k n) -> p k n", k=shape[0])
                    if i >= RING:
                        sp.wait_ge(piece_used, (PIECES - 1) * layer + i - RING + 1)
                    sp.dma_start(dst, src).then_inc(piece_loaded[s], 16)

                for j in range(4):
                    piece(P_IN + j, w_in[layer, 2 * j * P:2 * (j + 1) * P, :].rearrange("(k p) n -> p k n", p=P),
                          (2, IN_COLS))
                    if layer == 0 and j == 0:
                        load_x(1)
                for g in range(2):
                    piece(P_UQ[g], w_uq[layer, :, HG * g:HG * (g + 1), :].rearrange("(k p) h n -> p k (h n)", p=P),
                          (KQ, HG * QK))
                    piece(P_UKV[g], w_ukv[layer, :, HG * g:HG * (g + 1), :].rearrange("(k p) h n -> p k (h n)", p=P),
                          (KKV, HG * KV))
                for i, j in enumerate(WOUT_ORDER):
                    piece(P_OUT + i, w_out[layer, 2 * j * P:2 * (j + 1) * P, :].rearrange("(k p) n -> p k n", p=P),
                          (2, D))

            def load_gu(s, gate_w, up_w):
                sp.dma_start(raw_gu(s)[:, :, 0, :], gate_w).then_inc(raw_gu_loaded[s], 16)
                sp.dma_start(raw_gu(s)[:, :, 1, :], up_w).then_inc(raw_gu_loaded[s], 16)

            def load_d(s, down_w):
                sp.dma_start(raw_d(s).rearrange("p (k n) -> p k n", k=KF), down_w).then_inc(raw_d_loaded[s], 16)

            load_x(0)
            sp.dma_start(ident[:, :], c_ident).then_inc(ident_loaded, 16)
            attention_loads(0)

            def dense_gu(c, s):
                load_gu(s, w_gate_d[0, :, ts(c * FC, FC)].rearrange("(k p) n -> p k n", p=P),
                        w_up_d[0, :, ts(c * FC, FC)].rearrange("(k p) n -> p k n", p=P))

            def dense_d(c, s):
                load_d(s, w_down_d[0, ts(c * FC, FC), :].rearrange("(k p) n -> p k n", p=P))

            for c in range(2):
                sp.wait_ge(piece_used, PIECES - RING + 2 * (c + 1))
                dense_gu(c, c)
            sp.wait_ge(piece_used, PIECES - 1)
            dense_d(0, 0)
            wait_full(sp, 0, "o11")
            dense_d(1, 1)

            def dense_chunk(c, s):
                sp.wait_ge(gu_split, (c - 1) * 2)
                dense_gu(c, s)
                sp.wait_ge(d_split, c - 1)
                dense_d(c, s)

            with sp.Fori(1, DCH // 2) as j:
                for s in range(2):
                    dense_chunk(j * 2 + s, s)
            dense_chunk(DCH - 1, 0)
            sp.wait_ge(gu_split, 2 * DCH)
            sp.wait_ge(d_split, DCH)
            attention_loads(1)

            def expert_gu(e, c, s):
                load_gu(s, w_gate_e[0, ts(e, 1), :, ts(c * FC, FC)].rearrange("a (k p) n -> p (a k) n", p=P),
                        w_up_e[0, ts(e, 1), :, ts(c * FC, FC)].rearrange("a (k p) n -> p (a k) n", p=P))

            def expert_d(e, c, s):
                load_d(s, w_down_e[0, ts(e, 1), ts(c * FC, FC), :].rearrange("a (k p) n -> p (a k) n", p=P))

            def expert_chunk(n, e, c, s):
                sp.wait_ge(gu_split, (n + (DCH - 1)) * 2)
                expert_gu(e, c, s)
                sp.wait_ge(d_split, n + (DCH - 1))
                expert_d(e, c, s)

            for c in range(2):
                sp.wait_ge(piece_used, PIECES - 1 + PIECES - RING + 2 * (c + 1))
                expert_gu(0, c, c)
            sp.wait_ge(piece_used, 2 * (PIECES - 1))
            expert_d(0, 0, 0)
            wait_full(sp, 1, "o11")
            expert_d(0, 1, 1)
            with sp.Fori(1, ECH // 2) as j:
                for s in range(2):
                    expert_chunk(j * 2 + s, 0, j * 2 + s, s)
            with sp.Fori(1, EXPERTS) as e:
                with sp.Fori(0, ECH // 2) as j:
                    for s in range(2):
                        expert_chunk(e * ECH + j * 2 + s, e, j * 2 + s, s)
            sp.wait_ge(routed, 1)
            over = sp.value_load(most_int[0:1, 0:1], min_val=0, max_val=SEQ)
            with sp.If(over > SLOTS):
                with sp.Fori(EXPERTS, 2 * EXPERTS) as e:
                    with sp.Fori(0, ECH // 2) as j:
                        for s in range(2):
                            expert_chunk(e * ECH + j * 2 + s, e - EXPERTS, j * 2 + s, s)
            with sp.Else():
                sp.nop()
            for t in range(TT):
                sp.wait_ge(x_updated, 3 * TT + t + 1)
                sp.dma_start(out[0, t * P:(t + 1) * P, :], x[:, t, :]).then_inc(out_stored, 16)
            sp.wait_ge(out_stored, 16 * TT)

        @block.gpsimd
        def _(pool):
            def gains(dst, src, sem):
                pool.dma_start(dst, src.partition_broadcast(P)).then_inc(sem, 16)

            def swapped(dst, src, last):
                half = ROPE // 2
                nc.gpsimd.tensor_copy(dst[..., 0:ROPE], src)
                nc.gpsimd.tensor_copy(dst[..., ROPE:ROPE + half], src[..., half:ROPE])
                nc.gpsimd.tensor_copy(dst[..., ROPE + half:2 * ROPE], src[..., 0:half]).then_inc(last, 1)

            nc.gpsimd.memset(eps[:, :], EPS).then_inc(pad_ready, 1)
            gains(gpre[:, :], attn_pre_g[0, :], gpre_loaded)
            gains(gq[:, :], q_norm_g[0, :], glow_loaded)
            gains(gkv[:, :], kv_norm_g[0, :], glow_loaded)
            pool.dma_start(bands[:, :, :].rearrange("p g n -> p (g n)"), c_bands[:, 0:GROUPS * KPOS]).then_inc(tables_loaded, 16)
            pool.dma_start(cs[:, :], c_bands[:, GROUPS * KPOS:]).then_inc(tables_loaded, 16)
            pool.dma_start(mask[:, :], c_mask).then_inc(tables_loaded, 16)
            pool.dma_start(iota[:, :], c_iota[:, 0:P]).then_inc(tables_loaded, 16)
            pool.dma_start(rev, c_iota[:, P:]).then_inc(tables_loaded, 16)
            gains(gpost[:, :], attn_post_g[0, :], gpost_loaded)
            for layer in range(DEPTH):
                if layer:
                    pool.wait_ge(d_used, DU)
                    gains(gq[:, :], q_norm_g[1, :], glow_loaded)
                    gains(gkv[:, :], kv_norm_g[1, :], glow_loaded)
                    pool.dma_start(tri[:, :], c_rank[:, 0:P]).then_inc(rank_tables_loaded, 16)
                    pool.dma_start(ones[:, :], c_rank[:, P:]).then_inc(rank_tables_loaded, 16)
                    pool.dma_start(wr[:, :, :], w_router[0, :, :].rearrange("(k p) e -> p k e", p=P)).then_inc(rank_tables_loaded, 16)
                nc.gpsimd.memset(pwbd[:, :, :], 0.0).then_inc(pad_ready, 1)
                pool.wait_ge(pad_ready, layer + 2)
                for g in range(GROUPS):
                    a = (g % 2) * GDIM
                    pool.dma_start(pwbd[a:a + GDIM, g // 2, a:a + GDIM], pool_w[layer, g, :, :]).then_inc(pool_w_loaded, 16)
                pool.dma_start(psc[:, :], pool_scale[layer, :].rearrange("(a p) -> p a", p=P),
                               allow_slow_non_contiguous=True).then_inc(pool_w_loaded, 16)
                if layer == 0:
                    pool.wait_ge(h_ready, 2 * TT)
                gains_after = ffn_pre_g[layer, :]
                if layer:
                    pool.wait_ge(h_ready, 2 * (2 * layer + 1) * TT)
                gains(gpre[:, :], gains_after, gpre_loaded)
                def rope_of_z(t):
                    z_drained(pool, layer, t)
                    swapped(zr[:, t, :], z[:, t, QL + KVL:U0], zr_ready)

                def rope_of_w(g):
                    i = P_UQ[g]
                    pool.wait_ge(piece_split, PIECES * layer + i + 1)
                    if g:
                        wait_full(pool, layer, "qr2_0")
                    for dst, src in ((rw_hi, piece_hi[i]), (rw_lo, piece_lo[i])):
                        w = src[:, 0:KQ * HG * QK].rearrange("p (kh n) -> p kh n", n=QK)
                        swapped(dst[:, :, :, :].rearrange("p k h n -> p (k h) n"), w[:, :, NOPE:QK], rope_w_ready)

                rope_of_z(0)
                rope_of_w(0)
                rope_of_z(1)
                rope_of_w(1)
                pool.wait_ge(x_updated, (2 * layer + 1) * TT)
                gains(gpost[:, :], ffn_post_g[layer, :], gpost_loaded)
                if layer == 0:
                    pool.wait_ge(h_ready, 2 * 2 * TT)
                    gains(gpre[:, :], attn_pre_g[1, :], gpre_loaded)
                    pool.wait_ge(x_updated, 2 * TT)
                    gains(gpost[:, :], attn_post_g[1, :], gpost_loaded)
                else:
                    nc.gpsimd.memset(facc[:, :, :], 0.0).then_inc(facc_zeroed, 1)

        @block.scalar
        def _(act):
            copy, activation = nc.scalar.copy, nc.scalar.activation
            def square(src, width, dst, name, offset=0):
                square_no[name] = len(square_no) + 1
                activation(junk[:, offset:offset + src.free_size()], src, ACT.Square, scale=float(width) ** -0.5,
                           accum_out=dst).then_inc(squares, 1)

            def roots_ahead():
                activation(ahead, eps, ACT.Sqrt)

            def root_of(layer, n, t):
                root_no[layer, n, t] = len(root_no) + 1
                activation(root[n, t], sq[n, t], ACT.Sqrt, bias=eps[:, :]).then_inc(roots, 1)

            def norm(layer, n, t, src, width):
                square(src, width, sq[n, t], (layer, n, t))
                act.wait_ge(squares, square_no[layer, n, t])
                root_of(layer, n, t)

            def norm_of_banks(layer, name, t):
                for n, dst in enumerate((sq["f", t], sq_half[t])):
                    if name == "o":
                        wait_full(act, layer, f"o{t}{n}")
                    square(jb(layer, f"{name}{t}{n}")[:, :], D, dst, (layer, name, t, n), n * BK)
                act.wait_ge(mean_ready, (2 * layer + (name == "f")) * TT + t + 1)
                root_no[layer, name, t] = len(root_no) + 1
                activation(root["f", t], sq["f", t], ACT.Sqrt, bias=eps[:, :]).then_inc(roots, 1)

            def round_piece(layer, i):
                act.wait_ge(piece_loaded[i % RING], 16 * (2 * layer + i // RING + 1))
                used = (PIECES - 1) * layer
                if i < 4:
                    if layer and i == 0:
                        act.wait_ge(gu_full, DU)
                elif i < 8:
                    act.wait_ge(piece_used, used + (i - 3 if i < 6 else i - 1))
                elif i == 9:
                    act.wait_ge(piece_used, used + 8)
                words = slice(0, PIECE_WORDS[i])
                copy(piece_hi[i][:, words], slot(i % RING)[:, words]).then_inc(piece_rounded, 1)

            def attention(layer, loaded):
                if layer == 0:
                    roots_ahead()
                for t in range(TT):
                    if layer == 0:
                        act.wait_ge(x_loaded[t], 16)
                        square(x[:, t, :], D, sq["x", t], (0, "x", t))
                    else:
                        act.wait_ge(d_used, DU - 1 + t)
                        norm_of_banks(0, "f", t)
                    round_piece(layer, (0, 3)[t])
                    if layer:
                        norm_of_x(0, "f", t)
                    else:
                        act.wait_ge(squares, square_no[0, "x", t])
                        root_of(0, "x", t)
                    for i in range(2):
                        wait_full(act, layer, f"hT{t}{i}")
                        copy(hT_hi[:, 4 * i:4 * i + 4, t * P:(t + 1) * P], bank_k(layer, f"hT{t}{i}"))\
                            .then_inc(hT_rounded, 1)
                    if t == 0:
                        round_piece(layer, 1)
                        round_piece(layer, 2)

                def latent(name, a, k, t):
                    wait_full(act, layer, name)
                    copy(cT_hi[:, a:a + k, t * P:(t + 1) * P], bank_k(layer, name, k)).then_inc(cT_rounded, 1)

                for t in range(TT):
                    wait_full(act, layer, f"z{t}0")
                    act.wait_ge(rs_ready, 2 * layer + t + 1)
                    drain(activation(z[:, t, 0:HALF_IN], jb(layer, f"z{t}0")[:, 0:HALF_IN], ACT.Copy, scale=rs["x", t]),
                          layer, f"z{t}0")
                    z_drained(act, layer, t)
                    norm(layer, "kv", t, z[:, t, QL:QL + KVL], KVL)
                    norm(layer, "q", t, z[:, t, 0:QL], QL)
                    if t == 0:
                        for i in (4, 5):
                            round_piece(layer, i)
                    latent(f"cA{t}", 0, KQ, t)
                    if t == 0:
                        latent("cB0", KQ, KKV, 0)
                wait_full(act, layer, "pooled")
                drain(copy(pl[:, :, :].rearrange("p a n -> p (a n)"), jb(layer, "pooled")[:, :]), layer, "pooled")

                def projections(g):
                    a = HG * g
                    wait_full(act, layer, f"q01_{g}")
                    drain(copy(qT[:, a:a + 2, :].rearrange("p k n -> p (k n)"), jb(layer, f"q01_{g}")[:, :]),
                          layer, f"q01_{g}")
                    if g == 0:
                        latent("cB1", KQ, KKV, 1)
                    wait_full(act, layer, f"k01_{g}")
                    drain(copy(kT[:, a:a + 2, :].rearrange("p k n -> p (k n)"), jb(layer, f"k01_{g}")[:, :]),
                          layer, f"k01_{g}")
                    wait_full(act, layer, f"k2_{g}")
                    drain(copy(kT[:, a + 2, :], jb(layer, f"k2_{g}")[:, 0:SEQ]), layer, f"k2_{g}")

                def exps(g):
                    for i in range(HG * g, HG * (g + 1)):
                        act.wait_ge(max_ready, HEADS * layer + i + 1)
                        for b, (a, w) in enumerate(((0, P), (P, SEQ))):
                            last = activation(pr[:, i, a:a + w], pr[:, i, a:a + w], ACT.Exp,
                                              bias=neg_max[:, 2 * i + b:2 * i + b + 1],
                                              accum_out=p_sum[:, 2 * i + b:2 * i + b + 1])
                        last.then_inc(exp_ready, 1)

                def transposed(g):
                    for i in range(HG * g, HG * (g + 1)):
                        wait_full(act, layer, f"pT{i}")
                        drain(copy(prT[:, i, :], jb(layer, f"pT{i}")[:, 0:KPOS]), layer, f"pT{i}")

                def attended(g):
                    for i in range(HG * g, HG * (g + 1)):
                        wait_full(act, layer, f"a{i}")
                        copy(mixT_hi[:, i, :], jb(layer, f"a{i}")[:, 0:SEQ]).then_inc(mixT_rounded, 1)

                projections(0)
                round_piece(layer, 6)
                round_piece(layer, 7)
                exps(0)
                round_piece(layer, 8)
                projections(1)
                transposed(0)
                round_piece(layer, 9)
                round_piece(layer, 10)
                round_piece(layer, 11)
                exps(1)
                attended(0)
                act.wait_ge(pool_w_loaded, 16 * (GROUPS + 1) * (layer + 1))
                wait_full(act, layer, "poolout")
                for i in range(2):
                    activation(mixT_hi[:, HEADS + i, :], jb(layer, "poolout")[:, i * SEQ:(i + 1) * SEQ], ACT.Copy,
                               scale=psc[:, i:i + 1]).then_inc(mixT_rounded, 1)
                transposed(1)
                attended(1)
                roots_ahead()
                round_gu(0, 0, loaded)
                round_gu(0, 1)

            def norm_of_x(layer, name, t):
                act.wait_ge(x_updated, (2 * layer + (name == "f")) * TT + t + 1)
                norm((layer, name), "x", t, x[:, t, :], D)

            def junction(layer, name, t):
                norm_of_banks(layer, name, t)
                norm_of_x(layer, name, t)

            def round_gu(s, i, loaded=None, used=None):
                if loaded is not None:
                    act.wait_ge(raw_gu_loaded[s], loaded)
                if used is not None:
                    act.wait_ge(gu_full, used)
                copy(half_gu(hi, s, i), half_gu(raw, s, i)).then_inc(gu_hi, 1)

            def round_d(s, loaded, used=None):
                act.wait_ge(raw_d_loaded[s], loaded)
                if used is not None:
                    act.wait_ge(d_used, used)
                copy(hi[:, (4 + s) * SLOT:(5 + s) * SLOT], raw_d(s)).then_inc(d_hi, 1)

            def round_aT(u, s):
                act.wait_ge(tr_full, u + 1)
                act.wait_ge(d_used, u - 1)
                copy(aT_hi[:, s, :, :].rearrange("p k n -> p (k n)"), bank[2 + s][:, 0:FC]).then_inc(aT_part, 1)

            def silu(u, s, scale=1.0):
                act.wait_ge(gu_full, u + 1)
                if not (isinstance(u, int) and u == 0):
                    act.wait_ge(gated, u)
                activation(sg[:, :], bank[s][:, 0:FC], ACT.Silu, scale=scale).then_inc(silu_done, 1)

            def dense():
                for t in range(TT):
                    junction(0, "o", t)
                    for i in range(2):
                        wait_full(act, 0, f"fT{t}{i}")
                        copy(eT_hi[:, 4 * i:4 * i + 4, t * P:(t + 1) * P], bank_k(0, f"fT{t}{i}")).then_inc(eT_part, 1)
                silu(0, 0, rs["x", 0])

                def unit(c, t, s, first=False, more=True):
                    u = c * 2 + t
                    if t == 0:
                        round_d(s, loaded_d(c, s), None if isinstance(c, int) and c < 2 else (c - 1) * 2)
                    if not (first and t == 0):
                        if first:
                            act.wait_ge(tr_full, 1)
                            copy(aT_hi[:, 0, :, :].rearrange("p k n -> p (k n)"), bank[2][:, 0:FC]).then_inc(aT_part, 1)
                        else:
                            round_aT(u - 1, 1 - t)
                    if more:
                        if t == 0:
                            round_gu(1 - s, 0, loaded_gu(c + 1, 1 - s), None if first else c * 2)
                        else:
                            round_gu(1 - s, 1)
                    if not (first and t == 0):
                        silu(u, t, rs["x", t])

                def loaded_gu(c, s):
                    return ((c - s) // 2 + 1) * 32 if isinstance(c, int) else (c - s) * 16 + 32

                def loaded_d(c, s):
                    return ((c - s) // 2 + 1) * 16 if isinstance(c, int) else (c - s) * 8 + 16

                for t in range(TT):
                    unit(0, t, 0, first=True)
                for t in range(TT):
                    unit(1, t, 1)
                with act.Fori(1, DCH // 2) as j:
                    for s in range(2):
                        for t in range(TT):
                            unit(j * 2 + s, t, s)
                for t in range(TT):
                    unit(DCH - 1, t, 0, more=False)
                roots_ahead()
                round_aT(DU - 1, 1)

            PRE = ((DCH + 1) // 2, DCH // 2)

            def route():
                for t in range(TT):
                    junction(1, "o", t)
                    wait_full(act, 1, f"fT{t}0")
                    drain(copy(hT_route[:, 0:4, t * P:(t + 1) * P], bank_k(1, f"fT{t}0")), 1, f"fT{t}0")
                round_gu(1, 0, (PRE[1] + 1) * 32)
                round_gu(1, 1)
                round_d(0, (PRE[0] + 1) * 16)
                act.wait_ge(gap_ready, 1)
                activation(e2, gap, ACT.Exp).then_inc(e2_ready, 1)

            def gathered_rounded(e, b, i):
                act.wait_ge(gathered, e * 2 + i + 1)
                copy(xT_hi[b][:, 4 * i:4 * i + 4, :], bank[6 + i][:, :].rearrange("p (k n) -> p k n", k=4))\
                    .then_inc(eT_part, 1)

            def sums_out(e):
                act.wait_ge(d_used, e * ECH + (ECH + DU))
                copy(y[:, 0:BK], bank[4][:, :]).then_inc(y_ready, 1)

            def expert(e, b, first_one, last_one):
                def one(c_pair, s, more=True):
                    starts = isinstance(c_pair, int) and c_pair == 0
                    n = e * ECH + c_pair * 2 + s
                    k = e * (ECH // 2) + c_pair
                    u = n + DU
                    def next_gu():
                        round_gu(1 - s, 0, (k + s + 1 + PRE[1 - s]) * 32, u)

                    if starts and isinstance(e, int) and e == 0:
                        if s == 0:
                            round_d(1, (k + 1 + PRE[1]) * 16)
                        else:
                            next_gu()
                            round_gu(0, 1)
                            round_aT(u - 1, 0)
                        silu(u, s)
                        return
                    if starts and s == 1 and not first_one:
                        sums_out(e - 1)
                    round_d(s, (k + 1 + PRE[s]) * 16, n + (DU - 1))
                    if not (starts and s == 0 and first_one):
                        round_aT(u - 1, 1 - s)
                    if more:
                        next_gu()
                    silu(u, s)
                    if more:
                        round_gu(1 - s, 1)

                for s in range(2):
                    one(0, s)
                for i in range(3):
                    with act.Fori(HELD[i], HELD[i + 1]) as j:
                        for s in range(2):
                            one(j, s)
                    if i < 2 and not last_one:
                        gathered_rounded(e + 1, 1 - b, i)
                one(ECH // 2 - 1, 0)
                act.wait_ge(pgT_full, e + 1)
                copy(pgT[:, :], bank[6][:, 0:SEQ]).then_inc(pgT_ready, 1)
                one(ECH // 2 - 1, 1, more=not last_one)

            def experts(first):
                k = first * (ECH // 2)
                if first:
                    for i in range(2):
                        round_gu(0, i, (k + 1 + PRE[0]) * 32 if i == 0 else None, first * ECH + DU - 1 if i == 0 else None)
                for i in range(2):
                    gathered_rounded(first, 0, i)
                expert(first, 0, True, False)
                with act.Fori(0, EXPERTS // 2 - 1) as j:
                    for b in range(2):
                        expert(j * 2 + (first + 1 + b), 1 - b, False, False)
                last = first + EXPERTS - 1
                expert(last, 1, False, True)
                round_aT(last * ECH + (ECH - 1 + DU), 1)
                sums_out(last)

            act.wait_ge(pad_ready, 1)
            attention(0, 32)
            dense()
            attention(1, (PRE[0] + 1) * 32)
            route()
            experts(0)
            act.wait_ge(routed, 1)
            over = act.value_load(most_int[0:1, 0:1], min_val=0, max_val=SEQ)
            with act.If(over > SLOTS):
                experts(EXPERTS)
            with act.Else():
                act.nop()
            roots_ahead()
            act.wait_ge(f_ready, 1)
            for t in range(TT):
                norm(DEPTH, "f", t, facc[:, t, :], D)

        @block.vector
        def _(dve):
            V_ = nc.vector
            step = [0]

            def link(ins):
                step[0] += 1
                ins.then_inc(dve_step, 1)
                dve.wait_ge(dve_step, step[0])

            def inverse(layer, n, t, name=None):
                dve.wait_ge(roots, root_no[layer, name or n, t])
                return V_.reciprocal(rs[n, t], root[n, t])

            def weigh(t, i):
                half = slice(i * BK, (i + 1) * BK)
                V_.tensor_tensor(h[:, t, half], x[:, t, half], gpre[:, half], ALU.mult).then_inc(h_ready, 1)

            def junction(layer, name, t):
                number = 2 * layer + (name == "f")
                dve.wait_ge(gpost_loaded, 16 * (number + 1))
                for n in range(2):
                    a = n * BK
                    dve.wait_ge(squares, square_no[layer, name, t, n])
                    drain(V_.tensor_tensor(h[:, t, a:a + BK], jb(layer, f"{name}{t}{n}")[:, :], gpost[:, a:a + BK],
                                           ALU.mult), layer, f"{name}{t}{n}")
                V_.tensor_tensor(sq["f", t], sq["f", t], sq_half[t], ALU.add).then_inc(mean_ready, 1)
                link(inverse(layer, "f", t, name))
                wait_drained(dve, layer, f"{name}{t}0", f"{name}{t}1")
                dve.wait_ge(gpre_loaded, 16 * (number + 2))
                for i in range(2):
                    half = slice(i * BK, (i + 1) * BK)
                    new_x = V_.scalar_tensor_tensor(x[:, t, half], h[:, t, half], rs["f", t], x[:, t, half],
                                                    ALU.mult, ALU.add)
                    if i == 0:
                        link(new_x)
                    else:
                        new_x.then_inc(x_updated, 1)
                        dve.wait_ge(x_updated, number * TT + t + 1)
                    weigh(t, i)

            def attention(layer):
                before = (0, "f") if layer else 0
                rounded = 2 * TT * layer
                for t in range(TT):
                    if layer == 0:
                        dve.wait_ge(x_loaded[t], 16)
                        dve.wait_ge(gpre_loaded, 16)
                        for i in range(2):
                            weigh(t, i)
                    else:
                        dve.wait_ge(d_used, DU - 1 + t)
                        junction(0, "f", t)
                    low_piece(layer, (0, 3)[t])
                    for i in range(2):
                        dve.wait_ge(hT_rounded, rounded + 2 * t + i + 1)
                        part = (slice(None), slice(4 * i, 4 * i + 4), slice(t * P, (t + 1) * P))
                        drain(V_.tensor_tensor(hT_lo[part], bank_k(layer, f"hT{t}{i}"), f32v(hT_hi[part]), ALU.subtract),
                              layer, f"hT{t}{i}")
                    inverse(before, "x", t).then_inc(rs_ready, 1)
                    if t == 0:
                        low_piece(layer, 1)
                        low_piece(layer, 2)

                def low_latent(name, n, a, k, t):
                    dve.wait_ge(cT_rounded, rounded + n)
                    part = (slice(None), slice(a, a + k), slice(t * P, (t + 1) * P))
                    return V_.tensor_tensor(cT_lo[part], bank_k(layer, name, k), f32v(cT_hi[part]), ALU.subtract)

                def keys(t, n):
                    tok = slice(t * P, (t + 1) * P)
                    low_latent(f"cB{t}", n, KQ, KKV, t)
                    b = jb(layer, f"cB{t}")
                    V_.tensor_tensor(ta[0:ROPE, tok], b[0:ROPE, KVL:KVL + P], cs[0:ROPE, tok], ALU.mult)
                    drain(V_.tensor_tensor(tb[0:ROPE, tok], b[ROPE:P, KVL:KVL + P], cs[ROPE:P, tok], ALU.mult),
                          layer, f"cB{t}")
                    wait_drained(dve, layer, f"cB{t}")
                    link(V_.tensor_tensor(krT[0:ROPE, tok], ta[0:ROPE, tok], tb[0:ROPE, tok], ALU.add))
                    V_.tensor_copy(krT[ROPE:P, tok], krT[0:ROPE, tok]).then_inc(krT_ready, 1)

                dve.wait_ge(glow_loaded, 32 * (layer + 1))
                for t in range(TT):
                    wait_full(dve, layer, f"z{t}1")
                    dve.wait_ge(rs_ready, 2 * layer + t + 1)
                    drain(V_.tensor_scalar(z[:, t, HALF_IN:IN_COLS], jb(layer, f"z{t}1")[:, 0:HALF_IN], rs["x", t], None,
                                           ALU.mult), layer, f"z{t}1")
                    z_drained(dve, layer, t)
                    V_.tensor_tensor(cn[:, t, 0:QL], z[:, t, 0:QL], gq[:, :], ALU.mult).then_inc(cn_ready, 1)
                    link(inverse(layer, "kv", t))
                    V_.scalar_tensor_tensor(cn[:, t, QL:QL + KVL], z[:, t, QL:QL + KVL], rs["kv", t], gkv[:, :],
                                            ALU.mult, ALU.mult).then_inc(cn_ready, 1)
                    link(inverse(layer, "q", t))
                    link(V_.tensor_scalar(rs["q", t], rs["q", t], SCALE, None, ALU.mult))
                    if t == 0:
                        for i in (4, 5):
                            low_piece(layer, i)
                    drain(low_latent(f"cA{t}", 2 * t + 1, 0, KQ, t), layer, f"cA{t}")
                    if t == 0:
                        dve.wait_ge(tables_loaded, 80)
                        keys(0, 2)

                def projections(g):
                    a = HG * g
                    if g == 0:
                        keys(1, 4)

                    def values():
                        for t in range(TT):
                            wait_full(dve, layer, f"v{t}_{g}")
                            drain(V_.tensor_copy(v[:, t, a * VDIM:(a + HG) * VDIM], jb(layer, f"v{t}_{g}")[:, 0:HG * VDIM]),
                                  layer, f"v{t}_{g}")

                    if g:
                        values()
                    wait_full(dve, layer, f"r01_{g}")
                    csb = cs[:, :].unsqueeze(1).broadcast_to([P, 2, SEQ])
                    drain(V_.tensor_tensor(qrT[:, a:a + 2, :], jb(layer, f"r01_{g}")[:, :].rearrange("p (k n) -> p k n", k=2),
                                           csb, ALU.mult), layer, f"r01_{g}")
                    wait_full(dve, layer, f"qr2_{g}")
                    V_.tensor_copy(qT[:, a + 2, :], jb(layer, f"qr2_{g}")[:, 0:SEQ])
                    drain(V_.tensor_tensor(qrT[:, a + 2, :], jb(layer, f"qr2_{g}")[:, SEQ:2 * SEQ], cs[:, :], ALU.mult),
                          layer, f"qr2_{g}")
                    if g == 0:
                        values()

                def maxima(g):
                    for i in range(HG * g, HG * (g + 1)):
                        wait_full(dve, layer, f"s{i}")
                        for b, (a, w) in enumerate(((0, P), (P, SEQ))):
                            ins = V_.scalar_tensor_tensor(pr[:, i, a:a + w], jb(layer, f"s{i}")[:, a:a + w], rs["q", b],
                                                          mask[:, a:a + w], ALU.mult, ALU.add)
                        drain(ins, layer, f"s{i}")
                        wait_drained(dve, layer, f"s{i}")
                        V_.tensor_reduce(neg_max[:, 2 * i:2 * i + 1], pr[:, i, 0:P], AX.X, ALU.max, negate=True)
                        V_.tensor_reduce(neg_max[:, 2 * i + 1:2 * i + 2], pr[:, i, P:KPOS], AX.X, ALU.max, negate=True)\
                            .then_inc(max_ready, 1)

                def normalized(g):
                    for i in range(HG * g, HG * (g + 1)):
                        dve.wait_ge(exp_ready, HEADS * layer + i + 1)
                        link(V_.reciprocal(p_inv[:, 2 * i:2 * i + 2], p_sum[:, 2 * i:2 * i + 2]))
                        V_.tensor_scalar(pr[:, i, 0:P], pr[:, i, 0:P], p_inv[:, 2 * i:2 * i + 1], None, ALU.mult)
                        V_.tensor_scalar(pr[:, i, P:KPOS], pr[:, i, P:KPOS], p_inv[:, 2 * i + 1:2 * i + 2], None,
                                         ALU.mult).then_inc(probs_ready, 1)

                def low_mix(g):
                    for i in range(HG * g, HG * (g + 1)):
                        dve.wait_ge(mixT_rounded, KD * layer + i + 1 + (2 if g else 0))
                        drain(V_.tensor_tensor(mixT_lo[:, i, :], jb(layer, f"a{i}")[:, 0:SEQ], f32v(mixT_hi[:, i, :]),
                                               ALU.subtract), layer, f"a{i}")

                projections(0)
                low_piece(layer, 6)
                low_piece(layer, 7)
                maxima(0)
                normalized(0)
                low_piece(layer, 8)
                projections(1)
                maxima(1)
                normalized(1)
                low_mix(0)
                dve.wait_ge(mixT_rounded, KD * layer + HG + 2)
                for i in range(2):
                    ins = V_.scalar_tensor_tensor(mixT_lo[:, HEADS + i, :], jb(layer, "poolout")[:, i * SEQ:(i + 1) * SEQ],
                                                  psc[:, i:i + 1], f32v(mixT_hi[:, HEADS + i, :]), ALU.mult, ALU.subtract)
                drain(ins, layer, "poolout")
                low_piece(layer, 9)
                low_mix(1)
                low_piece(layer, 10)
                low_piece(layer, 11)
                for i in range(2):
                    low_gu(0, i, layer * 2 * DCH + i + 1)

            def low_piece(layer, i):
                dve.wait_ge(piece_rounded, PIECES * layer + i + 1)
                words = slice(0, PIECE_WORDS[i])
                V_.tensor_tensor(piece_lo[i][:, words], slot(i % RING)[:, words], f32v(piece_hi[i][:, words]), ALU.subtract)\
                    .then_inc(piece_split, 1)

            def low_gu(s, i, n):
                dve.wait_ge(gu_hi, n)
                a = 2 * s * SLOT + i * SLOT
                V_.tensor_tensor(lo[:, a:a + SLOT], raw[:, a:a + SLOT], f32v(hi[:, a:a + SLOT]), ALU.subtract)\
                    .then_inc(gu_split, 1)

            def low_d(s, n):
                dve.wait_ge(d_hi, n)
                a = (4 + s) * SLOT
                V_.tensor_tensor(lo[:, a:a + SLOT], raw[:, a:a + SLOT], f32v(hi[:, a:a + SLOT]), ALU.subtract)\
                    .then_inc(d_split, 1)

            def low_aT(u, s):
                dve.wait_ge(aT_part, u + 1)
                V_.tensor_tensor(aT_lo[:, s, :, :].rearrange("p k n -> p (k n)"), bank[2 + s][:, 0:FC],
                                 f32v(aT_hi[:, s, :, :]).rearrange("p k n -> p (k n)"), ALU.subtract)\
                    .then_inc(aT_ready, 1)

            def gate_up(u, s, scale=None):
                dve.wait_ge(silu_done, u + 1)
                if scale is None:
                    V_.tensor_tensor(acts[:, s, :], sg[:, :], bank[s][:, FC:2 * FC], ALU.mult).then_inc(gated, 1)
                else:
                    V_.scalar_tensor_tensor(acts[:, s, :], bank[s][:, FC:2 * FC], scale, sg[:, :], ALU.mult, ALU.mult)\
                        .then_inc(gated, 1)

            def dense():
                for t in range(TT):
                    junction(0, "o", t)
                    link(inverse((0, "o"), "x", t))
                    for i in range(2):
                        dve.wait_ge(eT_part, 2 * t + i + 1)
                        drain(V_.tensor_tensor(eT_lo[:, 4 * i:4 * i + 4, t * P:(t + 1) * P], bank_k(0, f"fT{t}{i}"),
                                               f32v(eT_hi[:, 4 * i:4 * i + 4, t * P:(t + 1) * P]), ALU.subtract),
                              0, f"fT{t}{i}")
                gate_up(0, 0, rs["x", 0])

                def unit(c, t, s, first=False, more=True):
                    u = c * 2 + t
                    if t == 0:
                        low_d(s, c + 1)
                    if not (first and t == 0):
                        low_aT(u - 1, 1 - t)
                    if more and first:
                        for i in range(TT * t):
                            low_gu(1 - s, i, c * 2 + (3 + i))
                    elif more:
                        low_gu(1 - s, t, c * 2 + (3 + t))
                    if not (first and t == 0):
                        gate_up(u, t, rs["x", t])

                for t in range(TT):
                    unit(0, t, 0, first=True)
                for t in range(TT):
                    unit(1, t, 1)
                with dve.Fori(1, DCH // 2) as j:
                    for s in range(2):
                        for t in range(TT):
                            unit(j * 2 + s, t, s)
                for t in range(TT):
                    unit(DCH - 1, t, 0, more=False)
                low_aT(DU - 1, 1)

            def over_e(a):
                return a.unsqueeze(2).broadcast_to([P, TT, EXPERTS])

            def route():
                for t in range(TT):
                    junction(1, "o", t)
                    wait_full(dve, 1, f"fT{t}1")
                    drain(V_.tensor_copy(hT_route[:, 4:8, t * P:(t + 1) * P], bank_k(1, f"fT{t}1")), 1, f"fT{t}1")
                    link(inverse((1, "o"), "x", t))
                    V_.tensor_scalar(h[:, t, :], h[:, t, :], rs["x", t], None, ALU.mult)

                low_gu(1, 0, (DCH + 1) * 2 + 1)

                revb = rev.unsqueeze(1).broadcast_to([P, TT, EXPERTS])
                wait_full(dve, 1, "logits")
                for t in range(TT):
                    ins = V_.tensor_scalar(lg[:, t, :], jb(1, "logits")[:, t * EXPERTS:(t + 1) * EXPERTS], rs["x", t], None,
                                           ALU.mult)
                drain(ins, 1, "logits")
                wait_drained(dve, 1, "logits")

                def top(src, m, oh):
                    link(V_.tensor_reduce(m, src, AX.X, ALU.max))
                    link(V_.tensor_tensor(eq, src, over_e(m), ALU.is_equal))
                    link(V_.tensor_tensor(key, eq, revb, ALU.mult))
                    link(V_.tensor_reduce(kk, key, AX.X, ALU.max))
                    link(V_.tensor_tensor(oh, key, over_e(kk), ALU.is_equal))

                top(lg, m1, oh1)
                link(V_.scalar_tensor_tensor(lg2, oh1, NEG, lg, ALU.mult, ALU.add))
                top(lg2, m2, oh2)
                V_.tensor_tensor(chosen, oh1, oh2, ALU.add).then_inc(chosen_ready, 1)
                V_.tensor_tensor(gap, m2, m1, ALU.subtract).then_inc(gap_ready, 1)
                low_d(0, DCH + 1)
                wait_full(dve, 1, "ranks")
                rk = jb(1, "ranks")
                V_.tensor_copy(rank, rk[:, 0:TT * EXPERTS].rearrange("p (t e) -> p t e", t=TT))
                ins = V_.tensor_reduce(most, rk[:, TT * EXPERTS:(TT + 1) * EXPERTS], AX.X, ALU.max)
                drain(ins, 1, "ranks")
                wait_drained(dve, 1, "ranks")

            def gates():
                dve.wait_ge(e2_ready, 1)
                link(V_.tensor_scalar(g2, e2, 1.0, None, ALU.add))
                link(V_.reciprocal(g1, g2))
                link(V_.tensor_tensor(g2, e2, g1, ALU.mult))
                V_.tensor_tensor(gate, oh1, over_e(g1), ALU.mult)
                link(V_.tensor_tensor(eq, oh2, over_e(g2), ALU.mult))
                link(V_.tensor_tensor(gate, gate, eq, ALU.add))
                V_.tensor_copy(most_int[:, :], most).then_inc(routed, 1)

            def picks(e, col_e):
                for t in range(TT):
                    last = V_.tensor_scalar(pick[:, t, :], iota[:, :], rank[:, t, ts(col_e, 1)], chosen[:, t, ts(col_e, 1)],
                                            ALU.is_equal, ALU.mult)
                last.then_inc(pick_ready, 1)

            def picks_gated(e, col_e):
                for t in range(TT):
                    last = V_.tensor_scalar(pick_gated[:, t, :], iota[:, :], rank[:, t, ts(col_e, 1)], gate[:, t, ts(col_e, 1)],
                                            ALU.is_equal, ALU.mult)
                last.then_inc(pick_gated_ready, 1)

            def gathered_low(e, b, i):
                dve.wait_ge(eT_part, e * 2 + (i + 5))
                V_.tensor_tensor(xT_lo[b][:, 4 * i:4 * i + 4, :], bank[6 + i][:, :].rearrange("p (k n) -> p k n", k=4),
                                 f32v(xT_hi[b][:, 4 * i:4 * i + 4, :]), ALU.subtract).then_inc(eT_ready, 1)

            def sums_out(e):
                dve.wait_ge(d_used, e * ECH + (ECH + DU))
                V_.tensor_copy(y[:, BK:2 * BK], bank[5][:, :]).then_inc(y_ready, 1)

            def add(e, t, b=6):
                for n in range(2):
                    dve.wait_ge(spread, e * 4 + (2 * t + n + 1))
                    V_.tensor_tensor(facc[:, t, n * BK:(n + 1) * BK], facc[:, t, n * BK:(n + 1) * BK],
                                     bank[b + n][:, :], ALU.add).then_inc(added, 1)

            def expert(e, b, first, first_one, last_one):
                def one(c_pair, s, more=True):
                    starts = isinstance(c_pair, int) and c_pair == 0
                    n = e * ECH + c_pair * 2 + s
                    u = n + DU
                    if starts and isinstance(e, int) and e == 0:
                        if s == 0:
                            low_d(1, DCH + 2)
                        else:
                            low_gu(0, 0, (DCH + 2) * 2 + 1)
                            low_aT(u - 1, 0)
                            low_gu(0, 1, (DCH + 2) * 2 + 2)
                        gate_up(u, s)
                        return
                    if starts and s == 1 and not first_one:
                        sums_out(e - 1)
                    low_d(s, n + (DCH + 1))
                    if not (starts and s == 0 and first_one):
                        low_aT(u - 1, 1 - s)
                    if more:
                        low_gu(1 - s, 0, (n + (DCH + 1)) * 2 + 1)
                    gate_up(u, s)
                    if starts and s == 1 and not first_one:
                        add(e - 1, 0)
                    if more:
                        low_gu(1 - s, 1, (n + (DCH + 1)) * 2 + 2)

                one(0, 0)
                if not last_one:
                    picks(e + 1, e - (first - 1))
                if not (first_one and first == 0):
                    dve.wait_ge(pgT_full, e)
                picks_gated(e, e - first)
                one(0, 1)
                one(1, 0)
                if not first_one:
                    add(e - 1, 1)
                one(1, 1)
                for i in range(3):
                    with dve.Fori(max(2, HELD[i]), HELD[i + 1]) as j:
                        for s in range(2):
                            one(j, s)
                    if i < 2 and not last_one:
                        gathered_low(e + 1, 1 - b, i)
                one(ECH // 2 - 1, 0)
                one(ECH // 2 - 1, 1, more=not last_one)

            def experts(first):
                picks(first, 0)
                if first == 0:
                    gates()
                    low_gu(1, 1, (DCH + 1) * 2 + 2)
                else:
                    for i in range(2):
                        low_gu(0, i, 2 * (first * ECH + DCH) + i + 1)
                for i in range(2):
                    gathered_low(first, 0, i)
                if first == 0:
                    dve.wait_ge(facc_zeroed, 1)
                expert(first, 0, first, True, False)
                with dve.Fori(0, EXPERTS // 2 - 1) as j:
                    for b in range(2):
                        expert(j * 2 + (first + 1 + b), 1 - b, first, False, False)
                last = first + EXPERTS - 1
                expert(last, 1, first, False, True)
                low_aT(last * ECH + (ECH - 1 + DU), 1)
                sums_out(last)
                dve.wait_ge(added, last * 4)
                for t in range(TT):
                    add(last, t, 6 * (1 - t))
                dve.wait_ge(added, last * 4 + 4)

            attention(0)
            dense()
            attention(1)
            route()
            experts(0)
            dve.wait_ge(routed, 1)
            over = dve.value_load(most_int[0:1, 0:1], min_val=0, max_val=SEQ)
            with dve.If(over > SLOTS):
                V_.tensor_scalar(rank, rank, -float(SLOTS), None, ALU.add).then_inc(routed, 1)
                dve.wait_ge(routed, 2)
                experts(EXPERTS)
            with dve.Else():
                dve.nop()
            dve.sem_inc(f_ready, 1)
            dve.wait_ge(gpost_loaded, 16 * 4)
            for t in range(TT):
                link(V_.tensor_tensor(h[:, t, :], facc[:, t, :], gpost[:, :], ALU.mult))
            for t in range(TT):
                link(inverse(DEPTH, "f", t))
                V_.scalar_tensor_tensor(x[:, t, :], h[:, t, :], rs["f", t], x[:, t, :], ALU.mult, ALU.add)\
                    .then_inc(x_updated, 1)

        @block.tensor
        def _(pe):
            mm = nc.tensor.matmul

            def split_mm(dst, a_hi, a_lo, b_hi, b_lo, start, stop, signal=None):
                first = mm(dst, a_hi, b_hi, start=start, stop=False)
                if signal is not None:
                    first.then_inc(signal, 1)
                mm(dst, a_hi, b_lo, start=False, stop=False)
                return mm(dst, a_lo, b_hi, start=False, stop=stop)

            def turned(t_hi, t_lo, k, t):
                tok = slice(t * P, (t + 1) * P)
                return t_hi[:, k, tok], t_lo[:, k, tok]

            def transposes(layer, name, t, n_h):
                pe.wait_ge(ident_loaded, 16)
                for i in range(2):
                    pe.wait_ge(h_ready, 2 * (n_h + t) + i + 1)
                    wait_free(layer, f"{name}{t}{i}")
                    for k in range(4):
                        last = nc.tensor.transpose(jb(layer, f"{name}{t}{i}")[:, k * P:(k + 1) * P],
                                                   h[:, t, (4 * i + k) * P:(4 * i + k + 1) * P], ident[:, :])
                    fill(last, layer, f"{name}{t}{i}")

            def attention(layer):
                def split(i):
                    pe.wait_ge(piece_split, PIECES * layer + i + 1)
                    return piece_hi[i], piece_lo[i]

                def drained(*names):
                    wait_drained(pe, layer, *names)

                def latents(t, part):
                    pe.wait_ge(cn_ready, 4 * layer + 2 * t + (1 if part == "A" else 2))
                    name = f"c{part}{t}"
                    wait_free(layer, name)
                    blocks = [cn[:, t, k * P:(k + 1) * P] for k in (range(KQ) if part == "A" else range(KQ, KQ + KKV))]
                    if part == "B":
                        pe.wait_ge(zr_ready, TT * layer + t + 1)
                        blocks.append(zr[:, t, :])
                    for j, b in enumerate(blocks):
                        last = nc.tensor.transpose(jb(layer, name)[:, j * P:(j + 1) * P], b, ident[:, :])
                        if part == "A" and t == 1 and j == 0:
                            last.then_inc(piece_used, 1)
                    fill(last, layer, name)

                transposes(layer, "hT", 0, 2 * layer * TT)
                for t in range(TT):
                    zb = [f"z{t}{n}" for n in range(2)]
                    for n in range(2):
                        wait_free(layer, zb[n])
                    for j in range(4):
                        if j == 3 and t == 0:
                            transposes(layer, "hT", 1, 2 * layer * TT)
                        if j >= 2 and t == 1:
                            latents(0, "AB"[j - 2])
                        parts = split(P_IN + j)
                        drained(f"hT{t}{j // 2}")
                        for k in range(2):
                            for n in range(2):
                                a = k * IN_COLS + n * HALF_IN
                                last = split_mm(jb(layer, zb[n])[:, 0:HALF_IN], *turned(hT_hi, hT_lo, 2 * j + k, t),
                                                *(w[:, a:a + HALF_IN] for w in parts),
                                                j == 0 and k == 0, j == 3 and k == 1)
                                if j == 3 and k == 1:
                                    fill(last, layer, zb[n])
                        if j < 3 and t == 1:
                            last.then_inc(piece_used, 1)
                latents(1, "A")

                pe.wait_ge(tables_loaded, 80)
                drained("z01", "z11")
                wait_free(layer, "pooled")
                for g in range(GROUPS):
                    a, c = (g % 2) * GDIM, (g // 2) * SEQ
                    o = jb(layer, "pooled")
                    u = [z[:, t, U0 + g * GDIM:U0 + (g + 1) * GDIM] for t in range(TT)]
                    mm(o[a:a + GDIM, c:c + P], u[0], bands[:, g, 0:P], start=True, stop=True)
                    mm(o[a:a + GDIM, c + P:c + SEQ], u[0], bands[:, g, P:SEQ], start=True, stop=False)
                    last = mm(o[a:a + GDIM, c + P:c + SEQ], u[1], bands[:, g, SEQ:KPOS], start=False, stop=True)
                fill(last, layer, "pooled")

                def over_k(dst, ks, lhs, rhs, name=None, piece_before=False):
                    for k in range(ks):
                        last = split_mm(dst, *lhs(k), *rhs(k), k == 0, k == ks - 1, piece_used if piece_before and k == 0 else None)
                    if name:
                        fill(last, layer, name)

                def projections(g):
                    wq = [w[:, 0:KQ * HG * QK].rearrange("p (k h n) -> p k h n", k=KQ, h=HG) for w in split(P_UQ[g])]
                    if g == 0:
                        drained("cA0", "cA1")

                    def c(k):
                        return cT_hi[:, k, :], cT_lo[:, k, :]

                    def q(dst, i, name=None):
                        over_k(dst, KQ, lambda k: [w[:, k, i, 0:NOPE] for w in wq], c, name)

                    def key(dst, i, name=None, piece_before=False):
                        over_k(dst, KKV, lambda k: [w[:, k, i, 0:NOPE] for w in wkv], lambda k: c(KQ + k), name, piece_before)

                    def rope(dst, i, name=None):
                        over_k(dst, KQ, lambda k: (rw_hi[:, k, i, :], rw_lo[:, k, i, :]), c, name)

                    wait_free(layer, f"q01_{g}")
                    q(jb(layer, f"q01_{g}")[:, 0:SEQ], 0)
                    q(jb(layer, f"q01_{g}")[:, SEQ:2 * SEQ], 1, f"q01_{g}")
                    wkv = []

                    def ropes():
                        pe.wait_ge(rope_w_ready, 4 * layer + 2 * g + 2)
                        wait_free(layer, f"r01_{g}")
                        rope(jb(layer, f"r01_{g}")[:, 0:SEQ], 0)
                        rope(jb(layer, f"r01_{g}")[:, SEQ:2 * SEQ], 1, f"r01_{g}")
                        wait_free(layer, f"qr2_{g}")
                        q(jb(layer, f"qr2_{g}")[:, 0:SEQ], 2)
                        rope(jb(layer, f"qr2_{g}")[:, SEQ:2 * SEQ], 2, f"qr2_{g}")

                    if g == 0:
                        latents(1, "B")
                        ropes()
                        drained("cB0", "cB1")
                    wkv += [w[:, 0:KKV * HG * KV].rearrange("p (k h n) -> p k h n", k=KKV, h=HG) for w in split(P_UKV[g])]
                    wait_free(layer, f"k01_{g}")
                    key(jb(layer, f"k01_{g}")[:, 0:SEQ], 0, piece_before=(g == 0))
                    key(jb(layer, f"k01_{g}")[:, SEQ:2 * SEQ], 1, f"k01_{g}")
                    wait_free(layer, f"k2_{g}")
                    key(jb(layer, f"k2_{g}")[:, 0:SEQ], 2, f"k2_{g}")
                    for t in range(TT):
                        wait_free(layer, f"v{t}_{g}")
                        over_k(jb(layer, f"v{t}_{g}")[:, 0:HG * VDIM].rearrange("p (h n) -> p h n", h=HG), KKV,
                               lambda k: turned(cT_hi, cT_lo, KQ + k, t), lambda k: [w[:, k, :, NOPE:KV] for w in wkv],
                               f"v{t}_{g}")
                    if g:
                        ropes()

                def scores(g):
                    drained(f"q01_{g}", f"k01_{g}", f"k2_{g}", f"r01_{g}", f"qr2_{g}")
                    pe.wait_ge(krT_ready, TT * (layer + 1))
                    for i in range(HG * g, HG * (g + 1)):
                        wait_free(layer, f"s{i}")
                        o = jb(layer, f"s{i}")
                        for b, (a, w) in enumerate(((0, P), (P, SEQ))):
                            ins = mm(o[:, a:a + w], qT[:, i, b * P:(b + 1) * P], kT[:, i, 0:w], start=True, stop=False)
                            if i == 0 and b == 0:
                                ins.then_inc(piece_used, 1)
                            last = mm(o[:, a:a + w], qrT[:, i, b * P:(b + 1) * P], krT[:, 0:w], start=False, stop=True)
                        fill(last, layer, f"s{i}")

                def transposed(g):
                    for i in range(HG * g, HG * (g + 1)):
                        wait_free(layer, f"pT{i}")
                        pe.wait_ge(probs_ready, HEADS * layer + i + 1)
                        for j in range(3):
                            last = nc.tensor.transpose(jb(layer, f"pT{i}")[:, j * P:(j + 1) * P],
                                                       pr[:, i, j * P:(j + 1) * P], ident[:, :])
                            if i == 0 and j < 2:
                                last.then_inc(piece_used, 1)
                        fill(last, layer, f"pT{i}")

                def attended(g):
                    drained(f"v0_{g}", f"v1_{g}")
                    for i in range(HG * g, HG * (g + 1)):
                        drained(f"pT{i}")
                        wait_free(layer, f"a{i}")
                        o = jb(layer, f"a{i}")
                        vi = [v[:, t, i * VDIM:(i + 1) * VDIM] for t in range(TT)]
                        mm(o[:, 0:P], vi[0], prT[:, i, 0:P], start=True, stop=True)
                        mm(o[:, P:SEQ], vi[0], prT[:, i, P:2 * P], start=True, stop=False)
                        last = mm(o[:, P:SEQ], vi[1], prT[:, i, 2 * P:3 * P], start=False, stop=True)
                        fill(last, layer, f"a{i}")

                projections(0)
                scores(0)
                projections(1)
                transposed(0)
                scores(1)
                attended(0)
                drained("pooled")
                pe.wait_ge(pool_w_loaded, 16 * (GROUPS + 1) * (layer + 1))
                wait_free(layer, "poolout")
                for a in range(2):
                    last = mm(jb(layer, "poolout")[:, a * SEQ:(a + 1) * SEQ], pwbd[:, a, :], pl[:, a, :],
                              start=True, stop=True)
                fill(last, layer, "poolout")
                transposed(1)
                attended(1)
                for t in range(TT):
                    for n in range(2):
                        wait_free(layer, f"o{t}{n}")
                    for i, j in enumerate(WOUT_ORDER):
                        if t == 0:
                            if j == 3:
                                drained("poolout")
                            else:
                                drained(f"a{2 * j}", f"a{2 * j + 1}")
                        elif i == 3:
                            transposes(layer, "fT", 0, (2 * layer + 1) * TT)
                        parts = split(P_OUT + i)
                        for n in range(2):
                            for k in range(2):
                                a = k * D + n * BK
                                last = split_mm(jb(layer, f"o{t}{n}")[:, :], *turned(mixT_hi, mixT_lo, 2 * j + k, t),
                                                *(w[:, a:a + BK] for w in parts), i == 0 and k == 0, i == 3 and k == 1)
                            if i == 3:
                                fill(last, layer, f"o{t}{n}")
                        if t == 1 and i < 3:
                            last.then_inc(piece_used, 1)

            def gate_up(s, b, t_hi, t_lo, ks):
                for k in ks:
                    last = split_mm(bank[b][:, :], t_hi[:, k, :], t_lo[:, k, :],
                                    part_gu(hi, s, k), part_gu(lo, s, k), k == 0, k == KD - 1)
                return last

            def turn(s):
                for k in range(KF):
                    last = nc.tensor.transpose(bank[2 + s][:, k * P:(k + 1) * P], acts[:, s, k * P:(k + 1) * P], ident[:, :])
                last.then_inc(tr_full, 1)

            def down(s_w, s_a, b0, start, stop):
                for n in range(2):
                    for k in range(KF):
                        last = split_mm(bank[b0 + n][:, :], aT_hi[:, s_a, k, :], aT_lo[:, s_a, k, :],
                                        part_d(hi, s_w, k, n), part_d(lo, s_w, k, n),
                                        start and k == 0, stop and k == KF - 1)
                last.then_inc(d_used, 1)

            FIRST_K, SECOND_K = range(0, KD // 2), range(KD // 2, KD)

            def dense():
                for b in range(4):
                    pe.wait_ge(bank_free[b], USES_BEFORE_UNITS[0][b] - (b in (2, 3)))

                def unit(c, t, s, first=False, start=False, stop=False):
                    u = c * 2 + t
                    pe.wait_ge(gu_split, c * 2 + 1)
                    if not first:
                        pe.wait_ge(gated, u - 1)
                    t_hi, t_lo = (part[:, :, t * P:(t + 1) * P] for part in (eT_hi, eT_lo))
                    gate_up(s, t, t_hi, t_lo, FIRST_K)
                    if not (first and t == 0):
                        pe.wait_ge(gated, u)
                        if not (isinstance(u, int) and u < 3):
                            pe.wait_ge(aT_ready, u - 2)
                        turn(1 - t)
                    pe.wait_ge(gu_split, c * 2 + 2)
                    last = gate_up(s, t, t_hi, t_lo, SECOND_K)
                    last.then_inc(gu_full, 1)
                    if not (first and t == 0):
                        pe.wait_ge(aT_ready, u)
                        if t == 0:
                            down(1 - s, 1, 6, start, stop)
                        else:
                            pe.wait_ge(d_split, c + 1)
                            down(s, 0, 4, start, stop)

                unit(0, 0, 0, first=True)
                transposes(0, "fT", 1, TT)
                wait_drained(pe, 0, "fT10", "fT11")
                for t in range(TT):
                    for n in range(2):
                        wait_free(0, f"f{t}{n}")
                unit(0, 1, 0, first=True, start=True)
                unit(1, 0, 1, start=True)
                unit(1, 1, 1)
                with pe.Fori(1, DCH // 2) as j:
                    for s in range(2):
                        for t in range(TT):
                            unit(j * 2 + s, t, s)
                unit(DCH - 1, 0, 0)
                unit(DCH - 1, 1, 0, stop=True)
                pe.wait_ge(gated, DU)
                turn(1)
                pe.wait_ge(aT_ready, DU)
                down(0, 1, 6, False, True)

            def route():
                pe.wait_ge(rank_tables_loaded, 48)
                wait_free(1, "logits")
                for t in range(TT):
                    if t:
                        transposes(1, "fT", t, 3 * TT)
                    wait_drained(pe, 1, f"fT{t}0", f"fT{t}1")
                    for k in range(KD):
                        last = mm(jb(1, "logits")[:, t * EXPERTS:(t + 1) * EXPERTS], hT_route[:, k, t * P:(t + 1) * P],
                                  wr[:, k, :], start=(k == 0), stop=(k == KD - 1))
                fill(last, 1, "logits")
                pe.wait_ge(chosen_ready, 1)
                wait_free(1, "ranks")
                o = jb(1, "ranks")
                mm(o[:, 0:EXPERTS], tri[:, :], chosen[:, 0, :], start=True, stop=True)
                mm(o[:, EXPERTS:2 * EXPERTS], ones[:, :], chosen[:, 0, :], start=True, stop=False)
                mm(o[:, EXPERTS:2 * EXPERTS], tri[:, :], chosen[:, 1, :], start=False, stop=True)
                mm(o[:, 2 * EXPERTS:3 * EXPERTS], ones[:, :], chosen[:, 0, :], start=True, stop=False)
                last = mm(o[:, 2 * EXPERTS:3 * EXPERTS], ones[:, :], chosen[:, 1, :], start=False, stop=True)
                fill(last, 1, "ranks")
                for b in range(8):
                    pe.wait_ge(bank_free[b], USES_BEFORE_UNITS[1][b])

            def gather(e, i):
                pe.wait_ge(pick_ready, e + 1)
                for k in range(4):
                    for t in range(TT):
                        last = mm(bank[6 + i][:, k * P:(k + 1) * P], h[:, t, (4 * i + k) * P:(4 * i + k + 1) * P],
                                  pick[:, t, :], start=(t == 0), stop=(t == TT - 1))
                last.then_inc(gathered, 1)

            def scatter(e, t, b=6):
                if t == 0:
                    pe.wait_ge(y_ready, e * 2 + 2)
                    pe.wait_ge(pgT_ready, e + 1)
                elif b == 6:
                    pe.wait_ge(added, e * 4 + 2)
                for n in range(2):
                    mm(bank[b + n][:, :], pgT[:, t * P:(t + 1) * P], y[:, n * BK:(n + 1) * BK],
                       start=True, stop=True).then_inc(spread, 1)

            def expert(e, b, first_one, last_one):
                def one(c_pair, s):
                    starts = isinstance(c_pair, int) and c_pair == 0
                    n = e * ECH + c_pair * 2 + s
                    u = n + DU
                    q = n + DCH
                    pe.wait_ge(gu_split, q * 2 + 1)
                    pe.wait_ge(gated, u - 1)
                    if starts and s == 0:
                        pe.wait_ge(eT_ready, e * 2 + 1)
                    gate_up(s, s, xT_hi[b], xT_lo[b], FIRST_K)
                    if starts and s == 0:
                        pe.wait_ge(eT_ready, e * 2 + 2)
                    after = not (starts and s == 0 and first_one)
                    if after:
                        pe.wait_ge(gated, u)
                        pe.wait_ge(aT_ready, u - 2)
                        turn(1 - s)
                    pe.wait_ge(gu_split, q * 2 + 2)
                    gate_up(s, s, xT_hi[b], xT_lo[b], SECOND_K).then_inc(gu_full, 1)
                    spreads = starts and s == 1 and not first_one
                    if spreads:
                        scatter(e - 1, 0)
                    if after:
                        pe.wait_ge(aT_ready, u)
                        pe.wait_ge(d_split, q)
                        down(1 - s, 1 - s, 4, starts and s == 1, starts and s == 0)
                    if spreads:
                        scatter(e - 1, 1)

                for s in range(2):
                    one(0, s)
                for i in range(3):
                    with pe.Fori(ASKED[i], ASKED[i + 1]) as j:
                        for s in range(2):
                            one(j, s)
                    if i == 0 and not first_one:
                        pe.wait_ge(added, e * 4)
                    if i < 2 and not last_one:
                        gather(e + 1, i)
                if not last_one:
                    pe.wait_ge(eT_ready, e * 2 + 3)
                pe.wait_ge(pick_gated_ready, e + 1)
                for t in range(TT):
                    last = nc.tensor.transpose(bank[6][:, t * P:(t + 1) * P], pick_gated[:, t, :], ident[:, :])
                last.then_inc(pgT_full, 1)
                for s in range(2):
                    one(ECH // 2 - 1, s)

            def experts(first):
                for i in range(2):
                    gather(first, i)
                expert(first, 0, True, False)
                with pe.Fori(0, EXPERTS // 2 - 1) as j:
                    for b in range(2):
                        expert(j * 2 + (first + 1 + b), 1 - b, False, False)
                last = first + EXPERTS - 1
                expert(last, 1, False, True)
                u = last * ECH + (ECH - 1 + DU)
                pe.wait_ge(gated, u + 1)
                turn(1)
                pe.wait_ge(aT_ready, u + 1)
                pe.wait_ge(d_split, u + (DCH - DU + 1))
                down(1, 1, 4, False, True)
                for t in range(TT):
                    scatter(last, t, 6 * (1 - t))
                pe.wait_ge(added, last * 4 + 4)

            attention(0)
            dense()
            attention(1)
            route()
            experts(0)
            pe.wait_ge(routed, 1)
            over = pe.value_load(most_int[0:1, 0:1], min_val=0, max_val=SEQ)
            with pe.If(over > SLOTS):
                experts(EXPERTS)
            with pe.Else():
                pe.nop()


_INS = ["x", "attn_pre_g", "attn_post_g", "ffn_pre_g", "ffn_post_g", "w_in", "q_norm_g", "kv_norm_g", "w_uq", "w_ukv",
        "pool_w", "pool_scale", "w_out", "w_gate_d", "w_up_d", "w_down_d", "w_router", "w_gate_e", "w_up_e", "w_down_e"]


def kernel(**inputs):
    import concourse.bacc as bacc
    from concourse.bass_utils import run_bass_kernel_spmd

    nc = bacc.Bacc("TRN2", target_bir_lowering=False, num_devices=1)
    arrays, args = {}, []
    given = {n: np.ascontiguousarray(inputs[n]) for n in _INS} | tables()
    for name, a in given.items():
        arrays[f"in_{name}"] = a
        args.append(nc.dram_tensor(f"in_{name}", a.shape, mybir.dt.from_np(a.dtype), kind="ExternalInput").ap())
    out = nc.dram_tensor("out_0", (1, SEQ, D), mybir.dt.float32, kind="ExternalOutput").ap()
    encoder_kernel(nc, *args, out)
    r = run_bass_kernel_spmd(nc, [arrays], core_ids=[0])
    return r.results[0]["out_0"]
```
